# Optimizing a Trainium2 kernel written in Bass

```python
import math
import jax
import jax.numpy as jnp
from jax import lax
import numpy as np

D_MODEL = 1024
BATCH = 1
SEQ = 512
DEPTH = 2

GRID_W = 64
CTX_LEN = 256
HEAD_DIM = 64
A_HEADS = 8
A_KV_HEADS = 2
B_HEADS = 8
WIN_R = 8
WIN_C = 16
C_HEADS = 4
C_DK = 128
C_DV = 128
CONV_K = 5
CHUNK = 64
Q_BLOCK = 128
D_FF = 4 * D_MODEL
N_BRANCH = 3
ROPE_BASE = 10000.0
EPS = 1e-6

A_Q = A_HEADS * HEAD_DIM
A_KV = A_KV_HEADS * HEAD_DIM
B_W = B_HEADS * HEAD_DIM
C_K = C_HEADS * C_DK
C_V = C_HEADS * C_DV
BRANCH_W = A_Q
IN_SPLITS = (A_Q, A_KV, A_KV, B_W, B_W, B_W, 2 * C_K + C_V, C_V, 2 * C_HEADS, 2 * C_HEADS, N_BRANCH * D_MODEL)
IN_OFFSETS = [int(o) for o in np.cumsum(IN_SPLITS)[:-1]]
N_IN = sum(IN_SPLITS)
F32 = jnp.float32

kernel_name = 'hybrid_dit_gqa_natten_gdelta'

def rms_norm(x, gain):
    xf = x.astype(F32)
    y = xf * lax.rsqrt(jnp.mean(xf * xf, axis=-1, keepdims=True) + EPS)
    return (y * gain.astype(F32)).astype(x.dtype)

def l2_norm(x):
    xf = x.astype(F32)
    return (xf * lax.rsqrt(jnp.sum(xf * xf, axis=-1, keepdims=True) + EPS)).astype(x.dtype)

def modulate(h, shift, scale):
    return h * (1 + scale) + shift

def heads(a, n):
    return a.reshape(*a.shape[:-1], n, a.shape[-1] // n)

def axial_rope(n_tok):
    t = jnp.arange(n_tok)
    row = (t // GRID_W).astype(F32)
    col = (t % GRID_W).astype(F32)
    axis_dim = HEAD_DIM // 2
    freqs = ROPE_BASE ** (-jnp.arange(0, axis_dim, 2, dtype=F32) / axis_dim)
    ang = jnp.concatenate([row[:, None] * freqs, col[:, None] * freqs], axis=-1)
    return jnp.cos(ang), jnp.sin(ang)

def apply_rope(x, cos, sin):
    xf = x.astype(F32).reshape(*x.shape[:-1], HEAD_DIM // 2, 2)
    x0, x1 = xf[..., 0], xf[..., 1]
    c, s = cos[:, None, :], sin[:, None, :]
    out = jnp.stack([x0 * c - x1 * s, x0 * s + x1 * c], axis=-1)
    return out.reshape(x.shape).astype(x.dtype)

def gqa_attend(q, k, v):
    s = jnp.einsum('bqhgd,bkhd->bhgqk', q, k).astype(F32) * (q.shape[-1] ** -0.5)
    p = jax.nn.softmax(s, axis=-1).astype(v.dtype)
    o = jnp.einsum('bhgqk,bkhd->bqhgd', p, v)
    return o.reshape(*o.shape[:2], -1)

def gqa_latent(q, k, v, kc, vc):
    B, S, H, dh = q.shape
    hkv = k.shape[2]
    k_all = jnp.concatenate([k, kc], axis=1)
    v_all = jnp.concatenate([v, vc], axis=1)
    qb = q.reshape(B, S // Q_BLOCK, Q_BLOCK, hkv, H // hkv, dh).swapaxes(0, 1)
    o = lax.map(lambda qi: gqa_attend(qi, k_all, v_all), qb)
    return o.swapaxes(0, 1).reshape(B, S, H * dh)

def neighbourhood_index(n_tok):
    rows = n_tok // GRID_W
    win_r = min(WIN_R, rows)
    t = jnp.arange(n_tok)
    r, col = t // GRID_W, t % GRID_W
    r0 = jnp.clip(r - win_r // 2, 0, rows - win_r)
    c0 = jnp.clip(col - WIN_C // 2, 0, GRID_W - WIN_C)
    kr = r0[:, None, None] + jnp.arange(win_r)[None, :, None]
    kcl = c0[:, None, None] + jnp.arange(WIN_C)[None, None, :]
    idx = (kr * GRID_W + kcl).reshape(n_tok, win_r * WIN_C)
    bidx = ((kr - r[:, None, None] + WIN_R - 1) * (2 * WIN_C - 1)
            + (kcl - col[:, None, None] + WIN_C - 1)).reshape(n_tok, win_r * WIN_C)
    return idx, bidx

def neighbourhood_latent(q, k, v, kc, vc, rpb):
    B, S, H, dh = q.shape
    idx, bidx = neighbourhood_index(S)
    nb = S // Q_BLOCK
    rpb_flat = rpb.reshape(H, -1)
    scale = dh ** -0.5

    def block(args):
        qi, ii, bi = args
        kg = jnp.take(k, ii, axis=1)
        vg = jnp.take(v, ii, axis=1)
        s_loc = jnp.einsum('bqhd,bqkhd->bhqk', qi, kg).astype(F32) * scale + rpb_flat[:, bi].astype(F32)[None]
        s_ctx = jnp.einsum('bqhd,bchd->bhqc', qi, kc).astype(F32) * scale
        p = jax.nn.softmax(jnp.concatenate([s_loc, s_ctx], axis=-1), axis=-1).astype(v.dtype)
        nk = ii.shape[-1]
        return (jnp.einsum('bhqk,bqkhd->bqhd', p[..., :nk], vg)
                + jnp.einsum('bhqc,bchd->bqhd', p[..., nk:], vc))

    qb = q.reshape(B, nb, Q_BLOCK, H, dh).swapaxes(0, 1)
    o = lax.map(block, (qb, idx.reshape(nb, Q_BLOCK, -1), bidx.reshape(nb, Q_BLOCK, -1)))
    return o.swapaxes(0, 1).reshape(B, S, H * dh)

def short_conv(x, w):
    y = lax.conv_general_dilated(x, w[:, None, :].astype(x.dtype), window_strides=(1,),
                                 padding=[(CONV_K // 2, CONV_K // 2)],
                                 dimension_numbers=('NWC', 'WIO', 'NWC'),
                                 feature_group_count=x.shape[-1])
    return jax.nn.silu(y)

def gdn_features(qkv, beta_raw, a_raw, conv_w, a_log, dt_bias):
    qkv = short_conv(qkv, conv_w)
    q, k, v = jnp.split(qkv, [C_K, 2 * C_K], axis=-1)
    q = l2_norm(heads(q, C_HEADS))
    k = l2_norm(heads(k, C_HEADS))
    v = heads(v, C_HEADS)
    beta = jax.nn.sigmoid(heads(beta_raw, 2).astype(F32))
    g = -jnp.exp(a_log.astype(F32)) * jax.nn.softplus(heads(a_raw, 2).astype(F32) + dt_bias.astype(F32))
    return q, k, v, beta, g

def gated_delta_chunked(q, k, v, beta, g, state0, with_output):
    B, T, H, dk = k.shape
    dv = v.shape[-1]
    n = T // CHUNK

    def chunks(a):
        a = a.astype(F32).reshape(B, n, CHUNK, H, *a.shape[3:])
        return jnp.moveaxis(a, 3, 2).swapaxes(0, 1)

    kc, vc, bc = chunks(k), chunks(v), chunks(beta)
    gc = jnp.cumsum(chunks(g), axis=-1)
    lower = jnp.tril(jnp.ones((CHUNK, CHUNK), dtype=bool))
    strict = jnp.tril(jnp.ones((CHUNK, CHUNK), dtype=bool), -1)
    decay = jnp.exp(jnp.where(lower, gc[..., :, None] - gc[..., None, :], -jnp.inf))
    kb = kc * bc[..., None]
    nil = jnp.where(strict, -jnp.einsum('nbhid,nbhjd->nbhij', kb, kc) * decay, 0.0)
    tinv = jnp.eye(CHUNK, dtype=F32) + nil
    power = nil
    for _ in range(int(math.log2(CHUNK)) - 1):
        power = power @ power
        tinv = tinv + tinv @ power
    w_v = tinv @ (vc * bc[..., None])
    k_cd = tinv @ (kb * jnp.exp(gc)[..., None])
    g_last = gc[..., -1]
    k_dec = kc * jnp.exp(g_last[..., None] - gc)[..., None]
    xs = (w_v, k_cd, k_dec, g_last)
    if with_output:
        qc = chunks(q) * (dk ** -0.5)
        xs = xs + (qc * jnp.exp(gc)[..., None], jnp.einsum('nbhid,nbhjd->nbhij', qc, kc) * decay)

    def step(state, inp):
        wv, kcd, kd, gl = inp[:4]
        v_new = wv - jnp.einsum('bhck,bhkv->bhcv', kcd, state)
        new_state = state * jnp.exp(gl)[..., None, None] + jnp.einsum('bhck,bhcv->bhkv', kd, v_new)
        if with_output:
            qd, aqk = inp[4:]
            o = jnp.einsum('bhck,bhkv->bhcv', qd, state) + jnp.einsum('bhij,bhjv->bhiv', aqk, v_new)
            return new_state, o
        return new_state, None

    state, outs = lax.scan(step, state0, xs)
    if not with_output:
        return None, state
    return outs.transpose(1, 0, 3, 2, 4).reshape(B, T, H, dv), state

def bidir_gated_delta(feat, cfeat, need_ctx):
    q, k, v, beta, g = feat
    cq, ck, cv, cbeta, cg = cfeat
    zero = jnp.zeros((k.shape[0], C_HEADS, C_DK, C_DV), F32)

    def flip(a):
        return jnp.flip(a, axis=1)

    oc_f, s_f = gated_delta_chunked(cq, ck, cv, cbeta[:, :, 0], cg[:, :, 0], zero, need_ctx)
    o_f, _ = gated_delta_chunked(q, k, v, beta[:, :, 0], g[:, :, 0], s_f, True)
    oc_r, s_r = gated_delta_chunked(flip(cq), flip(ck), flip(cv), flip(cbeta[:, :, 1]), flip(cg[:, :, 1]), zero, need_ctx)
    o_r, _ = gated_delta_chunked(flip(q), flip(k), flip(v), flip(beta[:, :, 1]), flip(g[:, :, 1]), s_r, True)
    o = o_f + flip(o_r)
    oc = oc_f + flip(oc_r) if need_ctx else None
    return o, oc

def gdn_output(o, z, o_norm):
    y = rms_norm(o, o_norm) * jax.nn.silu(heads(z, C_HEADS).astype(F32))
    return y.reshape(z.shape).astype(z.dtype)

def merge_branches(o_a, o_b, o_c, gate_raw, w_branch, w_out):
    br = jnp.einsum('btnc,ncd->btnd', jnp.stack([o_a, o_b, o_c], axis=-2), w_branch)
    gates = jax.nn.sigmoid(heads(gate_raw, N_BRANCH))
    return jnp.sum(gates * br, axis=-2) @ w_out

def sq_relu_mlp(h, w1, w2):
    return jnp.square(jax.nn.relu(h @ w1)) @ w2

def trunk_layer(x, xc, mod, mod_c, params, cos, sin, need_ctx):
    (norm_mix, w_in, q_norm_a, k_norm_a, rpb_b, conv_c, a_log_c, dt_bias_c, o_norm_c,
     w_branch, w_out, norm_ffn, w_ffn1, w_ffn2) = params
    sh_m, sc_m, gt_m, sh_f, sc_f, gt_f = jnp.split(mod, 6, axis=-1)
    csh_m, csc_m, cgt_m, csh_f, csc_f, cgt_f = jnp.split(mod_c, 6, axis=-1)

    h = modulate(rms_norm(x, norm_mix), sh_m, sc_m)
    hc = modulate(rms_norm(xc, norm_mix), csh_m, csc_m)
    (qa, ka, va, qb, kb, vb, qkv_c, z_c, beta_c, a_c, gate) = jnp.split(h @ w_in, IN_OFFSETS, axis=-1)
    (cqa, cka, cva, cqb, ckb, cvb, cqkv_c, cz_c, cbeta_c, ca_c, cgate) = jnp.split(hc @ w_in, IN_OFFSETS, axis=-1)

    qa = apply_rope(rms_norm(heads(qa, A_HEADS), q_norm_a), cos, sin)
    ka = apply_rope(rms_norm(heads(ka, A_KV_HEADS), k_norm_a), cos, sin)
    cka = rms_norm(heads(cka, A_KV_HEADS), k_norm_a)
    cva = heads(cva, A_KV_HEADS)
    o_a = gqa_latent(qa, ka, heads(va, A_KV_HEADS), cka, cva)

    ckb = heads(ckb, B_HEADS)
    cvb = heads(cvb, B_HEADS)
    o_b = neighbourhood_latent(heads(qb, B_HEADS), heads(kb, B_HEADS), heads(vb, B_HEADS), ckb, cvb, rpb_b)

    feat = gdn_features(qkv_c, beta_c, a_c, conv_c, a_log_c, dt_bias_c)
    cfeat = gdn_features(cqkv_c, cbeta_c, ca_c, conv_c, a_log_c, dt_bias_c)
    o_c, oc_c = bidir_gated_delta(feat, cfeat, need_ctx)
    o_c = gdn_output(o_c, z_c, o_norm_c)

    x = x + gt_m * merge_branches(o_a, o_b, o_c, gate, w_branch, w_out)
    x = x + gt_f * sq_relu_mlp(modulate(rms_norm(x, norm_ffn), sh_f, sc_f), w_ffn1, w_ffn2)

    if need_ctx:
        B, Lc = xc.shape[:2]
        cqa_h = rms_norm(heads(cqa, A_HEADS), q_norm_a).reshape(B, Lc, A_KV_HEADS, A_HEADS // A_KV_HEADS, HEAD_DIM)
        oc_a = gqa_attend(cqa_h, cka, cva)
        oc_b = gqa_attend(heads(cqb, B_HEADS)[:, :, :, None, :], ckb, cvb)
        oc_c = gdn_output(oc_c, cz_c, o_norm_c)
        xc = xc + cgt_m * merge_branches(oc_a, oc_b, oc_c, cgate, w_branch, w_out)
        xc = xc + cgt_f * sq_relu_mlp(modulate(rms_norm(xc, norm_ffn), csh_f, csc_f), w_ffn1, w_ffn2)
    return x, xc

def setup_inputs(seed: int = 0) -> dict:
    key = jax.random.key(seed)
    ks = jax.random.split(key, 24)

    def nrm(k, shape, scale):
        return scale * jax.random.normal(k, shape, F32)

    def gain(k, shape):
        return 1.0 + 0.02 * jax.random.normal(k, shape, F32)

    dt = jnp.exp(jax.random.uniform(ks[10], (DEPTH, 2, C_HEADS), F32, math.log(1e-3), math.log(1e-1)))
    return {
        'x': nrm(ks[0], (BATCH, SEQ, D_MODEL), 1.0),
        'c': nrm(ks[1], (BATCH, D_MODEL), 1.0),
        'ctx': nrm(ks[2], (BATCH, CTX_LEN, D_MODEL), 1.0),
        'c_ctx': nrm(ks[3], (D_MODEL,), 1.0),
        'w_mod': nrm(ks[4], (DEPTH, D_MODEL, 6 * D_MODEL), 0.5 * D_MODEL ** -0.5),
        'b_mod': nrm(ks[5], (DEPTH, 6 * D_MODEL), 0.01),
        'norm_mix': gain(ks[6], (DEPTH, D_MODEL)),
        'w_in': nrm(ks[7], (DEPTH, D_MODEL, N_IN), D_MODEL ** -0.5),
        'q_norm_a': gain(ks[8], (DEPTH, HEAD_DIM)),
        'k_norm_a': gain(ks[9], (DEPTH, HEAD_DIM)),
        'rpb_b': nrm(ks[11], (DEPTH, B_HEADS, 2 * WIN_R - 1, 2 * WIN_C - 1), 0.1),
        'conv_c': nrm(ks[12], (DEPTH, CONV_K, 2 * C_K + C_V), CONV_K ** -0.5),
        'a_log_c': jnp.log(jax.random.uniform(ks[13], (DEPTH, 2, C_HEADS), F32, 1.0, 16.0)),
        'dt_bias_c': dt + jnp.log(-jnp.expm1(-dt)),
        'o_norm_c': gain(ks[14], (DEPTH, C_DV)),
        'w_branch': nrm(ks[15], (DEPTH, N_BRANCH, BRANCH_W, D_MODEL), BRANCH_W ** -0.5),
        'w_out': nrm(ks[16], (DEPTH, D_MODEL, D_MODEL), D_MODEL ** -0.5),
        'norm_ffn': gain(ks[17], (DEPTH, D_MODEL)),
        'w_ffn1': nrm(ks[18], (DEPTH, D_MODEL, D_FF), D_MODEL ** -0.5),
        'w_ffn2': nrm(ks[19], (DEPTH, D_FF, D_MODEL), D_FF ** -0.5),
        'norm_final': gain(ks[20], (D_MODEL,)),
    }

def reference(x, c, ctx, c_ctx, w_mod, b_mod, norm_mix, w_in, q_norm_a, k_norm_a, rpb_b, conv_c,
              a_log_c, dt_bias_c, o_norm_c, w_branch, w_out, norm_ffn, w_ffn1, w_ffn2, norm_final):
    n_tok = x.shape[1]
    cos, sin = axial_rope(n_tok)
    xc = ctx
    for l in range(DEPTH):
        mod = (jax.nn.silu(c) @ w_mod[l] + b_mod[l])[:, None, :]
        mod_c = jax.nn.silu(c_ctx) @ w_mod[l] + b_mod[l]
        params = (norm_mix[l], w_in[l], q_norm_a[l], k_norm_a[l], rpb_b[l], conv_c[l], a_log_c[l],
                  dt_bias_c[l], o_norm_c[l], w_branch[l], w_out[l], norm_ffn[l], w_ffn1[l], w_ffn2[l])
        x, xc = trunk_layer(x, xc, mod, mod_c, params, cos, sin, l < DEPTH - 1)
    return rms_norm(x, norm_final)


_drawn_inputs = setup_inputs


def setup_inputs(seed=0):
    import zlib

    import numpy as np

    out = dict(_drawn_inputs(seed))
    spreads = {}
    factors = {'b_mod': 2.698,
     'norm_mix': 8.0,
     'q_norm_a': 8.0,
     'k_norm_a': 8.0,
     'rpb_b': 23.861,
     'o_norm_c': 8.0,
     'norm_ffn': 4.414,
     'norm_final': 8.768}
    for name, (base, spread) in spreads.items():
        noise = np.random.default_rng([zlib.crc32(name.encode()), seed]).standard_normal(out[name].shape)
        drawn = base * np.exp(spread * noise) if base else spread * noise
        out[name] = jnp.asarray(drawn.astype(out[name].dtype))
    for name, factor in factors.items():
        out[name] = (out[name] * factor).astype(out[name].dtype)
    return out
```

```python
from contextlib import ExitStack

import numpy as np
import concourse.bass as bass
from concourse import mybir

F32 = mybir.dt.float32
ALU = mybir.AluOpType
ACT = mybir.ActivationFunctionType
AX = mybir.AxisListType

P = 128
D = 1024
KC = D // P
LAT, CTX = 512, 256
TOK = LAT + CTX
TT, LT = TOK // P, LAT // P
DEPTH = 2
GRID_W, ROWS = 64, LAT // 64
HD = 64
A_H, A_KV, B_H, C_H = 8, 2, 8, 4
WIN_R, WIN_C = 8, 16
CONV = 5
FF = 4 * D
EPS = 1e-6
NEG = -1e30
SCALE = HD ** -0.5
O_QA, O_KA, O_VA, O_QB, O_KB, O_VB, O_QKV, O_Z, O_BETA, O_A, O_GATE = (
    int(v) for v in np.cumsum([0, 512, 128, 128, 512, 512, 512, 1536, 512, 8, 8]))
SLOT = KC * 512
NSLOT = 2
C_ID, C_ONE, C_BLK, C_ROT, C_UI, C_LI, C_US, C_LS, C_COS, C_SIN, C_MASK = (
    int(v) for v in np.cumsum([0, P, P, P, P, P, P, P, P, LAT, LAT]))
C_N = C_MASK + GRID_W
R_BMOD, R_MIX, R_FFN, R_CONV, R_ONORM, R_QN, R_KN, R_FIN = 0, 48, 56, 64, 124, 125, 126, 127


def constants():
    c = np.zeros((P, C_N), np.float32)
    i = np.arange(P)
    same = (i[:, None] // 64) == (i[None, :] // 64)
    c[:, C_ID:C_ID + P] = np.eye(P)
    c[:, C_ONE:C_ONE + P] = 1
    c[:, C_BLK:C_BLK + P] = same
    for m in range(0, P, 2):
        c[m + 1, C_ROT + m] = -1
        c[m, C_ROT + m + 1] = 1
    c[:, C_UI:C_UI + P] = same & (i[:, None] <= i[None, :])
    c[:, C_LI:C_LI + P] = same & (i[:, None] >= i[None, :])
    c[:, C_US:C_US + P] = same & (i[:, None] < i[None, :])
    c[:, C_LS:C_LS + P] = same & (i[:, None] > i[None, :])
    t = np.arange(LAT)
    freq = (10000.0 ** (-np.arange(0, HD // 2, 2, dtype=np.float32) / np.float32(HD // 2))).astype(np.float32)
    pair = (i % HD) // 2
    pos = np.where((pair < 16)[:, None], (t // GRID_W)[None, :], (t % GRID_W)[None, :]).astype(np.float32)
    ang = pos * freq[pair % 16][:, None]
    c[:, C_COS:C_COS + LAT] = np.cos(ang)
    c[:, C_SIN:C_SIN + LAT] = np.sin(ang)
    col = i % GRID_W
    c0 = np.clip(col - WIN_C // 2, 0, GRID_W - WIN_C)
    kc = np.arange(GRID_W)
    inside = (kc[None, :] >= c0[:, None]) & (kc[None, :] < c0[:, None] + WIN_C)
    c[:, C_MASK:C_MASK + GRID_W] = np.where(inside, 0.0, NEG)
    return c


class Signal:

    def __init__(self, nc, ctx, name, book):
        self.sem = ctx.enter_context(nc.semaphore(name))
        self.n, self.book, self.name = 0, book, name

    def mark(self, *key, by=1):
        self.n += by
        self.book[(self.name,) + key] = self.n
        return self.sem, by

    def at(self, *key):
        if self.book["final"]:
            return self.sem, self.book[(self.name,) + key]
        return self.sem, 1


def program(nc, a, out, scratch, toeplitz, book):
    book["final"] = book.get("final", False)
    with ExitStack() as ctx:
        def sb(name, shape):
            return ctx.enter_context(nc.sbuf_tensor(name, shape, F32))

        def sig(name):
            return Signal(nc, ctx, name, book)

        xT = sb("xT", [P, KC, TOK])
        hT = sb("hT", [P, KC, TOK])
        wring = sb("wring", [P, NSLOT, SLOT])
        cst = sb("cst", [P, C_N])
        pcol = sb("pcol", [P, P])
        ccol = sb("ccol", [P, 2, KC])
        modc = sb("modc", [P, 48, 2])
        gain = sb("gain", [P, 2, KC, 2])
        small = sb("small", [P, 64])
        eps = sb("eps", [P, 1])
        R = sb("R", [P, 27648])
        PS = [ctx.enter_context(nc.psum_tensor(f"ps{i}", [P, 1024], F32)) for i in range(4)]

        def r(at, *shape):
            n = int(np.prod(shape))
            v = R[:, at:at + n]
            if len(shape) == 2:
                v = v.rearrange("p (a b) -> p a b", a=shape[0])
            if len(shape) == 3:
                v = v.rearrange("p (a b c) -> p a b c", a=shape[0], b=shape[1])
            return v

        ident, ones, blk, rot = (cst[:, c:c + P] for c in (C_ID, C_ONE, C_BLK, C_ROT))
        oC, oA, oB = r(0, 4, TOK), r(3072, 4, TOK), r(6144, 4, TOK)
        S0 = 9216
        sq_n, rs_n = r(24576, 2, TOK), r(24576 + 2 * TOK, TOK)
        qT, kT = r(0, 4, TOK), r(3072, 4, TOK)
        ktok, vtok, Otok = r(6144, TT, 512), r(9216, TT, 512), r(12288, TT, 512)
        U0 = 15360
        rbuf, ebuf, wbuf, pbuf, p2buf, tbuf, xbuf, aqbuf, qdbuf, vbbuf = (
            [r(U0 + (2 * b + d) * 512, 4, P) for d in range(2)] for b in range(10))
        state = r(U0 + 10240, 2, 8, P)
        craw = r(U0, 2, TOK + 8)
        cacc = r(U0 + 2048, 2, TOK + 8)
        csq, crr = r(U0 + 6144, 2, TOK), r(U0 + 8192, 2, TOK)
        vT4 = r(12288, 4, TOK)
        siluz = r(9216, 4, TOK)
        osq = r(6144, TT, 512)
        bg = sb("bg", [P, TT, 16])
        gt = sb("gt", [P, TT, 8])
        gtmp = sb("gtmp", [P, TT, 8])
        gcs = sb("gcs", [P, TT, 32])
        gex = sb("gex", [P, TT, 4, 8])
        nbeta = sb("nbeta", [P, TT, 8])
        abc = sb("abc", [P, 2, 8])
        qk = r(S0, 6, TOK)
        va = r(S0 + 4608, TT, 128)
        asq, arr = r(S0 + 5376, TOK), r(S0 + 6144, TOK)
        rtmp = r(S0 + 6912, 2, LAT)
        prob = r(S0 + 9216 + 1792, 2, TOK)
        probT = r(S0 + 9216 + 1792 + 1536, 2, TT, P)
        qB, kB, vB = r(S0, 4, TOK), r(S0 + 3072, 4, TOK), r(S0 + 6144, TT, 512)
        ebias = r(S0 + 9216, 2, 14, GRID_W)
        stat = sb("stat", [P, 2, 4])
        mT = r(S0, KC, TOK)
        gsig = r(S0 + 6144, 2, TOK)
        fT = r(0, FF // P, TOK)
        prow = sb("prow", [P, P])
        craw_c = sb("craw_c", [P, 2, KC])
        bpad = ctx.enter_context(nc.sbuf_tensor("bpad", [B_H * 15, 127], F32))
        tiles = ([4, 5, 0, 1, 2, 3], [5, 4, 3, 2, 1, 0])
        masks = {k: cst[:, c:c + P] for k, c in (("UI", C_UI), ("LI", C_LI), ("US", C_US), ("LS", C_LS))}
        m_cum, m_strict, m_aq = ("UI", "LI"), ("LS", "US"), ("UI", "LI")

        def want_out(l, t):
            return l == 0 or t < LT

        def flat(v):
            return v.rearrange("p a b -> p (a b)")

        def over_heads(v):
            return v.unsqueeze(1).to_broadcast([P, C_H, P])

        def along(v, n=P):
            return v.unsqueeze(2).to_broadcast([v.shape[0], v.shape[1], n])

        def power(d, i):
            one, two = (pbuf[d], tbuf[d]), (p2buf[d], rbuf[d])
            return (*one, *two) if i % 2 == 0 else (*two, *one)

        ps_full = [ctx.enter_context(nc.semaphore(f"ps_full{i}")) for i in range(4)]
        ps_free = [ctx.enter_context(nc.semaphore(f"ps_free{i}")) for i in range(4)]
        w_full = [ctx.enter_context(nc.semaphore(f"w_full{i}")) for i in range(NSLOT)]
        params_in, cond_in, consts_in = sig("params_in"), sig("cond_in"), sig("consts_in")
        x_in = [sig(f"x_in{t}") for t in range(TT)]
        act_done, dve_done, pool_done, pe_done = sig("act_done"), sig("dve_done"), sig("pool_done"), sig("pe_done")
        abc_in, rpb_in, pad_out, skew_out, out_done, e_in = (sig(n) for n in ("abc_in", "rpb_in", "pad_out", "skew_out", "out_done", "e_in"))
        block = ctx.enter_context(nc.Block())
        turn = {"n": 0, "w": 0}

        def take(pe, *key):
            n = turn["n"]
            turn["n"] += 1
            book[("ps",) + key] = n
            if n >= 4:
                pe.wait_ge(ps_free[n % 4], 2 * (n // 4))
            return PS[n % 4]

        def full(*key):
            n = book.get(("ps",) + key, 0) if book["final"] else 0
            return ps_full[n % 4], n // 4 + 1

        def filled(*key):
            return ps_full[book[("ps",) + key] % 4], 1

        def pair(*key):
            return PS[book.get(("ps",) + key, 0) % 4]

        def free(*key, by=2):
            return ps_free[book.get(("ps",) + key, 0) % 4], by

        def read(*key):
            n = book.get(("ps",) + key, 0) if book["final"] else 0
            return ps_free[n % 4], 2 * (n // 4 + 1)

        def read_first(*key):
            sem, n = read(*key)
            return sem, n - 1

        def att_items(l):
            return [(h, t) for h in range(A_H) for t in range(TT if l == 0 else LT)]

        slots = []

        def slot_key(l, name, i=0):
            return ("slot", l, name, i)

        w_in = a["w_in"]

        def cols(w, l, c0, n):
            return w[l, :, c0:c0 + n].rearrange("(k p) n -> p k n", p=P)

        def plan(l):
            for i in range(12):
                yield "mod", i, [(lambda s: s.rearrange("p (k n) -> p k n", k=KC),
                                  a["w_mod"][l, :, 512 * i:512 * i + 512].rearrange("(p k) n -> p k n", k=KC))]
            full512 = lambda s: s.rearrange("p (k n) -> p k n", k=KC)
            yield "ba", 0, [(lambda s: s[:, 0:KC * 16].rearrange("p (k n) -> p k n", k=KC), cols(w_in, l, O_BETA, 16))]
            for i in range(3):
                yield "c", i, [(full512, cols(w_in, l, O_QKV + 512 * i, 512))]
            yield "z", 0, [(full512, cols(w_in, l, O_Z, 512))]
            yield "qa", 0, [(full512, cols(w_in, l, O_QA, 512))]
            pieces = []
            for g in range(A_KV):
                for u in range(2):
                    pieces.append((lambda s, c=(2 * g + u) * HD: full512(s)[:, :, c:c + HD],
                                   cols(w_in, l, O_KA + g * HD, HD)))
            pieces.append((lambda s: full512(s)[:, :, 256:384], cols(w_in, l, O_VA, 128)))
            yield "kva", 0, pieces
            for n, o in (("qb", O_QB), ("kb", O_KB), ("vb", O_VB)):
                yield n, 0, [(full512, cols(w_in, l, o, 512))]
            for half in range(2):
                for n in range(3):
                    yield "gate", 3 * half + n, [(full512, cols(w_in, l, O_GATE + n * D + 512 * half, 512))]
                    yield "br", 3 * half + n, [(lambda s: s[:, 0:2048].rearrange("p (k n) -> p k n", k=4),
                                                a["w_branch"][l, n, :, 512 * half:512 * half + 512]
                                                .rearrange("(k p) n -> p k n", p=P))]
            for i in range(2):
                yield "out", i, [(full512, cols(a["w_out"], l, 512 * i, 512))]
            for i in range(8):
                yield "ff1", i, [(full512, cols(a["w_ffn1"], l, 512 * i, 512))]
            for i in range(8):
                yield "ff2", i, [(lambda s: s.rearrange("p (k n) -> p k n", k=32), cols(a["w_ffn2"], l, 128 * i, 128))]

        slots = [(l, name, i, pieces) for l in range(DEPTH) for name, i, pieces in plan(l)]
        where, counts, total = {}, [0] * NSLOT, 0
        for n, (l, name, i, pieces) in enumerate(slots):
            counts[n % NSLOT] += 16 * len(pieces)
            where[l, name, i] = (n % NSLOT, counts[n % NSLOT])

        def weights(pe, l, name, i=0):
            s, n = where[l, name, i]
            pe.wait_ge(w_full[s], n)
            return wring[:, s, :]

        def slot_read(l, name, i, *key):
            book["last", l, name, i] = key


        @block.tensor
        def _(pe):
            turn["n"] = 0
            mm, tr = nc.tensor.matmul, nc.tensor.transpose

            def project(key, w, m0, ntok, rhs=hT, kn=KC, width=128, inc=True):
                ps = take(pe, *key)
                for t0, t1 in ((0, LAT), (LAT, TOK))[:1 if ntok == LAT else 2]:
                    for k in range(kn):
                        last = mm(ps[:, t0:t1], w[:, k, m0:m0 + width], rhs[:, k, t0:t1],
                                  start=(k == 0), stop=(k == kn - 1))
                last.then_inc(*filled(*key))

            def attention(l, br):
                q, k, v = (qk, qk, va) if br == "A" else (qB, kB, vB)
                work = att_items(l)
                for i in range(len(work) + 2):
                    if i < len(work):
                        h, t = work[i]
                        if i == 0:
                            pe.wait_ge(*(dve_done.at("rope", l, 5) if br == "A" else read("kb", l, 3)))
                            pe.wait_ge(*(read("va", l) if br == "A" else read("vb", l, 5)))
                        lo = HD * (h % 2)
                        kc = 4 + h // 4 if br == "A" else h // 2
                        qs = q[lo:lo + HD, h // 2, t * P:t * P + P]
                        ps = take(pe, "S", br, l, i)
                        if t < LT:
                            mm(ps[:, 0:LAT], qs, k[lo:lo + HD, kc, 0:LAT], start=True, stop=True)
                            last = mm(ps[:, LAT:TOK], qs, k[lo:lo + HD, kc, LAT:TOK], start=True, stop=True)
                        else:
                            last = mm(ps[:, 0:CTX], qs, k[lo:lo + HD, kc, LAT:TOK], start=True, stop=True)
                        last.then_inc(*filled("S", br, l, i))
                    if 1 <= i <= len(work):
                        j = i - 1
                        nk = TT if work[j][1] < LT else TT - LT
                        pe.wait_ge(*dve_done.at("prob", br, l, j))
                        ps = take(pe, "T", br, l, j)
                        for b in range(nk):
                            last = tr(ps[:, b * P:b * P + P], prob[:, j % 2, b * P:b * P + P], ident)
                        last.then_inc(*filled("T", br, l, j))
                    if i >= 2:
                        j = i - 2
                        h, t = work[j]
                        b0 = 0 if t < LT else LT
                        c0 = HD * (h // 4 if br == "A" else h)
                        pe.wait_ge(*read("T", br, l, j))
                        ps = take(pe, "O", br, l, j)
                        for b in range(b0, TT):
                            last = mm(ps[0:HD, 0:P], v[:, b, c0:c0 + HD], probT[:, j % 2, b - b0, :],
                                      start=(b == b0), stop=(b == TT - 1))
                        last.then_inc(*filled("O", br, l, j))

            def norm(l, which, ntok):
                ps = take(pe, "ss", l, which)
                for k in range(KC):
                    pe.wait_ge(*act_done.at("sq", l, which, k))
                    for t0, t1 in ((0, LAT), (LAT, TOK))[:1 if ntok == LAT else 2]:
                        last = mm(ps[:, t0:t1], ones, sq_n[:, k % 2, t0:t1], start=(k == 0), stop=(k == KC - 1))
                    if k < KC - 1:
                        last.then_inc(*pe_done.mark("ss", l, which, k))
                last.then_inc(*filled("ss", l, which))

            pe.wait_ge(*consts_in.at())
            for l in range(DEPTH):
                if l == 0:
                    for t in range(TT):
                        pe.wait_ge(*x_in[t].at())
                        ps = take(pe, "x", t)
                        for k in range(KC):
                            last = tr(ps[:, k * P:k * P + P], r(S0 + 1024 * t, 1024)[:, k * P:k * P + P], ident)
                        last.then_inc(*filled("x", t))
                pe.wait_ge(*params_in.at(l))
                ps = take(pe, "params", l)
                tr(ps[:, 0:P], prow[:, :], ident).then_inc(*filled("params", l))
                pe.wait_ge(*act_done.at("ccol"))
                for i in range(12):
                    w = weights(pe, l, "mod", i).rearrange("p (k n) -> p k n", k=KC)
                    ps = take(pe, "mod", l, i)
                    for m in range(4):
                        for k in range(KC):
                            last = mm(ps[:, 2 * m:2 * m + 2], w[:, k, m * P:m * P + P], ccol[:, :, k],
                                      start=(k == 0), stop=(k == KC - 1))
                    last.then_inc(*filled("mod", l, i))
                    slot_read(l, "mod", i, "mod", l, i)
                norm(l, "mix", TOK)
                pe.wait_ge(*act_done.at("h", l, "mix"))
                w = weights(pe, l, "ba")[:, 0:KC * 16].rearrange("p (k n) -> p k n", k=KC)
                ps = take(pe, "ba", l)
                for t in range(TT):
                    for k in range(KC):
                        last = mm(ps[:, 16 * t:16 * t + 16], hT[:, k, t * P:t * P + P], w[:, k, :],
                                  start=(k == 0), stop=(k == KC - 1))
                last.then_inc(*filled("ba", l))
                slot_read(l, "ba", 0, "ba", l)
                for i in range(3):
                    w = weights(pe, l, "c", i).rearrange("p (k n) -> p k n", k=KC)
                    for m in range(4):
                        project(("c", l, i, m), w, m * P, TOK)
                    slot_read(l, "c", i, "c", l, i, 3)
                for m in range(4):
                    pe.wait_ge(*act_done.at("silu", l, 2, m))
                    ps = take(pe, "vtok", l, m)
                    for t in range(TT):
                        last = tr(ps[:, t * P:t * P + P], vT4[:, m, t * P:t * P + P], ident)
                    last.then_inc(*filled("vtok", l, m))
                for j in range(8):
                    pe.wait_ge(*act_done.at("csq", l, j))
                    ps = take(pe, "css", l, j)
                    for t0, t1 in ((0, LAT), (LAT, TOK)):
                        last = mm(ps[:, t0:t1], ones, csq[:, j % 2, t0:t1], start=True, stop=True)
                    last.then_inc(*filled("css", l, j))
                for h in range(4):
                    pe.wait_ge(*dve_done.at("l2", l, 4 + h))
                    ps = take(pe, "ktok", l, h)
                    for t in range(TT):
                        last = tr(ps[:, t * P:t * P + P], kT[:, h, t * P:t * P + P], ident)
                    last.then_inc(*filled("ktok", l, h))
                pe.wait_ge(*dve_done.at("g", l))
                ps = take(pe, "gc", l)
                for t in range(TT):
                    b = 32 * t
                    mm(ps[:, b:b + 4], cst[:, C_UI:C_UI + P], gt[:, t, 0:4], start=True, stop=True)
                    mm(ps[:, b + 4:b + 8], cst[:, C_LI:C_LI + P], gt[:, t, 4:8], start=True, stop=True)
                    mm(ps[:, b + 8:b + 16], blk, gt[:, t, :], start=True, stop=True)
                    for c in range(2):
                        last = mm(ps[:, b + 16 + 8 * c:b + 24 + 8 * c], blk[:, 64 * c:64 * c + 1].to_broadcast([P, P]),
                                  gt[:, t, :], start=True, stop=True)
                last.then_inc(*filled("gc", l))
                pe.wait_ge(*read("ktok", l, 3))
                for s in range(TT):
                    for d in range(2):
                        t = tiles[d][s]
                        pe.wait_ge(*pool_done.at("R", l, s, d))
                        ps = take(pe, "bc", l, s, d)
                        mm(ps[:, 0:512], ones, flat(rbuf[d]), start=True, stop=True).then_inc(*filled("bc", l, s, d))
                        ps = take(pe, "G", l, s, d)
                        for h in range(C_H):
                            kk = kT[:, h, t * P:t * P + P]
                            mm(ps[:, h * P:h * P + P], kk, kk, start=True, stop=True)
                            last = mm(ps[:, 512 + h * P:512 + h * P + P], kk, qT[:, h, t * P:t * P + P],
                                      start=True, stop=True)
                        last.then_inc(*filled("G", l, s, d))
                    for d in range(2):
                        pe.wait_ge(*dve_done.at("A", l, s, d))
                        ps = take(pe, "AT", l, s, d)
                        for h in range(C_H):
                            last = tr(ps[:, h * P:h * P + P], pbuf[d][:, h, :], ident)
                        last.then_inc(*filled("AT", l, s, d))
                    for i in range(5):
                        for d in range(2):
                            src, srcT, dst, dstT = power(d, i)
                            pe.wait_ge(*(read("pw", l, s, d, i - 1) if i else read("AT", l, s, d)))
                            ps = take(pe, "pw", l, s, d, i)
                            for h in range(C_H):
                                last = mm(ps[:, h * P:h * P + P], srcT[:, h, :], src[:, h, :], start=True, stop=True)
                                if i < 4:
                                    last = mm(ps[:, 512 + h * P:512 + h * P + P], src[:, h, :], srcT[:, h, :],
                                              start=True, stop=True)
                            last.then_inc(*filled("pw", l, s, d, i))
                        for d in range(2):
                            src, srcT, dst, dstT = power(d, i)
                            pe.wait_ge(*read("pw", l, s, d, i))
                            pe.wait_ge(*(read("X", l, s, d, i - 1) if i else read("AT", l, s, d)))
                            ps = take(pe, "X", l, s, d, i)
                            for h in range(C_H):
                                last = mm(ps[:, h * P:h * P + P], dst[:, h, :], xbuf[d][:, h, :], start=True, stop=True)
                            last.then_inc(*filled("X", l, s, d, i))
                    for d in range(2):
                        pe.wait_ge(*pool_done.at("kbe", l, s, d))
                        pe.wait_ge(*read("X", l, s, d, 4))
                        ps = take(pe, "kcd", l, s, d)
                        for h in range(C_H):
                            last = mm(ps[:, h * P:h * P + P], wbuf[d][:, h, :], xbuf[d][:, h, :], start=True, stop=True)
                        last.then_inc(*filled("kcd", l, s, d))
                    for c in range(2):
                        for d in range(2):
                            t, cc, n = tiles[d][s], (c if d == 0 else 1 - c), 2 * s + c
                            lo, hi = 64 * cc, 64 * cc + 64
                            S = state[:, n % 2, :, :]
                            if c == 0:
                                pe.wait_ge(*read("kcd", l, s, d))
                                pe.wait_ge(*pool_done.at("vb", l, s, d))
                            pe.wait_ge(*(read("so", l, n - 1, d) if n else dve_done.at("S0", l)))
                            ps = take(pe, "vn", l, n, d)
                            for h in range(C_H):
                                o = ps[0:64, h * P:h * P + P]
                                mm(o, ebuf[d][:, h, lo:hi], S[:, 4 * d + h, :], start=True, stop=False)
                                last = mm(o, xbuf[d][lo:hi, h, lo:hi], vbbuf[d][lo:hi, h, :], start=False, stop=True)
                            last.then_inc(*filled("vn", l, n, d))
                        for d in range(2):
                            t, cc, n = tiles[d][s], (c if d == 0 else 1 - c), 2 * s + c
                            lo, hi = 64 * cc, 64 * cc + 64
                            S = state[:, n % 2, :, :]
                            pe.wait_ge(*read("vn", l, n, d))
                            pe.wait_ge(*pool_done.at("kd", l, s, d))
                            pe.wait_ge(*pool_done.at("AQ", l, s, d))
                            ps = take(pe, "so", l, n, d)
                            for h in range(C_H):
                                vn = tbuf[d][lo:hi, h, :]
                                last = mm(ps[:, h * P:h * P + P], pbuf[d][lo:hi, h, :], vn, start=True, stop=True)
                            if want_out(l, t):
                                for h in range(C_H):
                                    o = ps[0:64, 512 + h * P:512 + h * P + P]
                                    mm(o, qdbuf[d][:, h, lo:hi], S[:, 4 * d + h, :], start=True, stop=False)
                                    last = mm(o, aqbuf[d][lo:hi, h, lo:hi], tbuf[d][lo:hi, h, :], start=False, stop=True)
                            last.then_inc(*filled("so", l, n, d))
                w = weights(pe, l, "z").rearrange("p (k n) -> p k n", k=KC)
                for m in range(4):
                    project(("z", l, m), w, m * P, TOK if l == 0 else LAT)
                slot_read(l, "z", 0, "z", l, 3)
                for t in range(TT if l == 0 else LT):
                    pe.wait_ge(*dve_done.at("onrm", l))
                    ps = take(pe, "oT", l, t)
                    for h in range(C_H):
                        last = tr(ps[:, h * P:h * P + P], Otok[:, t, h * P:h * P + P], ident)
                    last.then_inc(*filled("oT", l, t))
                pe.wait_ge(*read("oT", l, (TT if l == 0 else LT) - 1))
                w = weights(pe, l, "qa").rearrange("p (k n) -> p k n", k=KC)
                for m in range(4):
                    project(("qk", l, m), w, m * P, TOK if l == 0 else LAT)
                slot_read(l, "qa", 0, "qk", l, 3)
                w = weights(pe, l, "kva").rearrange("p (k n) -> p k n", k=KC)
                for m in range(2):
                    project(("qk", l, 4 + m), w, m * P, TOK)
                ps = take(pe, "va", l)
                for t in range(TT):
                    for k in range(KC):
                        last = mm(ps[:, t * P:t * P + P], hT[:, k, t * P:t * P + P], w[:, k, 256:384],
                                  start=(k == 0), stop=(k == KC - 1))
                last.then_inc(*filled("va", l))
                slot_read(l, "kva", 0, "va", l)
                for j in range(6):
                    n = TOK if (l == 0 or j >= 4) else LAT
                    pe.wait_ge(*act_done.at("asq", l, j))
                    ps = take(pe, "ass", l, j)
                    for t0, t1 in ((0, LAT), (LAT, TOK))[:1 if n == LAT else 2]:
                        last = mm(ps[:, t0:t1], blk, asq[:, t0:t1], start=True, stop=True)
                    last.then_inc(*filled("ass", l, j))
                    pe.wait_ge(*dve_done.at("qkn", l, j))
                    ps = take(pe, "rot", l, j)
                    mm(ps[:, 0:LAT], rot, qk[:, j, 0:LAT], start=True, stop=True).then_inc(*filled("rot", l, j))
                attention(l, "A")
                w = weights(pe, l, "qb").rearrange("p (k n) -> p k n", k=KC)
                for m in range(4):
                    project(("qb", l, m), w, m * P, TOK if l == 0 else LAT)
                slot_read(l, "qb", 0, "qb", l, 3)
                w = weights(pe, l, "kb").rearrange("p (k n) -> p k n", k=KC)
                for m in range(4):
                    project(("kb", l, m), w, m * P, TOK)
                slot_read(l, "kb", 0, "kb", l, 3)
                w = weights(pe, l, "vb").rearrange("p (k n) -> p k n", k=KC)
                for t in range(TT):
                    ps = take(pe, "vb", l, t)
                    for k in range(KC):
                        last = mm(ps[:, 0:512], hT[:, k, t * P:t * P + P], w[:, k, :], start=(k == 0), stop=(k == KC - 1))
                    last.then_inc(*filled("vb", l, t))
                slot_read(l, "vb", 0, "vb", l, 5)
                attention(l, "B")
                nt = TOK if l == 0 else LAT
                for half in range(2):
                    for n, o in enumerate((oA, oB, oC)):
                        w = weights(pe, l, "gate", 3 * half + n).rearrange("p (k n) -> p k n", k=KC)
                        wb = weights(pe, l, "br", 3 * half + n)[:, 0:2048].rearrange("p (k n) -> p k n", k=4)
                        for m in range(4):
                            project(("gate", l, half, n, m), w, m * P, nt)
                            project(("br", l, half, n, m), wb, m * P, nt, rhs=o, kn=4)
                        slot_read(l, "gate", 3 * half + n, "gate", l, half, n, 3)
                        slot_read(l, "br", 3 * half + n, "br", l, half, n, 3)
                pe.wait_ge(*pool_done.at("merge", l, 1, 2, 3))
                for i in range(2):
                    w = weights(pe, l, "out", i).rearrange("p (k n) -> p k n", k=KC)
                    for m in range(4):
                        project(("out", l, 4 * i + m), w, m * P, nt, rhs=mT)
                    slot_read(l, "out", i, "out", l, 4 * i + 3)
                norm(l, "ffn", nt)
                pe.wait_ge(*act_done.at("h", l, "ffn"))
                for i in range(8):
                    w = weights(pe, l, "ff1", i).rearrange("p (k n) -> p k n", k=KC)
                    for m in range(4):
                        project(("ff1", l, 4 * i + m), w, m * P, nt)
                    slot_read(l, "ff1", i, "ff1", l, 4 * i + 3)
                pe.wait_ge(*pool_done.at("ff1", l, 31))
                for i in range(8):
                    w = weights(pe, l, "ff2", i).rearrange("p (k n) -> p k n", k=32)
                    project(("ff2", l, i), w, 0, nt, rhs=fT, kn=32)
                    slot_read(l, "ff2", i, "ff2", l, i)
            pe.wait_ge(*params_in.at(DEPTH))
            ps = take(pe, "params", DEPTH)
            tr(ps[:, 0:KC], prow[0:KC, :], ident[0:KC, 0:KC]).then_inc(*filled("params", DEPTH))
            norm(DEPTH, "fin", LAT)
            pe.wait_ge(*act_done.at("h", DEPTH, "fin"))
            for t in range(LT):
                ps = take(pe, "fin", t)
                for k in range(KC):
                    last = tr(ps[:, k * P:k * P + P], hT[:, k, t * P:t * P + P], ident)
                last.then_inc(*filled("fin", t))

        def spans(n):
            return ((0, LAT, 0), (LAT, TOK, 1))[:1 if n == LAT else 2]

        def merge_item(x):
            return x // 12, x // 4 % 3, x % 4

        def attention(eng, l, br):
            work = att_items(l)
            for i in range(len(work) + 1):
                if i < len(work):
                    n = TOK if work[i][1] < LT else CTX
                    eng.wait_ge(*dve_done.at("nm", br, l, i))
                    if i >= 2:
                        eng.wait_ge(*full("T", br, l, i - 2))
                    nc.scalar.activation(prob[:, i % 2, 0:n], pair("S", br, l, i)[:, 0:n], ACT.Exp, scale=SCALE,
                                         bias=stat[:, i % 2, 1:2], accum_out=stat[:, i % 2, 2:3])\
                        .then_inc(*free("S", br, l, i))
                if i:
                    j = i - 1
                    nb = TT if work[j][1] < LT else TT - LT
                    eng.wait_ge(*full("T", br, l, j))
                    if j >= 2:
                        eng.wait_ge(*full("O", br, l, j - 2))
                    nc.scalar.activation(probT[:, j % 2, 0:nb, :],
                                         pair("T", br, l, j)[:, 0:nb * P].rearrange("p (b n) -> p b n", b=nb), ACT.Copy)\
                        .then_inc(*free("T", br, l, j))

        @block.sync
        def _(sp):
            sp.dma_start(cst[:, :], a["consts"]).then_inc(*consts_in.mark(by=16))
            for t in range(TT):
                src = a["x"][0, t * P:t * P + P, :] if t < LT else a["ctx"][0, (t - LT) * P:(t - LT) * P + P, :]
                sp.dma_start(r(S0 + 1024 * t, 1024), src).then_inc(*x_in[t].mark(by=16))
            for n, (l, name, i, pieces) in enumerate(slots):
                if n >= NSLOT:
                    sp.wait_ge(*full(*book.get(("last",) + slots[n - NSLOT][:3], ("x", 0))))
                for dst, src in pieces:
                    sp.dma_start(dst(wring[:, n % NSLOT, :]), src).then_inc(w_full[n % NSLOT], 16)
            for t in range(LT):
                sp.wait_ge(*read("fin", t))
                sp.dma_start(out[0, t * P:t * P + P, :], r(S0 + 1024 * t, 1024)).then_inc(*out_done.mark(t, by=16))
            sp.wait_ge(*out_done.at(LT - 1))

        @block.scalar
        def _(act):
            A = nc.scalar.activation

            def norm(l, which, ntok):
                for k in range(KC):
                    if l == 0 and which == "mix":
                        if k == 0:
                            act.wait_ge(*read("x", TT - 1))
                    else:
                        act.wait_ge(*read({"mix": "ff2", "ffn": "out", "fin": "ff2"}[which], l - (which != "ffn"), k))
                    if k >= 2:
                        act.wait_ge(*pe_done.at("ss", l, which, k - 2))
                    elif k == 0 and which == "fin":
                        act.wait_ge(*read("ff2", l - 1, KC - 1))
                    A(sq_n[:, k % 2, 0:ntok], xT[:, k, 0:ntok], ACT.Square).then_inc(*act_done.mark("sq", l, which, k))
                act.wait_ge(*full("ss", l, which))
                act.wait_ge(*dve_done.at("eps"))
                A(rs_n[:, 0:ntok], pair("ss", l, which)[:, 0:ntok], ACT.Sqrt, scale=1.0 / D, bias=eps[:, 0:1])\
                    .then_inc(*free("ss", l, which))
                for k in range(KC):
                    act.wait_ge(*dve_done.at("hx", l, which, k))
                    for t0, t1, c in spans(ntok):
                        if which == "fin":
                            last = A(hT[:, k, t0:t1], hT[:, k, t0:t1], ACT.Copy, scale=pcol[:, k:k + 1])
                        else:
                            w = which == "ffn"
                            last = A(hT[:, k, t0:t1], hT[:, k, t0:t1], ACT.Identity, scale=gain[:, int(w), k, c:c + 1],
                                     bias=modc[:, 24 * w + k, c:c + 1])
                        if k < KC - 1 or t1 < ntok:
                            last.then_inc(*act_done.mark("hk", l, which, k, c))
                last.then_inc(*act_done.mark("h", l, which))

            act.wait_ge(*cond_in.at())
            A(ccol[:, :, :], craw_c[:, :, :], ACT.Silu).then_inc(*act_done.mark("ccol"))
            for l in range(DEPTH):
                nt = TOK if l == 0 else LAT
                if l == 0:
                    for t in range(TT):
                        act.wait_ge(*full("x", t))
                        A(xT[:, :, t * P:t * P + P], pair("x", t)[:, :].rearrange("p (k n) -> p k n", k=KC), ACT.Copy)\
                            .then_inc(*free("x", t))
                norm(l, "mix", TOK)
                act.wait_ge(*full("ba", l))
                A(bg[:, :, 0:8], pair("ba", l)[:, 0:96].rearrange("p (t n) -> p t n", t=TT)[:, :, 0:8], ACT.Sigmoid)\
                    .then_inc(*free("ba", l, by=1))
                act.wait_ge(*dve_done.at("absa", l))
                A(gtmp[:, :, :], gtmp[:, :, :], ACT.Exp, scale=-1.0).then_inc(*act_done.mark("expa", l))
                act.wait_ge(*dve_done.at("1+e", l))
                A(gtmp[:, :, :], gtmp[:, :, :], ACT.Ln).then_inc(*act_done.mark("lna", l))
                act.wait_ge(*abc_in.at(l))
                A(abc[:, 0, :], abc[:, 0, :], ACT.Exp).then_inc(*act_done.mark("expA", l))
                act.wait_ge(*dve_done.at("craw0", l))

                def silu(j):
                    i, m = divmod(j, 4)
                    act.wait_ge(*dve_done.at("conv", l, j))
                    o = (qT, kT, vT4)[i][:, m, :]
                    A(o[:, 0:LAT], cacc[:, j % 2, 0:LAT], ACT.Silu).then_inc(*act_done.mark("silu0", l, i, m))
                    A(o[:, LAT:TOK], cacc[:, j % 2, LAT + 4:TOK + 4], ACT.Silu).then_inc(*act_done.mark("silu", l, i, m))

                for j in range(12):
                    i, m = divmod(j, 4)
                    act.wait_ge(*full("c", l, i, m))
                    if j >= 2:
                        act.wait_ge(*dve_done.at("conv", l, j - 2))
                    ps = pair("c", l, i, m)
                    A(craw[:, j % 2, 2:2 + LAT], ps[:, 0:LAT], ACT.Copy).then_inc(*free("c", l, i, m, by=1))
                    A(craw[:, j % 2, LAT + 6:TOK + 6], ps[:, LAT:TOK], ACT.Copy).then_inc(*free("c", l, i, m, by=1))
                    if j:
                        silu(j - 1)
                silu(11)
                for j in range(9):
                    if j < 8:
                        x = (qT, kT)[j // 4][:, j % 4, :]
                        if j == 0:
                            act.wait_ge(*act_done.at("silu", l, 2, 3))
                        if j >= 2:
                            act.wait_ge(*full("css", l, j - 2))
                        A(csq[:, j % 2, :], x, ACT.Square).then_inc(*act_done.mark("csq", l, j))
                    if j:
                        act.wait_ge(*full("css", l, j - 1))
                        if j >= 3:
                            act.wait_ge(*dve_done.at("l2", l, j - 3))
                        A(crr[:, (j - 1) % 2, :], pair("css", l, j - 1)[:, 0:TOK], ACT.Sqrt, bias=eps[:, 0:1])\
                            .then_inc(*free("css", l, j - 1))
                act.wait_ge(*read("gc", l))
                A(gex[:, :, 0, :], gcs[:, :, 0:8], ACT.Exp).then_inc(*act_done.mark("gex0", l))
                A(gex[:, :, 2:4, :].rearrange("p t a b -> p t (a b)"), gcs[:, :, 16:32], ACT.Exp)\
                    .then_inc(*act_done.mark("gex2", l))
                act.wait_ge(*dve_done.at("gdiff", l))
                A(gex[:, :, 1, :], gtmp[:, :, :], ACT.Exp).then_inc(*act_done.mark("gex1", l))
                for s in range(TT):
                    for d in range(2):
                        act.wait_ge(*full("bc", l, s, d))
                        if s:
                            act.wait_ge(*full("vn", l, 2 * s - 1, d))
                        A(flat(ebuf[d]), pair("bc", l, s, d)[:, 0:512], ACT.Exp).then_inc(*free("bc", l, s, d, by=1))
                        act.wait_ge(*read("bc", l, s, d))
                        A(flat(wbuf[d]), flat(wbuf[d]), ACT.Abs).then_inc(*act_done.mark("abs", l, s, d))
                        act.wait_ge(*act_done.at("abs", l, s, d))
                        A(flat(wbuf[d]), flat(wbuf[d]), ACT.Exp, scale=-1.0).then_inc(*act_done.mark("W", l, s, d))
                    for i in range(5):
                        for d in range(2):
                            act.wait_ge(*full("pw", l, s, d, i))
                            if i == 0:
                                act.wait_ge(*dve_done.at("A", l, s, d))
                            A(flat(power(d, i)[2]), pair("pw", l, s, d, i)[:, 0:512], ACT.Copy)\
                                .then_inc(*free("pw", l, s, d, i, by=1 if i < 4 else 2))
                    for d in range(2):
                        act.wait_ge(*full("kcd", l, s, d))
                        act.wait_ge(*pool_done.at("qd", l, s, d))
                        A(flat(ebuf[d]), pair("kcd", l, s, d)[:, 0:512], ACT.Copy, scale=-1.0)\
                            .then_inc(*free("kcd", l, s, d))
                    for c in range(2):
                        for d in range(2):
                            n, lo = 2 * s + c, 64 * (c if d == 0 else 1 - c)
                            act.wait_ge(*full("vn", l, n, d))
                            A(flat(tbuf[d])[lo:lo + 64, :], pair("vn", l, n, d)[0:64, 0:512], ACT.Copy)\
                                .then_inc(*free("vn", l, n, d))
                for m in range(4):
                    act.wait_ge(*full("z", l, m))
                    A(siluz[:, m, 0:nt], pair("z", l, m)[:, 0:nt], ACT.Silu).then_inc(*free("z", l, m))
                act.wait_ge(*dve_done.at("oss", l))
                A(small[:, 0:24], small[:, 0:24], ACT.Sqrt, scale=1.0 / P, bias=eps[:, 0:1])\
                    .then_inc(*act_done.mark("ors", l))
                for j in range(6):
                    n = TOK if j >= 4 else nt
                    act.wait_ge(*full("qk", l, j))
                    A(qk[:, j, 0:n], pair("qk", l, j)[:, 0:n], ACT.Copy).then_inc(*free("qk", l, j))
                act.wait_ge(*full("va", l))
                A(flat(va), pair("va", l)[:, 0:TOK], ACT.Copy).then_inc(*free("va", l))
                act.wait_ge(*read("va", l))
                for j in range(6):
                    n = TOK if j >= 4 else nt
                    if j:
                        act.wait_ge(*full("ass", l, j - 1))
                        act.wait_ge(*dve_done.at("qkn", l, j - 1))
                    A(asq[:, 0:n], qk[:, j, 0:n], ACT.Square).then_inc(*act_done.mark("asq", l, j))
                    act.wait_ge(*full("ass", l, j))
                    A(arr[:, 0:n], pair("ass", l, j)[:, 0:n], ACT.Sqrt, scale=1.0 / HD, bias=eps[:, 0:1])\
                        .then_inc(*free("ass", l, j))
                attention(act, l, "A")
                for name, dst in (("qb", qB), ("kb", kB)):
                    n = TOK if name == "kb" else nt
                    for m in range(4):
                        act.wait_ge(*full(name, l, m))
                        A(dst[:, m, 0:n], pair(name, l, m)[:, 0:n], ACT.Copy).then_inc(*free(name, l, m))
                for t in range(TT):
                    act.wait_ge(*full("vb", l, t))
                    A(vB[:, t, :], pair("vb", l, t)[:, 0:512], ACT.Copy).then_inc(*free("vb", l, t))
                attention(act, l, "B")
                for x in range(24):
                    half, n, m = x // 12, x // 4 % 3, x % 4
                    act.wait_ge(*full("gate", l, half, n, m))
                    if x >= 2:
                        act.wait_ge(*read("br", l, *merge_item(x - 2)))
                        if merge_item(x - 2)[1]:
                            act.wait_ge(*pool_done.at("merge", l, *merge_item(x - 2)))
                    A(gsig[:, x % 2, 0:nt], pair("gate", l, half, n, m)[:, 0:nt], ACT.Sigmoid)\
                        .then_inc(*free("gate", l, half, n, m))
                norm(l, "ffn", nt)
                for j in range(32):
                    act.wait_ge(*full("ff1", l, j))
                    A(fT[:, j, 0:nt], pair("ff1", l, j)[:, 0:nt], ACT.Relu).then_inc(*free("ff1", l, j))
            norm(DEPTH, "fin", LAT)
            for t in range(LT):
                act.wait_ge(*full("fin", t))
                A(r(S0 + 1024 * t, 1024), pair("fin", t)[:, :], ACT.Copy).then_inc(*free("fin", t))

        @block.vector
        def _(dve):
            V = nc.vector

            def norm(l, which, ntok):
                dve.wait_ge(*read("ss", l, which))
                V.reciprocal(rs_n[:, 0:ntok], rs_n[:, 0:ntok]).then_inc(*dve_done.mark("rs", l, which))
                dve.wait_ge(*dve_done.at("rs", l, which))
                for k in range(KC):
                    V.tensor_tensor(hT[:, k, 0:ntok], xT[:, k, 0:ntok], rs_n[:, 0:ntok], ALU.mult)\
                        .then_inc(*dve_done.mark("hx", l, which, k))

            def attention(l, br):
                work = att_items(l)
                o = oA if br == "A" else oB
                for i in range(len(work) + 3):
                    if i < len(work):
                        h, t = work[i]
                        n = TOK if t < LT else CTX
                        dve.wait_ge(*full("S", br, l, i))
                        ps = pair("S", br, l, i)
                        if br == "B" and t < LT:
                            dve.wait_ge(*pool_done.at("E", l, h))
                            V.tensor_tensor(ps[:, 0:LAT], ps[:, 0:LAT],
                                            ebias[:, h % 2, 6 - 2 * t + 0:14 - 2 * t, :].rearrange("p a b -> p (a b)"),
                                            ALU.add).then_inc(*dve_done.mark("bias", l, i))
                            dve.wait_ge(*dve_done.at("bias", l, i))
                        if i >= 2:
                            dve.wait_ge(*read("S", br, l, i - 2))
                        V.tensor_reduce(stat[:, i % 2, 0:1], ps[:, 0:n], AX.X, ALU.max, negate=True)\
                            .then_inc(*dve_done.mark("max", br, l, i))
                        dve.wait_ge(*dve_done.at("max", br, l, i))
                        V.tensor_scalar(stat[:, i % 2, 1:2], stat[:, i % 2, 0:1], SCALE, None, ALU.mult)\
                            .then_inc(*dve_done.mark("nm", br, l, i))
                    if 1 <= i <= len(work):
                        j = i - 1
                        n = TOK if work[j][1] < LT else CTX
                        dve.wait_ge(*read("S", br, l, j))
                        V.reciprocal(stat[:, j % 2, 3:4], stat[:, j % 2, 2:3]).then_inc(*dve_done.mark("rsum", br, l, j))
                        dve.wait_ge(*dve_done.at("rsum", br, l, j))
                        V.tensor_scalar(prob[:, j % 2, 0:n], prob[:, j % 2, 0:n], stat[:, j % 2, 3:4], None, ALU.mult)\
                            .then_inc(*dve_done.mark("prob", br, l, j))
                    if i >= 3:
                        j = i - 3
                        h, t = work[j]
                        dve.wait_ge(*full("O", br, l, j))
                        lo = HD * (h % 2)
                        V.tensor_copy(o[lo:lo + HD, h // 2, t * P:t * P + P], pair("O", br, l, j)[0:HD, 0:P])\
                            .then_inc(*free("O", br, l, j))

            V.memset(eps[:, :], EPS).then_inc(*dve_done.mark("eps"))
            for l in range(DEPTH):
                nt = TOK if l == 0 else LAT
                dve.wait_ge(*full("params", l))
                V.tensor_copy(pcol[:, :], pair("params", l)[:, 0:P]).then_inc(*free("params", l))
                dve.wait_ge(*read("params", l))
                for i in range(12):
                    dve.wait_ge(*full("mod", l, i))
                    V.tensor_tensor(modc[:, 4 * i:4 * i + 4, :],
                                    pair("mod", l, i)[:, 0:8].rearrange("p (m c) -> p m c", m=4),
                                    along(pcol[:, R_BMOD + 4 * i:R_BMOD + 4 * i + 4], 2), ALU.add)\
                        .then_inc(*free("mod", l, i))
                dve.wait_ge(*read("mod", l, 11))
                for w in range(2):
                    V.scalar_tensor_tensor(out=gain[:, w, :, :], in0=modc[:, 24 * w + 8:24 * w + 16, :], scalar=1.0,
                                           in1=along(pcol[:, R_MIX + 8 * w:R_MIX + 8 * w + 8], 2),
                                           op0=ALU.add, op1=ALU.mult).then_inc(*dve_done.mark("gain", l, w))
                norm(l, "mix", TOK)
                dve.wait_ge(*read_first("ba", l))
                dve.wait_ge(*abc_in.at(l))
                V.tensor_tensor(gt[:, :, :], pair("ba", l)[:, 0:96].rearrange("p (t n) -> p t n", t=TT)[:, :, 8:16],
                                abc[:, 1, :].unsqueeze(1).to_broadcast([P, TT, 8]), ALU.add)\
                    .then_inc(*free("ba", l, by=1))
                dve.wait_ge(*read("ba", l))
                V.scalar_tensor_tensor(out=gtmp[:, :, :], in0=gt[:, :, :], scalar=-1.0, in1=gt[:, :, :],
                                       op0=ALU.mult, op1=ALU.max).then_inc(*dve_done.mark("absa", l))
                dve.wait_ge(*act_done.at("expa", l))
                V.tensor_scalar(gtmp[:, :, :], gtmp[:, :, :], 1.0, None, ALU.add).then_inc(*dve_done.mark("1+e", l))
                dve.wait_ge(*act_done.at("lna", l))
                V.scalar_tensor_tensor(out=gt[:, :, :], in0=gt[:, :, :], scalar=0.0, in1=gtmp[:, :, :],
                                       op0=ALU.max, op1=ALU.add).then_inc(*dve_done.mark("sp", l))
                dve.wait_ge(*act_done.at("expA", l))
                dve.wait_ge(*dve_done.at("sp", l))
                V.scalar_tensor_tensor(out=gt[:, :, :], in0=gt[:, :, :], scalar=-1.0,
                                       in1=abc[:, 0, :].unsqueeze(1).to_broadcast([P, TT, 8]),
                                       op0=ALU.mult, op1=ALU.mult).then_inc(*dve_done.mark("g", l))
                V.tensor_scalar(nbeta[:, :, :], bg[:, :, 0:8], -1.0, None, ALU.mult).then_inc(*dve_done.mark("nbeta", l))
                if l:
                    dve.wait_ge(*read("ff2", l - 1, KC - 1))
                V.memset(craw[:, :, :], 0.0).then_inc(*dve_done.mark("craw0", l))
                W = TOK + 4
                for j in range(12):
                    dve.wait_ge(*read("c", l, j // 4, j % 4))
                    if j >= 2:
                        dve.wait_ge(*act_done.at("silu", l, (j - 2) // 4, (j - 2) % 4))
                    for q in range(CONV):
                        tap = pcol[:, R_CONV + 12 * q + j:R_CONV + 12 * q + j + 1]
                        if q == 0:
                            ins = V.tensor_scalar(cacc[:, j % 2, 0:W], craw[:, j % 2, 0:W], tap, None, ALU.mult)
                        else:
                            dve.wait_ge(*dve_done.at("tap", l, j, q - 1))
                            ins = V.scalar_tensor_tensor(out=cacc[:, j % 2, 0:W], in0=craw[:, j % 2, q:q + W],
                                                         scalar=tap, in1=cacc[:, j % 2, 0:W], op0=ALU.mult, op1=ALU.add)
                        ins.then_inc(*dve_done.mark(*(("tap", l, j, q) if q < CONV - 1 else ("conv", l, j))))
                for m in range(4):
                    dve.wait_ge(*full("vtok", l, m))
                    V.tensor_copy(vtok[:, :, m * P:m * P + P],
                                  pair("vtok", l, m)[:, 0:TOK].rearrange("p (t n) -> p t n", t=TT))\
                        .then_inc(*free("vtok", l, m))
                for j in range(8):
                    x = (qT, kT)[j // 4][:, j % 4, :]
                    dve.wait_ge(*read("css", l, j))
                    V.reciprocal(crr[:, j % 2, :], crr[:, j % 2, :]).then_inc(*dve_done.mark("crr", l, j))
                    dve.wait_ge(*dve_done.at("crr", l, j))
                    V.scalar_tensor_tensor(out=x, in0=x, scalar=float(P) ** -0.5 if j < 4 else 1.0,
                                           in1=crr[:, j % 2, :], op0=ALU.mult, op1=ALU.mult)\
                        .then_inc(*dve_done.mark("l2", l, j))
                for h in range(4):
                    dve.wait_ge(*full("ktok", l, h))
                    V.tensor_copy(ktok[:, :, h * P:h * P + P],
                                  pair("ktok", l, h)[:, 0:TOK].rearrange("p (t n) -> p t n", t=TT))\
                        .then_inc(*free("ktok", l, h))
                dve.wait_ge(*full("gc", l))
                V.tensor_copy(gcs[:, :, :], pair("gc", l)[:, 0:32 * TT].rearrange("p (t n) -> p t n", t=TT))\
                    .then_inc(*free("gc", l))
                dve.wait_ge(*read("gc", l))
                V.tensor_tensor(gtmp[:, :, :], gcs[:, :, 8:16], gcs[:, :, 0:8], ALU.subtract)\
                    .then_inc(*dve_done.mark("gdiff", l))
                dve.wait_ge(*act_done.at("gex0", l))
                V.tensor_tensor(gex[:, :, 0, :], gex[:, :, 0, :], bg[:, :, 0:8], ALU.mult)\
                    .then_inc(*dve_done.mark("gb", l))
                V.memset(state[:, 0, :, :], 0.0).then_inc(*dve_done.mark("S0", l))
                seen = set()
                for s in range(TT):
                    for d in range(2):
                        t = tiles[d][s]
                        dve.wait_ge(*read_first("bc", l, s, d))
                        if s:
                            dve.wait_ge(*full("kcd", l, s - 1, d))
                        V.tensor_tensor(wbuf[d], pair("bc", l, s, d)[:, 0:512].rearrange("p (h n) -> p h n", h=C_H),
                                        along(gcs[:, t, 4 * d:4 * d + 4]), ALU.subtract)\
                            .then_inc(*free("bc", l, s, d, by=1))
                        dve.wait_ge(*act_done.at("W", l, s, d))
                        dve.wait_ge(*full("G", l, s, d))
                        if s:
                            dve.wait_ge(*full("so", l, 2 * s - 1, d))
                        ps = pair("G", l, s, d)
                        V.tensor_tensor(flat(pbuf[d]), ps[:, 0:512], flat(wbuf[d]), ALU.mult)\
                            .then_inc(*free("G", l, s, d, by=1))
                        V.tensor_tensor(flat(aqbuf[d]), ps[:, 512:1024], flat(wbuf[d]), ALU.mult)\
                            .then_inc(*free("G", l, s, d, by=1))
                        dve.wait_ge(*read("G", l, s, d))
                        dve.wait_ge(*pool_done.at("MB", l, s, d))
                        V.tensor_tensor(pbuf[d], pbuf[d], p2buf[d], ALU.mult).then_inc(*dve_done.mark("A", l, s, d))
                    for d in range(2):
                        dve.wait_ge(*full("AT", l, s, d))
                        ps = pair("AT", l, s, d)
                        V.tensor_copy(flat(tbuf[d]), ps[:, 0:512]).then_inc(*free("AT", l, s, d, by=1))
                        V.tensor_tensor(xbuf[d], ps[:, 0:512].rearrange("p (h n) -> p h n", h=C_H), over_heads(ident),
                                        ALU.add).then_inc(*free("AT", l, s, d, by=1))
                    for i in range(5):
                        if i < 4:
                            for d in range(2):
                                dve.wait_ge(*full("pw", l, s, d, i))
                                V.tensor_copy(flat(power(d, i)[3]), pair("pw", l, s, d, i)[:, 512:1024])\
                                    .then_inc(*free("pw", l, s, d, i, by=1))
                        for d in range(2):
                            dve.wait_ge(*full("X", l, s, d, i))
                            V.tensor_tensor(flat(xbuf[d]), pair("X", l, s, d, i)[:, 0:512], flat(xbuf[d]), ALU.add)\
                                .then_inc(*free("X", l, s, d, i))
                    for c in range(2):
                        for d in range(2):
                            t, cc, n = tiles[d][s], (c if d == 0 else 1 - c), 2 * s + c
                            lo = 64 * cc
                            ps = pair("so", l, n, d)
                            dve.wait_ge(*full("so", l, n, d))
                            if want_out(l, t):
                                o = Otok[lo:lo + 64, t, :]
                                if (t, cc) in seen:
                                    V.tensor_tensor(o, ps[0:64, 512:1024], o, ALU.add).then_inc(*free("so", l, n, d, by=1))
                                else:
                                    V.tensor_copy(o, ps[0:64, 512:1024]).then_inc(*free("so", l, n, d, by=1))
                                seen.add((t, cc))
                            dve.wait_ge(*pool_done.at("Sdec", l, n, d))
                            S1 = state[:, (n + 1) % 2, 4 * d:4 * d + 4, :].rearrange("p a b -> p (a b)")
                            V.tensor_tensor(S1, ps[:, 0:512], S1, ALU.add)\
                                .then_inc(*free("so", l, n, d, by=1 if want_out(l, t) else 2))
                to = TT if l == 0 else LT
                dve.wait_ge(*pool_done.at("osq", l))
                V.tensor_reduce(small[:, 0:4 * to], osq[:, 0:to, :].rearrange("p t (h n) -> p (t h) n", h=C_H), AX.X,
                                ALU.add).then_inc(*dve_done.mark("oss", l))
                dve.wait_ge(*act_done.at("ors", l))
                V.reciprocal(small[:, 32:32 + 4 * to], small[:, 0:4 * to]).then_inc(*dve_done.mark("orr", l))
                dve.wait_ge(*dve_done.at("orr", l))
                ov = Otok[:, 0:to, :].rearrange("p t (h n) -> p (t h) n", h=C_H)
                V.tensor_tensor(ov, ov, along(small[:, 32:32 + 4 * to]), ALU.mult).then_inc(*dve_done.mark("onrm", l))
                for t in range(to):
                    dve.wait_ge(*full("oT", l, t))
                    if t == 0:
                        dve.wait_ge(*read("z", l, 3))
                    V.scalar_tensor_tensor(out=oC[:, :, t * P:t * P + P],
                                           in0=pair("oT", l, t)[:, 0:512].rearrange("p (h n) -> p h n", h=C_H),
                                           scalar=pcol[:, R_ONORM:R_ONORM + 1], in1=siluz[:, :, t * P:t * P + P],
                                           op0=ALU.mult, op1=ALU.mult).then_inc(*free("oT", l, t))
                for j in range(6):
                    n = TOK if j >= 4 else nt
                    dve.wait_ge(*read("ass", l, j))
                    V.reciprocal(arr[:, 0:n], arr[:, 0:n]).then_inc(*dve_done.mark("arr", l, j))
                    dve.wait_ge(*dve_done.at("arr", l, j))
                    g = pcol[:, (R_QN if j < 4 else R_KN):(R_QN if j < 4 else R_KN) + 1]
                    V.scalar_tensor_tensor(out=qk[:, j, 0:n], in0=qk[:, j, 0:n], scalar=g, in1=arr[:, 0:n],
                                           op0=ALU.mult, op1=ALU.mult).then_inc(*dve_done.mark("qkn", l, j))
                    dve.wait_ge(*full("rot", l, j))
                    V.tensor_tensor(rtmp[:, 0, :], pair("rot", l, j)[:, 0:LAT], cst[:, C_SIN:C_SIN + LAT], ALU.mult)\
                        .then_inc(*free("rot", l, j))
                    dve.wait_ge(*pool_done.at("cos", l, j))
                    dve.wait_ge(*read("rot", l, j))
                    V.tensor_tensor(qk[:, j, 0:LAT], rtmp[:, 0, :], rtmp[:, 1, :], ALU.add)\
                        .then_inc(*dve_done.mark("rope", l, j))
                attention(l, "A")
                attention(l, "B")
                for x in range(24):
                    half, n, m = merge_item(x)
                    dve.wait_ge(*full("br", l, half, n, m))
                    dve.wait_ge(*read("gate", l, half, n, m))
                    dst = mT[:, 4 * half + m, 0:nt] if n == 0 else gsig[:, x % 2, 0:nt]
                    V.tensor_tensor(dst, pair("br", l, half, n, m)[:, 0:nt], gsig[:, x % 2, 0:nt], ALU.mult)\
                        .then_inc(*free("br", l, half, n, m))
                for j in range(KC):
                    dve.wait_ge(*full("out", l, j))
                    sp_ = spans(nt)
                    for t0, t1, c in sp_:
                        V.scalar_tensor_tensor(out=xT[:, j, t0:t1], in0=pair("out", l, j)[:, t0:t1],
                                               scalar=modc[:, 16 + j, c:c + 1], in1=xT[:, j, t0:t1],
                                               op0=ALU.mult, op1=ALU.add).then_inc(*free("out", l, j, by=2 // len(sp_)))
                norm(l, "ffn", nt)
                for j in range(KC):
                    dve.wait_ge(*full("ff2", l, j))
                    sp_ = spans(nt)
                    for t0, t1, c in sp_:
                        V.scalar_tensor_tensor(out=xT[:, j, t0:t1], in0=pair("ff2", l, j)[:, t0:t1],
                                               scalar=modc[:, 40 + j, c:c + 1], in1=xT[:, j, t0:t1],
                                               op0=ALU.mult, op1=ALU.add).then_inc(*free("ff2", l, j, by=2 // len(sp_)))
            dve.wait_ge(*full("params", DEPTH))
            V.tensor_copy(pcol[:, 0:KC], pair("params", DEPTH)[:, 0:KC]).then_inc(*free("params", DEPTH))
            norm(DEPTH, "fin", LAT)

        @block.gpsimd
        def _(pool):
            G = nc.gpsimd
            crow = a["conv_c"]
            for c, n in enumerate(("c", "c_ctx")):
                v = a[n][0] if n == "c" else a[n]
                pool.dma_start(craw_c[:, c, :], v.rearrange("(p k) -> p k", k=KC)).then_inc(*cond_in.mark(by=16))

            def params(l):
                if l:
                    pool.wait_ge(*full("params", l - 1))
                rows = lambda v: v.rearrange("(k p) -> k p", p=P)
                one = lambda v: v.rearrange("(a n) -> a n", a=1)
                if l == DEPTH:
                    return [(prow[0:KC, :], rows(a["norm_final"]))]
                out_ = [(prow[R_BMOD:R_BMOD + 48, :], rows(a["b_mod"][l])),
                        (prow[R_MIX:R_MIX + KC, :], rows(a["norm_mix"][l])),
                        (prow[R_FFN:R_FFN + KC, :], rows(a["norm_ffn"][l]))]
                for q in range(CONV):
                    out_.append((prow[R_CONV + 12 * q:R_CONV + 12 * q + 12, :], rows(crow[l, q])))
                out_.append((prow[R_ONORM:R_ONORM + 1, :], one(a["o_norm_c"][l])))
                for row, name in ((R_QN, "q_norm_a"), (R_KN, "k_norm_a")):
                    for u in range(2):
                        out_.append((prow[row:row + 1, u * HD:u * HD + HD], one(a[name][l])))
                out_.append((prow[R_FIN:R_FIN + 1, :], rows(a["norm_final"])[0:1, :]))
                return out_

            def load_params(l):
                for dst, src in params(l):
                    pool.dma_start(dst, src).then_inc(*params_in.mark(l, by=16))

            load_params(0)
            for l in range(DEPTH):
                nt = TOK if l == 0 else LAT
                if l:
                    pool.wait_ge(*dve_done.at("g", l - 1))
                for u, name in enumerate(("a_log_c", "dt_bias_c")):
                    pool.dma_start(abc[:, u, :], a[name][l].rearrange("(a d) h -> a (d h)", a=1).to_broadcast([P, 8]))\
                        .then_inc(*abc_in.mark(l, by=16))
                load_params(l + 1)
                if l:
                    pool.wait_ge(*e_in.at(l - 1, B_H - 1))
                G.memset(bpad[:, :], 0.0).then_inc(*pool_done.mark("bpad0", l))
                pool.wait_ge(*pool_done.at("bpad0", l))
                pool.dma_start(bpad[:, 48:79], a["rpb_b"][l].rearrange("h r c -> (h r) c"))\
                    .then_inc(*rpb_in.mark(l, by=16))
                pool.wait_ge(*rpb_in.at(l))
                G.tensor_scalar(bpad[:, :], bpad[:, :], 1.0 / SCALE, None, ALU.mult).then_inc(*pool_done.mark("bpad", l))
                pool.wait_ge(*pool_done.at("bpad", l))
                pool.dma_start(scratch.rearrange("(r c) -> r c", c=127), bpad[:, :]).then_inc(*pad_out.mark(l, by=16))
                pool.wait_ge(*pad_out.at(l))
                skew = bass.AP(scratch.tensor, 63, [[127, B_H * 15], [-1, GRID_W], [1, GRID_W]])
                pool.dma_start(toeplitz, skew).then_inc(*skew_out.mark(l, by=16))
                for s in range(TT):
                    for d in range(2):
                        t = tiles[d][s]
                        if s == 0:
                            pool.wait_ge(*read("gc", l))
                            pool.wait_ge(*dve_done.at("nbeta", l))
                            pool.wait_ge(*dve_done.at("l2", l, 7))
                            pool.wait_ge(*read("ktok", l, 3))
                        if s:
                            pool.wait_ge(*full("so", l, 2 * s - 1, d))
                        G.tensor_tensor(rbuf[d], over_heads(masks[m_cum[d]]), along(gt[:, t, 4 * d:4 * d + 4]), ALU.mult)\
                            .then_inc(*pool_done.mark("R", l, s, d))
                        G.tensor_tensor(p2buf[d], over_heads(masks[m_strict[d]]), along(nbeta[:, t, 4 * d:4 * d + 4]),
                                        ALU.mult).then_inc(*pool_done.mark("MB", l, s, d))
                        G.tensor_tensor(vbbuf[d], vtok[:, t, :].rearrange("p (h n) -> p h n", h=C_H),
                                        along(bg[:, t, 4 * d:4 * d + 4]), ALU.mult).then_inc(*pool_done.mark("vb", l, s, d))
                    for d in range(2):
                        t = tiles[d][s]
                        pool.wait_ge(*read("bc", l, s, d))
                        G.tensor_tensor(qdbuf[d], qT[:, :, t * P:t * P + P], ebuf[d], ALU.mult)\
                            .then_inc(*pool_done.mark("qd", l, s, d))
                        pool.wait_ge(*read("G", l, s, d))
                        G.tensor_tensor(aqbuf[d], aqbuf[d], over_heads(masks[m_aq[d]]), ALU.mult)\
                            .then_inc(*pool_done.mark("AQ", l, s, d))
                        pool.wait_ge(*dve_done.at("gb", l))
                        G.tensor_tensor(wbuf[d], ktok[:, t, :].rearrange("p (h n) -> p h n", h=C_H),
                                        along(gex[:, t, 0, 4 * d:4 * d + 4]), ALU.mult)\
                            .then_inc(*pool_done.mark("kbe", l, s, d))
                    for d in range(2):
                        t = tiles[d][s]
                        pool.wait_ge(*full("pw", l, s, d, 4))
                        pool.wait_ge(*act_done.at("gex1", l))
                        G.tensor_tensor(pbuf[d], ktok[:, t, :].rearrange("p (h n) -> p h n", h=C_H),
                                        along(gex[:, t, 1, 4 * d:4 * d + 4]), ALU.mult)\
                            .then_inc(*pool_done.mark("kd", l, s, d))
                    for c in range(2):
                        for d in range(2):
                            t, cc, n = tiles[d][s], (c if d == 0 else 1 - c), 2 * s + c
                            pool.wait_ge(*(read("so", l, n - 1, d) if n else dve_done.at("S0", l)))
                            G.tensor_tensor(state[:, (n + 1) % 2, 4 * d:4 * d + 4, :], state[:, n % 2, 4 * d:4 * d + 4, :],
                                            along(gex[:, t, 2 + cc, 4 * d:4 * d + 4]), ALU.mult)\
                                .then_inc(*pool_done.mark("Sdec", l, n, d))
                to = TT if l == 0 else LT
                for d in range(2):
                    pool.wait_ge(*read("so", l, 2 * TT - 1, d))
                G.tensor_tensor(osq[:, 0:to, :], Otok[:, 0:to, :], Otok[:, 0:to, :], ALU.mult)\
                    .then_inc(*pool_done.mark("osq", l))
                for j in range(6):
                    pool.wait_ge(*dve_done.at("qkn", l, j))
                    if j:
                        pool.wait_ge(*dve_done.at("rope", l, j - 1))
                    G.tensor_tensor(rtmp[:, 1, :], qk[:, j, 0:LAT], cst[:, C_COS:C_COS + LAT], ALU.mult)\
                        .then_inc(*pool_done.mark("cos", l, j))
                pool.wait_ge(*skew_out.at(l))
                per = LT if l else TT
                for h in range(B_H):
                    if h >= 2:
                        pool.wait_ge(*full("T", "B", l, per * (h - 1) - 1))
                    for u in range(2):
                        src = toeplitz[15 * h + 1 - u:15 * h + 15 - u].rearrange("j c k -> c j k")
                        pool.dma_start(ebias[u * 64:u * 64 + 64, h % 2, :, :], src).then_inc(*e_in.mark(l, h, by=16))
                    pool.wait_ge(*e_in.at(l, h))
                    e = ebias[:, h % 2, :, :]
                    G.tensor_tensor(e, e, cst[:, C_MASK:C_MASK + GRID_W].unsqueeze(1).to_broadcast([P, 14, GRID_W]), ALU.add)\
                        .then_inc(*pool_done.mark("E", l, h))
                for x in range(24):
                    half, n, m = merge_item(x)
                    if n == 0:
                        continue
                    pool.wait_ge(*read("br", l, half, n, m))
                    pool.wait_ge(*(read("br", l, half, 0, m) if n == 1 else pool_done.at("merge", l, half, 1, m)))
                    acc = mT[:, 4 * half + m, 0:nt]
                    G.tensor_tensor(acc, acc, gsig[:, x % 2, 0:nt], ALU.add).then_inc(*pool_done.mark("merge", l, half, n, m))
                for j in range(32):
                    pool.wait_ge(*read("ff1", l, j))
                    G.tensor_tensor(fT[:, j, 0:nt], fT[:, j, 0:nt], fT[:, j, 0:nt], ALU.mult)\
                        .then_inc(*pool_done.mark("ff1", l, j))


_INS = ["x", "c", "ctx", "c_ctx", "w_mod", "b_mod", "norm_mix", "w_in", "q_norm_a", "k_norm_a", "rpb_b", "conv_c",
        "a_log_c", "dt_bias_c", "o_norm_c", "w_branch", "w_out", "norm_ffn", "w_ffn1", "w_ffn2", "norm_final"]


def build(nc, arrays, book):
    a = {k: nc.dram_tensor(f"in_{k}", v.shape, F32, kind="ExternalInput").ap() for k, v in arrays.items()}
    out = nc.dram_tensor("out_0", (1, LAT, D), F32, kind="ExternalOutput").ap()
    scratch = nc.dram_tensor("bias_pad", (B_H * 15 * 127,), F32, kind="Internal").ap()
    toeplitz = nc.dram_tensor("bias_skewed", (B_H * 15, GRID_W, GRID_W), F32, kind="Internal").ap()
    program(nc, a, out, scratch, toeplitz, book)


def kernel(**inputs):
    import concourse.bacc as _bacc
    from concourse.bass_utils import run_bass_kernel_spmd as _run

    arrays = {k: np.ascontiguousarray(inputs[k]) for k in _INS}
    arrays["consts"] = constants()
    book = {"final": False}
    build(_bacc.Bacc("TRN2", target_bir_lowering=False, num_devices=1), arrays, book)
    book["final"] = True
    nc = _bacc.Bacc("TRN2", target_bir_lowering=False, num_devices=1)
    build(nc, arrays, book)
    r = _run(nc, [{f"in_{k}": v for k, v in arrays.items()}], core_ids=[0])
    return r.results[0]["out_0"]
```

```python
from contextlib import ExitStack

import numpy as np
import concourse.bass as bass
from concourse import mybir

F32 = mybir.dt.float32
F32R = mybir.dt.float32r
ALU = mybir.AluOpType
ACT = mybir.ActivationFunctionType
AX = mybir.AxisListType

P = 128
D = 1024
KC = D // P
LAT, CTX = 512, 256
TOK = LAT + CTX
TT, LT = TOK // P, LAT // P
DEPTH = 2
GRID_W, ROWS = 64, LAT // 64
HD = 64
A_H, A_KV, B_H, C_H = 8, 2, 8, 4
WIN_R, WIN_C = 8, 16
CONV = 5
FF = 4 * D
EPS = 1e-6
NEG = -1e30
SCALE = HD ** -0.5
O_QA, O_KA, O_VA, O_QB, O_KB, O_VB, O_QKV, O_Z, O_BETA, O_A, O_GATE = (
    int(v) for v in np.cumsum([0, 512, 128, 128, 512, 512, 512, 1536, 512, 8, 8]))
SLOT = KC * P
NRAW, NSPL = 3, 3
GF = 4
C_ID, C_ONE, C_BLK, C_ROT, C_UI, C_LI, C_US, C_LS, C_COS, C_SIN, C_MASK = (
    int(v) for v in np.cumsum([0, P, P, P, P, P, P, P, P, LAT, LAT]))
C_N = C_MASK + GRID_W
R_BMOD, R_MIX, R_FFN, R_CONV, R_ONORM, R_QN, R_KN, R_FIN = 0, 48, 56, 64, 124, 125, 126, 127


def constants():
    c = np.zeros((P, C_N), np.float32)
    i = np.arange(P)
    same = (i[:, None] // 64) == (i[None, :] // 64)
    c[:, C_ID:C_ID + P] = np.eye(P)
    c[:, C_ONE:C_ONE + P] = 1
    c[:, C_BLK:C_BLK + P] = same
    for m in range(0, P, 2):
        c[m + 1, C_ROT + m] = -1
        c[m, C_ROT + m + 1] = 1
    c[:, C_UI:C_UI + P] = same & (i[:, None] <= i[None, :])
    c[:, C_LI:C_LI + P] = same & (i[:, None] >= i[None, :])
    c[:, C_US:C_US + P] = same & (i[:, None] < i[None, :])
    c[:, C_LS:C_LS + P] = same & (i[:, None] > i[None, :])
    t = np.arange(LAT)
    freq = (10000.0 ** (-np.arange(0, HD // 2, 2, dtype=np.float32) / np.float32(HD // 2))).astype(np.float32)
    pair = (i % HD) // 2
    pos = np.where((pair < 16)[:, None], (t // GRID_W)[None, :], (t % GRID_W)[None, :]).astype(np.float32)
    ang = pos * freq[pair % 16][:, None]
    c[:, C_COS:C_COS + LAT] = np.cos(ang)
    c[:, C_SIN:C_SIN + LAT] = np.sin(ang)
    col = i % GRID_W
    c0 = np.clip(col - WIN_C // 2, 0, GRID_W - WIN_C)
    kc = np.arange(GRID_W)
    inside = (kc[None, :] >= c0[:, None]) & (kc[None, :] < c0[:, None] + WIN_C)
    c[:, C_MASK:C_MASK + GRID_W] = np.where(inside, 0.0, NEG)
    return c


class Signal:

    def __init__(self, nc, ctx, name, book):
        self.sem = ctx.enter_context(nc.semaphore(name))
        self.n, self.book, self.name = 0, book, name

    def mark(self, *key, by=1):
        self.n += by
        self.book[(self.name,) + key] = self.n
        return self.sem, by

    def at(self, *key):
        if self.book["final"]:
            return self.sem, self.book[(self.name,) + key]
        return self.sem, 1


def program(nc, a, out, scratch, toeplitz, x_store, book):
    book["final"] = book.get("final", False)
    with ExitStack() as ctx:
        def sb(name, shape):
            return ctx.enter_context(nc.sbuf_tensor(name, shape, F32))

        def sig(name):
            return Signal(nc, ctx, name, book)

        hh, hl = (ctx.enter_context(nc.sbuf_tensor(n, [P, KC, TOK], F32R)) for n in ("hh", "hl"))
        wring = sb("wring", [P, NRAW, SLOT])
        wh, wl = (ctx.enter_context(nc.sbuf_tensor(n, [P, NSPL, SLOT], F32R)) for n in ("wh", "wl"))
        cst = sb("cst", [P, C_N])
        pcols = sb("pcols", [P, 2, P])
        ccol = sb("ccol", [P, 2, KC])
        modcs = sb("modcs", [P, 2, 48, 2])
        gains = sb("gains", [P, 2, 2, KC, 2])
        small = sb("small", [P, 64])
        eps = sb("eps", [P, 1])
        XT0, RN = 21504, 27648
        r_at = nc.sbuf_base if not callable(nc.sbuf_base) else nc.sbuf_base()
        r_at = (r_at + 31) // 32 * 32
        R = sb("R", [P, RN])
        fh, fl = (nc.alloc_sbuf_tensor_at(n, [P, 2, GF, TOK], F32R, offset=r_at + 4 * o)
                  for n, o in (("fh", 0), ("fl", 2 * GF * TOK)))
        PS = [ctx.enter_context(nc.psum_tensor(f"ps{i}", [P, 1024], F32)) for i in range(4)]

        def r(at, *shape):
            n = int(np.prod(shape))
            v = R[:, at:at + n]
            if len(shape) == 2:
                v = v.rearrange("p (a b) -> p a b", a=shape[0])
            if len(shape) == 3:
                v = v.rearrange("p (a b c) -> p a b c", a=shape[0], b=shape[1])
            return v

        ident, ones, blk, rot = (cst[:, c:c + P] for c in (C_ID, C_ONE, C_BLK, C_ROT))
        oC, oA, oB = r(0, 4, TOK), r(3072, 4, TOK), r(6144, 4, TOK)
        S0 = 9216
        N0 = 4 * GF * TOK
        sq_n, rs_n, ht = r(N0, 2, TOK), r(N0 + 2 * TOK, TOK), r(N0 + 3 * TOK, 2, TOK)
        ftmp = r(N0, 2, TOK)
        xT = r(XT0, KC, TOK)
        fin_T = r(0, KC, TOK)
        qT, kT = r(0, 4, TOK), r(3072, 4, TOK)
        ktok, vtok, Otok = r(6144, TT, 512), r(9216, TT, 512), r(12288, TT, 512)
        U0 = 15360
        rbuf, ebuf, wbuf, pbuf, p2buf, tbuf, xbuf, aqbuf, qdbuf, vbbuf = (
            [r(U0 + (2 * b + d) * 512, 4, P) for d in range(2)] for b in range(10))
        state = r(U0 + 10240, 2, 8, P)
        craw = r(U0, 2, TOK + 8)
        cacc = r(U0 + 2048, 2, TOK + 8)
        csq, crr = r(U0 + 6144, 2, TOK), r(U0 + 8192, 2, TOK)
        vT4 = r(12288, 4, TOK)
        siluz = r(9216, 4, TOK)
        osq = r(6144, TT, 512)
        bg = sb("bg", [P, TT, 16])
        gt = sb("gt", [P, TT, 8])
        gtmp = sb("gtmp", [P, TT, 8])
        gcs = sb("gcs", [P, TT, 32])
        gex = sb("gex", [P, TT, 4, 8])
        nbeta = sb("nbeta", [P, TT, 8])
        abc = sb("abc", [P, 2, 8])
        qk = r(S0, 6, TOK)
        va = r(S0 + 4608, TT, 128)
        asq, arr = r(S0 + 5376, TOK), r(S0 + 6144, TOK)
        rtmp = r(S0 + 6912, 2, LAT)
        prob = r(S0 + 9216 + 1792, 2, TOK)
        probT = r(S0 + 9216 + 1792 + 1536, 2, TT, P)
        qB, kB, vB = r(S0, 4, TOK), r(S0 + 3072, 4, TOK), r(S0 + 6144, TT, 512)
        ebias = r(S0 + 9216, 2, 14, GRID_W)
        stat = sb("stat", [P, 2, 4])
        mT = r(S0, KC, TOK)
        gsig = r(S0 + 6144, 2, TOK)
        vraw = prob
        prow = sb("prow", [P, P])
        craw_c = sb("craw_c", [P, 2, KC])
        bpad = ctx.enter_context(nc.sbuf_tensor("bpad", [B_H * 15, 127], F32))
        tiles = ([4, 5, 0, 1, 2, 3], [5, 4, 3, 2, 1, 0])
        masks = {k: cst[:, c:c + P] for k, c in (("UI", C_UI), ("LI", C_LI), ("US", C_US), ("LS", C_LS))}
        NG = FF // P // GF
        m_cum, m_strict, m_aq = ("UI", "LI"), ("LS", "US"), ("UI", "LI")

        def want_out(l, t):
            return l == 0 or t < LT

        def flat(v):
            return v.rearrange("p a b -> p (a b)")

        def over_heads(v):
            return v.unsqueeze(1).to_broadcast([P, C_H, P])

        def along(v, n=P):
            return v.unsqueeze(2).to_broadcast([v.shape[0], v.shape[1], n])

        def power(d, i):
            one, two = (pbuf[d], tbuf[d]), (p2buf[d], rbuf[d])
            return (*one, *two) if i % 2 == 0 else (*two, *one)

        ps_full = [ctx.enter_context(nc.semaphore(f"ps_full{i}")) for i in range(4)]
        ps_free = [ctx.enter_context(nc.semaphore(f"ps_free{i}")) for i in range(4)]
        w_full = [ctx.enter_context(nc.semaphore(f"w_full{i}")) for i in range(NRAW)]
        params_in, cond_in, consts_in = sig("params_in"), sig("cond_in"), sig("consts_in")
        spilled, x_back = sig("spilled"), sig("x_back")
        x_in = [sig(f"x_in{t}") for t in range(TT)]
        act_done, dve_done, pool_done, pe_done = sig("act_done"), sig("dve_done"), sig("pool_done"), sig("pe_done")
        abc_in, rpb_in, pad_out, skew_out, out_done, e_in = (sig(n) for n in ("abc_in", "rpb_in", "pad_out", "skew_out", "out_done", "e_in"))
        block = ctx.enter_context(nc.Block())
        turn = {"n": 0, "w": 0}

        def take(pe, *key):
            n = turn["n"]
            turn["n"] += 1
            book[("ps",) + key] = n
            if n >= 4:
                pe.wait_ge(ps_free[n % 4], 2 * (n // 4))
            return PS[n % 4]

        def full(*key):
            n = book.get(("ps",) + key, 0) if book["final"] else 0
            return ps_full[n % 4], n // 4 + 1

        def filled(*key):
            return ps_full[book[("ps",) + key] % 4], 1

        def pair(*key):
            return PS[book.get(("ps",) + key, 0) % 4]

        def free(*key, by=2):
            return ps_free[book.get(("ps",) + key, 0) % 4], by

        def read(*key):
            n = book.get(("ps",) + key, 0) if book["final"] else 0
            return ps_free[n % 4], 2 * (n // 4 + 1)

        def read_first(*key):
            sem, n = read(*key)
            return sem, n - 1

        def att_items(l):
            return [(h, t) for h in range(A_H) for t in range(TT if l == 0 else LT)]

        w_in = a["w_in"]

        def cols(w, l, c0, n=P, r0=0, rn=KC):
            return w[l, r0 * P:(r0 + rn) * P, c0:c0 + n].rearrange("(k p) n -> p k n", p=P)

        def mod_slot(l, i):
            return l, "mod", i, KC, [(0, P, a["w_mod"][l, :, P * i:P * i + P].rearrange("(p k) n -> p k n", k=KC))], False

        def plan():
            for i in range(16):
                yield mod_slot(0, i)
            for l in range(DEPTH):
                yield l, "ba", 0, KC, [(0, 16, cols(w_in, l, O_BETA, 16))], True
                for i in range(12):
                    yield l, "c", i, KC, [(0, P, cols(w_in, l, O_QKV + P * i))], True
                if l == 0:
                    for i in range(16, 48):
                        yield mod_slot(0, i)
                    for i in range(48):
                        yield mod_slot(1, i)
                for name, o, n in (("z", O_Z, 4), ("qa", O_QA, 4)):
                    for i in range(n):
                        yield l, name, i, KC, [(0, P, cols(w_in, l, o + P * i))], True
                for g in range(A_KV):
                    yield l, "ka", g, KC, [(u * HD, HD, cols(w_in, l, O_KA + g * HD, HD)) for u in range(2)], True
                yield l, "va", 0, KC, [(0, P, cols(w_in, l, O_VA))], True
                for name, o in (("qb", O_QB), ("kb", O_KB), ("vb", O_VB)):
                    for i in range(4):
                        yield l, name, i, KC, [(0, P, cols(w_in, l, o + P * i))], True
                for i in range(24):
                    dc, n = divmod(i, 3)
                    yield l, "gate", i, KC, [(0, P, cols(w_in, l, O_GATE + n * D + P * dc))], True
                    yield l, "br", i, 4, [(0, P, a["w_branch"][l, n, :, P * dc:P * dc + P]
                                           .rearrange("(k p) n -> p k n", p=P))], False
                for i in range(8):
                    yield l, "out", i, KC, [(0, P, cols(a["w_out"], l, P * i))], True
                for g in range(FF // P // GF + 1):
                    if g < FF // P // GF:
                        for i in range(GF):
                            yield l, "ff1", GF * g + i, KC, [(0, P, cols(a["w_ffn1"], l, P * (GF * g + i)))], True
                    if g:
                        for i in range(4):
                            yield l, "ff2", 4 * (g - 1) + i, GF, \
                                [(0, 2 * P, cols(a["w_ffn2"], l, 2 * P * i, 2 * P, GF * (g - 1), GF))], True

        slots = list(plan())
        where, counts = {}, [0] * NRAW
        order = []
        for n, (l, name, i, kn, pieces, split_) in enumerate(slots):
            counts[n % NRAW] += 16 * len(pieces)
            where[l, name, i] = (n, counts[n % NRAW], len(order))
            if split_:
                order.append((l, name, i))

        def slot_view(t, s, l, name, i):
            kn, pieces = slots[where[l, name, i][0]][3:5]
            n = sum(p[1] for p in pieces)
            return t[:, s, 0:kn * n].rearrange("p (k n) -> p k n", k=kn)

        def raw_weights(eng, l, name, i):
            n, count, _ = where[l, name, i]
            eng.wait_ge(w_full[n % NRAW], count)
            return slot_view(wring, n % NRAW, l, name, i)

        def weights(pe, l, name, i=0):
            pe.wait_ge(*pool_done.at("wlo", l, name, i))
            s = where[l, name, i][2] % NSPL
            return slot_view(wh, s, l, name, i), slot_view(wl, s, l, name, i)

        def slot_read(l, name, i, *key):
            book["last", l, name, i] = key


        @block.tensor
        def _(pe):
            turn["n"] = 0
            mm, tr = nc.tensor.matmul, nc.tensor.transpose

            def project(key, w, ntok, rhs=None, kn=KC, m0=0, ready=None, ps=None, done=True):
                (ah, al), (rh, rl) = w, rhs or (hh, hl)
                ps = take(pe, *key)
                for t0, t1 in ((0, LAT), (LAT, TOK))[:1 if ntok == LAT else 2]:
                    for k in range(kn):
                        if ready and t0 == 0:
                            pe.wait_ge(*ready(k))
                        ahk, alk = ah[:, k, m0:m0 + P], al[:, k, m0:m0 + P]
                        mm(ps[:, t0:t1], ahk, rh[:, k, t0:t1], start=(k == 0), stop=False)
                        mm(ps[:, t0:t1], ahk, rl[:, k, t0:t1], start=False, stop=False)
                        last = mm(ps[:, t0:t1], alk, rh[:, k, t0:t1], start=False, stop=(k == kn - 1))
                last.then_inc(*filled(*key))

            def modulation(l, i):
                w = raw_weights(pe, l, "mod", i)
                ps = take(pe, "mod", l, i)
                for k in range(KC):
                    last = mm(ps[:, 0:2], w[:, k, :], ccol[:, :, k], start=(k == 0), stop=(k == KC - 1))
                last.then_inc(*filled("mod", l, i))
                slot_read(l, "mod", i, "mod", l, i)

            def turn_values(key, src, i, into):
                pe.wait_ge(*i)
                ps = take(pe, *key)
                for t in range(TT):
                    last = tr(ps[:, t * P:t * P + P], src[:, t * P:t * P + P], ident)
                last.then_inc(*filled(*key))

            def attention(l, br):
                q, k, v = (qk, qk, va) if br == "A" else (qB, kB, vB)
                work = att_items(l)
                for i in range(len(work) + 2):
                    if i < len(work):
                        h, t = work[i]
                        if i == 0:
                            pe.wait_ge(*(dve_done.at("rope", l, 5) if br == "A" else read("kb", l, 3)))
                            pe.wait_ge(*(read("va", l) if br == "A" else read("vb", l, 3)))
                        lo = HD * (h % 2)
                        kc = 4 + h // 4 if br == "A" else h // 2
                        qs = q[lo:lo + HD, h // 2, t * P:t * P + P]
                        ps = take(pe, "S", br, l, i)
                        if t < LT:
                            mm(ps[:, 0:LAT], qs, k[lo:lo + HD, kc, 0:LAT], start=True, stop=True)
                            last = mm(ps[:, LAT:TOK], qs, k[lo:lo + HD, kc, LAT:TOK], start=True, stop=True)
                        else:
                            last = mm(ps[:, 0:CTX], qs, k[lo:lo + HD, kc, LAT:TOK], start=True, stop=True)
                        last.then_inc(*filled("S", br, l, i))
                    if 1 <= i <= len(work):
                        j = i - 1
                        nk = TT if work[j][1] < LT else TT - LT
                        pe.wait_ge(*dve_done.at("prob", br, l, j))
                        ps = take(pe, "T", br, l, j)
                        for b in range(nk):
                            last = tr(ps[:, b * P:b * P + P], prob[:, j % 2, b * P:b * P + P], ident)
                        last.then_inc(*filled("T", br, l, j))
                    if i >= 2:
                        j = i - 2
                        h, t = work[j]
                        b0 = 0 if t < LT else LT
                        c0 = HD * (h // 4 if br == "A" else h)
                        pe.wait_ge(*read("T", br, l, j))
                        ps = take(pe, "O", br, l, j)
                        for b in range(b0, TT):
                            last = mm(ps[0:HD, 0:P], v[:, b, c0:c0 + HD], probT[:, j % 2, b - b0, :],
                                      start=(b == b0), stop=(b == TT - 1))
                        last.then_inc(*filled("O", br, l, j))

            def norm(l, which, ntok):
                ps = take(pe, "ss", l, which)
                for k in range(KC):
                    pe.wait_ge(*act_done.at("sq", l, which, k))
                    for t0, t1 in ((0, LAT), (LAT, TOK))[:1 if ntok == LAT else 2]:
                        last = mm(ps[:, t0:t1], ones, sq_n[:, k % 2, t0:t1], start=(k == 0), stop=(k == KC - 1))
                    if k < KC - 1:
                        last.then_inc(*pe_done.mark("ss", l, which, k))
                last.then_inc(*filled("ss", l, which))

            pe.wait_ge(*consts_in.at())
            for l in range(DEPTH):
                if l == 0:
                    for t in range(TT):
                        pe.wait_ge(*x_in[t].at())
                        ps = take(pe, "x", t)
                        for k in range(KC):
                            last = tr(ps[:, k * P:k * P + P], r(S0 + 1024 * t, 1024)[:, k * P:k * P + P], ident)
                        last.then_inc(*filled("x", t))
                if l == 0:
                    for ll in range(DEPTH):
                        pe.wait_ge(*params_in.at(ll))
                        ps = take(pe, "params", ll)
                        tr(ps[:, 0:P], prow[:, :], ident).then_inc(*filled("params", ll))
                    pe.wait_ge(*act_done.at("ccol"))
                    for i in range(16):
                        modulation(0, i)
                norm(l, "mix", TOK)
                bw = weights(pe, l, "ba")
                for k in range(KC):
                    pe.wait_ge(*dve_done.at("h", l, "mix", k))
                ps = take(pe, "ba", l)
                for t in range(TT):
                    for k in range(KC):
                        xh, xl = hh[:, k, t * P:t * P + P], hl[:, k, t * P:t * P + P]
                        o = ps[:, 16 * t:16 * t + 16]
                        mm(o, xh, bw[0][:, k, :], start=(k == 0), stop=False)
                        mm(o, xh, bw[1][:, k, :], start=False, stop=False)
                        last = mm(o, xl, bw[0][:, k, :], start=False, stop=(k == KC - 1))
                last.then_inc(*filled("ba", l))
                slot_read(l, "ba", 0, "ba", l)
                for j in range(12):
                    project(("c", l, j // 4, j % 4), weights(pe, l, "c", j), TOK)
                    slot_read(l, "c", j, "c", l, j // 4, j % 4)
                for m in range(4):
                    pe.wait_ge(*act_done.at("silu", l, 2, m))
                    ps = take(pe, "vtok", l, m)
                    for t in range(TT):
                        last = tr(ps[:, t * P:t * P + P], vT4[:, m, t * P:t * P + P], ident)
                    last.then_inc(*filled("vtok", l, m))
                for j in range(8):
                    pe.wait_ge(*act_done.at("csq", l, j))
                    ps = take(pe, "css", l, j)
                    for t0, t1 in ((0, LAT), (LAT, TOK)):
                        last = mm(ps[:, t0:t1], ones, csq[:, j % 2, t0:t1], start=True, stop=True)
                    last.then_inc(*filled("css", l, j))
                for h in range(4):
                    pe.wait_ge(*dve_done.at("l2", l, 4 + h))
                    ps = take(pe, "ktok", l, h)
                    for t in range(TT):
                        last = tr(ps[:, t * P:t * P + P], kT[:, h, t * P:t * P + P], ident)
                    last.then_inc(*filled("ktok", l, h))
                pe.wait_ge(*dve_done.at("g", l))
                ps = take(pe, "gc", l)
                for t in range(TT):
                    b = 32 * t
                    mm(ps[:, b:b + 4], cst[:, C_UI:C_UI + P], gt[:, t, 0:4], start=True, stop=True)
                    mm(ps[:, b + 4:b + 8], cst[:, C_LI:C_LI + P], gt[:, t, 4:8], start=True, stop=True)
                    mm(ps[:, b + 8:b + 16], blk, gt[:, t, :], start=True, stop=True)
                    for c in range(2):
                        last = mm(ps[:, b + 16 + 8 * c:b + 24 + 8 * c], blk[:, 64 * c:64 * c + 1].to_broadcast([P, P]),
                                  gt[:, t, :], start=True, stop=True)
                last.then_inc(*filled("gc", l))
                pe.wait_ge(*read("ktok", l, 3))
                for s in range(TT):
                    for d in range(2):
                        t = tiles[d][s]
                        pe.wait_ge(*pool_done.at("R", l, s, d))
                        ps = take(pe, "bc", l, s, d)
                        mm(ps[:, 0:512], ones, flat(rbuf[d]), start=True, stop=True).then_inc(*filled("bc", l, s, d))
                        ps = take(pe, "G", l, s, d)
                        for h in range(C_H):
                            kk = kT[:, h, t * P:t * P + P]
                            mm(ps[:, h * P:h * P + P], kk, kk, start=True, stop=True)
                            last = mm(ps[:, 512 + h * P:512 + h * P + P], kk, qT[:, h, t * P:t * P + P],
                                      start=True, stop=True)
                        last.then_inc(*filled("G", l, s, d))
                    for d in range(2):
                        pe.wait_ge(*dve_done.at("A", l, s, d))
                        ps = take(pe, "AT", l, s, d)
                        for h in range(C_H):
                            last = tr(ps[:, h * P:h * P + P], pbuf[d][:, h, :], ident)
                        last.then_inc(*filled("AT", l, s, d))
                    if l == 0 and s == 0:
                        filler = iter([(0, i) for i in range(16, 48)] + [(1, i) for i in range(48)])
                    for i in range(5):
                        for d in range(2):
                            src, srcT, dst, dstT = power(d, i)
                            pe.wait_ge(*(read("pw", l, s, d, i - 1) if i else read("AT", l, s, d)))
                            ps = take(pe, "pw", l, s, d, i)
                            for h in range(C_H):
                                last = mm(ps[:, h * P:h * P + P], srcT[:, h, :], src[:, h, :], start=True, stop=True)
                                if i < 4:
                                    last = mm(ps[:, 512 + h * P:512 + h * P + P], src[:, h, :], srcT[:, h, :],
                                              start=True, stop=True)
                            last.then_inc(*filled("pw", l, s, d, i))
                        for d in range(2):
                            src, srcT, dst, dstT = power(d, i)
                            pe.wait_ge(*read("pw", l, s, d, i))
                            pe.wait_ge(*(read("X", l, s, d, i - 1) if i else read("AT", l, s, d)))
                            ps = take(pe, "X", l, s, d, i)
                            for h in range(C_H):
                                last = mm(ps[:, h * P:h * P + P], dst[:, h, :], xbuf[d][:, h, :], start=True, stop=True)
                            last.then_inc(*filled("X", l, s, d, i))
                        if l == 0:
                            for _, m in zip(range(3), filler):
                                modulation(*m)
                    for d in range(2):
                        pe.wait_ge(*pool_done.at("kbe", l, s, d))
                        pe.wait_ge(*read("X", l, s, d, 4))
                        ps = take(pe, "kcd", l, s, d)
                        for h in range(C_H):
                            last = mm(ps[:, h * P:h * P + P], wbuf[d][:, h, :], xbuf[d][:, h, :], start=True, stop=True)
                        last.then_inc(*filled("kcd", l, s, d))
                    for c in range(2):
                        for d in range(2):
                            t, cc, n = tiles[d][s], (c if d == 0 else 1 - c), 2 * s + c
                            lo, hi = 64 * cc, 64 * cc + 64
                            S = state[:, n % 2, :, :]
                            if c == 0:
                                pe.wait_ge(*read("kcd", l, s, d))
                                pe.wait_ge(*pool_done.at("vb", l, s, d))
                            pe.wait_ge(*(read("so", l, n - 1, d) if n else dve_done.at("S0", l)))
                            ps = take(pe, "vn", l, n, d)
                            for h in range(C_H):
                                o = ps[0:64, h * P:h * P + P]
                                mm(o, ebuf[d][:, h, lo:hi], S[:, 4 * d + h, :], start=True, stop=False)
                                last = mm(o, xbuf[d][lo:hi, h, lo:hi], vbbuf[d][lo:hi, h, :], start=False, stop=True)
                            last.then_inc(*filled("vn", l, n, d))
                        for d in range(2):
                            t, cc, n = tiles[d][s], (c if d == 0 else 1 - c), 2 * s + c
                            lo, hi = 64 * cc, 64 * cc + 64
                            S = state[:, n % 2, :, :]
                            pe.wait_ge(*read("vn", l, n, d))
                            pe.wait_ge(*pool_done.at("kd", l, s, d))
                            pe.wait_ge(*pool_done.at("AQ", l, s, d))
                            ps = take(pe, "so", l, n, d)
                            for h in range(C_H):
                                vn = tbuf[d][lo:hi, h, :]
                                last = mm(ps[:, h * P:h * P + P], pbuf[d][lo:hi, h, :], vn, start=True, stop=True)
                            if want_out(l, t):
                                for h in range(C_H):
                                    o = ps[0:64, 512 + h * P:512 + h * P + P]
                                    mm(o, qdbuf[d][:, h, lo:hi], S[:, 4 * d + h, :], start=True, stop=False)
                                    last = mm(o, aqbuf[d][lo:hi, h, lo:hi], tbuf[d][lo:hi, h, :], start=False, stop=True)
                            last.then_inc(*filled("so", l, n, d))
                for m in range(4):
                    project(("z", l, m), weights(pe, l, "z", m), TOK if l == 0 else LAT)
                    slot_read(l, "z", m, "z", l, m)
                for t in range(TT if l == 0 else LT):
                    pe.wait_ge(*dve_done.at("onrm", l))
                    ps = take(pe, "oT", l, t)
                    for h in range(C_H):
                        last = tr(ps[:, h * P:h * P + P], Otok[:, t, h * P:h * P + P], ident)
                    last.then_inc(*filled("oT", l, t))
                pe.wait_ge(*read("oT", l, (TT if l == 0 else LT) - 1))
                for m in range(4):
                    project(("qk", l, m), weights(pe, l, "qa", m), TOK if l == 0 else LAT)
                    slot_read(l, "qa", m, "qk", l, m)
                for m in range(2):
                    project(("qk", l, 4 + m), weights(pe, l, "ka", m), TOK)
                    slot_read(l, "ka", m, "qk", l, 4 + m)
                project(("vaT", l), weights(pe, l, "va"), TOK)
                slot_read(l, "va", 0, "vaT", l)
                turn_values(("va", l), vraw[:, 0, :], read("vaT", l), va)
                for j in range(6):
                    n = TOK if (l == 0 or j >= 4) else LAT
                    pe.wait_ge(*act_done.at("asq", l, j))
                    ps = take(pe, "ass", l, j)
                    for t0, t1 in ((0, LAT), (LAT, TOK))[:1 if n == LAT else 2]:
                        last = mm(ps[:, t0:t1], blk, asq[:, t0:t1], start=True, stop=True)
                    last.then_inc(*filled("ass", l, j))
                    pe.wait_ge(*dve_done.at("qkn", l, j))
                    ps = take(pe, "rot", l, j)
                    mm(ps[:, 0:LAT], rot, qk[:, j, 0:LAT], start=True, stop=True).then_inc(*filled("rot", l, j))
                attention(l, "A")
                for m in range(4):
                    project(("qb", l, m), weights(pe, l, "qb", m), TOK if l == 0 else LAT)
                    slot_read(l, "qb", m, "qb", l, m)
                for m in range(4):
                    project(("kb", l, m), weights(pe, l, "kb", m), TOK)
                    slot_read(l, "kb", m, "kb", l, m)
                for m in range(4):
                    project(("vbT", l, m), weights(pe, l, "vb", m), TOK)
                    slot_read(l, "vb", m, "vbT", l, m)
                    if m:
                        turn_values(("vb", l, m - 1), vraw[:, (m - 1) % 2, :], read("vbT", l, m - 1), vB)
                turn_values(("vb", l, 3), vraw[:, 1, :], read("vbT", l, 3), vB)
                attention(l, "B")
                nt = TOK if l == 0 else LAT
                for x in range(24):
                    project(("gate", l, x), weights(pe, l, "gate", x), nt)
                    slot_read(l, "gate", x, "gate", l, x)
                    w = raw_weights(pe, l, "br", x)
                    ps = take(pe, "br", l, x)
                    for t0, t1 in ((0, LAT), (LAT, TOK))[:1 if nt == LAT else 2]:
                        for k in range(4):
                            last = mm(ps[:, t0:t1], w[:, k, :], (oA, oB, oC)[x % 3][:, k, t0:t1],
                                      start=(k == 0), stop=(k == 3))
                    last.then_inc(*filled("br", l, x))
                    slot_read(l, "br", x, "br", l, x)
                for i in range(8):
                    project(("out", l, i), weights(pe, l, "out", i), nt,
                            ready=(lambda k: dve_done.at("mlo", l, k)) if i == 0 else None)
                    slot_read(l, "out", i, "out", l, i)
                norm(l, "ffn", nt)
                for g in range(NG + 1):
                    if g < NG:
                        for i in range(GF * g, GF * g + GF):
                            project(("ff1", l, i), weights(pe, l, "ff1", i), nt,
                                    ready=(lambda k: dve_done.at("h", l, "ffn", k)) if i == 0 else None)
                            slot_read(l, "ff1", i, "ff1", l, i)
                    if g:
                        b = (g - 1) % 2
                        pe.wait_ge(*dve_done.at("flo", l, GF * g - 1))
                        for i in range(4):
                            w = weights(pe, l, "ff2", 4 * (g - 1) + i)
                            for u in range(2):
                                project(("ff2", l, g - 1, 2 * i + u), w, nt, rhs=(fh[:, b, :, :], fl[:, b, :, :]),
                                        kn=GF, m0=u * P)
                            slot_read(l, "ff2", 4 * (g - 1) + i, "ff2", l, g - 1, 2 * i + 1)
            pe.wait_ge(*params_in.at(DEPTH))
            ps = take(pe, "params", DEPTH)
            tr(ps[:, 0:KC], prow[0:KC, :], ident[0:KC, 0:KC]).then_inc(*filled("params", DEPTH))
            norm(DEPTH, "fin", LAT)
            pe.wait_ge(*act_done.at("fin", KC - 1))
            for t in range(LT):
                ps = take(pe, "fin", t)
                for k in range(KC):
                    last = tr(ps[:, k * P:k * P + P], fin_T[:, k, t * P:t * P + P], ident)
                last.then_inc(*filled("fin", t))

        def spans(n):
            return ((0, LAT, 0), (LAT, TOK, 1))[:1 if n == LAT else 2]

        def attention(eng, l, br):
            work = att_items(l)
            for i in range(len(work) + 1):
                if i < len(work):
                    n = TOK if work[i][1] < LT else CTX
                    eng.wait_ge(*dve_done.at("nm", br, l, i))
                    if i >= 2:
                        eng.wait_ge(*full("T", br, l, i - 2))
                    nc.scalar.activation(prob[:, i % 2, 0:n], pair("S", br, l, i)[:, 0:n], ACT.Exp, scale=SCALE,
                                         bias=stat[:, i % 2, 1:2], accum_out=stat[:, i % 2, 2:3])\
                        .then_inc(*free("S", br, l, i))
                if i:
                    j = i - 1
                    nb = TT if work[j][1] < LT else TT - LT
                    eng.wait_ge(*full("T", br, l, j))
                    if j >= 2:
                        eng.wait_ge(*full("O", br, l, j - 2))
                    nc.scalar.activation(probT[:, j % 2, 0:nb, :],
                                         pair("T", br, l, j)[:, 0:nb * P].rearrange("p (b n) -> p b n", b=nb), ACT.Copy)\
                        .then_inc(*free("T", br, l, j))

        @block.sync
        def _(sp):
            sp.dma_start(cst[:, :], a["consts"]).then_inc(*consts_in.mark(by=16))
            for t in range(TT):
                src = a["x"][0, t * P:t * P + P, :] if t < LT else a["ctx"][0, (t - LT) * P:(t - LT) * P + P, :]
                sp.dma_start(r(S0 + 1024 * t, 1024), src).then_inc(*x_in[t].mark(by=16))
            for n, (l, name, i, kn, pieces, _) in enumerate(slots):
                if n >= NRAW:
                    before = slots[n - NRAW][:3]
                    if slots[n - NRAW][5]:
                        sp.wait_ge(*pool_done.at("wlo", *before))
                    else:
                        sp.wait_ge(*full(*book.get(("last",) + before, ("x", 0))))
                for c0, cn, src in pieces:
                    sp.dma_start(slot_view(wring, n % NRAW, l, name, i)[:, :, c0:c0 + cn], src)\
                        .then_inc(w_full[n % NRAW], 16)
            for t in range(LT):
                sp.wait_ge(*read("fin", t))
                sp.dma_start(out[0, t * P:t * P + P, :], r(16384 + 1024 * t, 1024)).then_inc(*out_done.mark(t, by=16))
            sp.wait_ge(*out_done.at(LT - 1))

        @block.scalar
        def _(act):
            A = nc.scalar.activation

            def norm(l, which, ntok):
                for k in range(KC):
                    if l == 0 and which == "mix":
                        if k == 0:
                            act.wait_ge(*read("x", TT - 1))
                    else:
                        act.wait_ge(*(read("out", l, k) if which == "ffn" else read("ff2", l - 1, NG - 1, k)))
                    if k >= 2:
                        act.wait_ge(*pe_done.at("ss", l, which, k - 2))
                    A(sq_n[:, k % 2, 0:ntok], xT[:, k, 0:ntok], ACT.Square).then_inc(*act_done.mark("sq", l, which, k))
                act.wait_ge(*full("ss", l, which))
                act.wait_ge(*dve_done.at("eps"))
                A(rs_n[:, 0:ntok], pair("ss", l, which)[:, 0:ntok], ACT.Sqrt, scale=1.0 / D, bias=eps[:, 0:1])\
                    .then_inc(*free("ss", l, which))
                if which == "ffn" or l == 0:
                    act.wait_ge(*dve_done.at("gain", l, int(which == "ffn")))
                for k in range(KC):
                    act.wait_ge(*dve_done.at("hx", l, which, k))
                    if which == "fin":
                        A(fin_T[:, k, 0:ntok], ht[:, k % 2, 0:ntok], ACT.Copy, scale=pcols[:, 0, k:k + 1])\
                            .then_inc(*act_done.mark("fin", k))
                        continue
                    w = int(which == "ffn")
                    for t0, t1, c in spans(ntok):
                        A(ht[:, k % 2, t0:t1], ht[:, k % 2, t0:t1], ACT.Identity, scale=gains[:, l, w, k, c:c + 1],
                          bias=modcs[:, l, 24 * w + k, c:c + 1]).then_inc(*act_done.mark("aff", l, which, k))
                    act.wait_ge(*act_done.at("aff", l, which, k))
                    A(hh[:, k, 0:ntok], ht[:, k % 2, 0:ntok], ACT.Copy).then_inc(*act_done.mark("hhi", l, which, k))

            act.wait_ge(*cond_in.at())
            A(ccol[:, :, :], craw_c[:, :, :], ACT.Silu).then_inc(*act_done.mark("ccol"))
            for l in range(DEPTH):
                nt = TOK if l == 0 else LAT
                if l == 0:
                    for t in range(TT):
                        act.wait_ge(*full("x", t))
                        A(xT[:, :, t * P:t * P + P], pair("x", t)[:, :].rearrange("p (k n) -> p k n", k=KC), ACT.Copy)\
                            .then_inc(*free("x", t))
                norm(l, "mix", TOK)
                act.wait_ge(*full("ba", l))
                A(bg[:, :, 0:8], pair("ba", l)[:, 0:96].rearrange("p (t n) -> p t n", t=TT)[:, :, 0:8], ACT.Sigmoid)\
                    .then_inc(*free("ba", l, by=1))
                act.wait_ge(*dve_done.at("absa", l))
                A(gtmp[:, :, :], gtmp[:, :, :], ACT.Exp, scale=-1.0).then_inc(*act_done.mark("expa", l))
                act.wait_ge(*dve_done.at("1+e", l))
                A(gtmp[:, :, :], gtmp[:, :, :], ACT.Ln).then_inc(*act_done.mark("lna", l))
                act.wait_ge(*abc_in.at(l))
                A(abc[:, 0, :], abc[:, 0, :], ACT.Exp).then_inc(*act_done.mark("expA", l))
                act.wait_ge(*dve_done.at("craw0", l))

                def silu(j):
                    i, m = divmod(j, 4)
                    act.wait_ge(*dve_done.at("conv", l, j))
                    o = (qT, kT, vT4)[i][:, m, :]
                    A(o[:, 0:LAT], cacc[:, j % 2, 0:LAT], ACT.Silu).then_inc(*act_done.mark("silu0", l, i, m))
                    A(o[:, LAT:TOK], cacc[:, j % 2, LAT + 4:TOK + 4], ACT.Silu).then_inc(*act_done.mark("silu", l, i, m))

                for j in range(12):
                    i, m = divmod(j, 4)
                    act.wait_ge(*full("c", l, i, m))
                    if j >= 2:
                        act.wait_ge(*dve_done.at("conv", l, j - 2))
                    ps = pair("c", l, i, m)
                    A(craw[:, j % 2, 2:2 + LAT], ps[:, 0:LAT], ACT.Copy).then_inc(*free("c", l, i, m, by=1))
                    A(craw[:, j % 2, LAT + 6:TOK + 6], ps[:, LAT:TOK], ACT.Copy).then_inc(*free("c", l, i, m, by=1))
                    if j:
                        silu(j - 1)
                silu(11)
                for j in range(9):
                    if j < 8:
                        x = (qT, kT)[j // 4][:, j % 4, :]
                        if j == 0:
                            act.wait_ge(*act_done.at("silu", l, 2, 3))
                        if j >= 2:
                            act.wait_ge(*full("css", l, j - 2))
                        A(csq[:, j % 2, :], x, ACT.Square).then_inc(*act_done.mark("csq", l, j))
                    if j:
                        act.wait_ge(*full("css", l, j - 1))
                        if j >= 3:
                            act.wait_ge(*dve_done.at("l2", l, j - 3))
                        A(crr[:, (j - 1) % 2, :], pair("css", l, j - 1)[:, 0:TOK], ACT.Sqrt, bias=eps[:, 0:1])\
                            .then_inc(*free("css", l, j - 1))
                act.wait_ge(*read("gc", l))
                A(gex[:, :, 0, :], gcs[:, :, 0:8], ACT.Exp).then_inc(*act_done.mark("gex0", l))
                A(gex[:, :, 2:4, :].rearrange("p t a b -> p t (a b)"), gcs[:, :, 16:32], ACT.Exp)\
                    .then_inc(*act_done.mark("gex2", l))
                act.wait_ge(*dve_done.at("gdiff", l))
                A(gex[:, :, 1, :], gtmp[:, :, :], ACT.Exp).then_inc(*act_done.mark("gex1", l))
                for s in range(TT):
                    for d in range(2):
                        act.wait_ge(*full("bc", l, s, d))
                        if s:
                            act.wait_ge(*full("vn", l, 2 * s - 1, d))
                        A(flat(ebuf[d]), pair("bc", l, s, d)[:, 0:512], ACT.Exp).then_inc(*free("bc", l, s, d, by=1))
                        act.wait_ge(*read("bc", l, s, d))
                        A(flat(wbuf[d]), flat(wbuf[d]), ACT.Abs).then_inc(*act_done.mark("abs", l, s, d))
                        act.wait_ge(*act_done.at("abs", l, s, d))
                        A(flat(wbuf[d]), flat(wbuf[d]), ACT.Exp, scale=-1.0).then_inc(*act_done.mark("W", l, s, d))
                    for i in range(5):
                        for d in range(2):
                            act.wait_ge(*full("pw", l, s, d, i))
                            if i == 0:
                                act.wait_ge(*dve_done.at("A", l, s, d))
                            A(flat(power(d, i)[2]), pair("pw", l, s, d, i)[:, 0:512], ACT.Copy)\
                                .then_inc(*free("pw", l, s, d, i, by=1 if i < 4 else 2))
                    for d in range(2):
                        act.wait_ge(*full("kcd", l, s, d))
                        act.wait_ge(*pool_done.at("qd", l, s, d))
                        A(flat(ebuf[d]), pair("kcd", l, s, d)[:, 0:512], ACT.Copy, scale=-1.0)\
                            .then_inc(*free("kcd", l, s, d))
                    for c in range(2):
                        for d in range(2):
                            n, lo = 2 * s + c, 64 * (c if d == 0 else 1 - c)
                            act.wait_ge(*full("vn", l, n, d))
                            A(flat(tbuf[d])[lo:lo + 64, :], pair("vn", l, n, d)[0:64, 0:512], ACT.Copy)\
                                .then_inc(*free("vn", l, n, d))
                for m in range(4):
                    act.wait_ge(*full("z", l, m))
                    A(siluz[:, m, 0:nt], pair("z", l, m)[:, 0:nt], ACT.Silu).then_inc(*free("z", l, m))
                act.wait_ge(*dve_done.at("oss", l))
                A(small[:, 0:24], small[:, 0:24], ACT.Sqrt, scale=1.0 / P, bias=eps[:, 0:1])\
                    .then_inc(*act_done.mark("ors", l))
                for j in range(6):
                    n = TOK if j >= 4 else nt
                    act.wait_ge(*full("qk", l, j))
                    A(qk[:, j, 0:n], pair("qk", l, j)[:, 0:n], ACT.Copy).then_inc(*free("qk", l, j))
                act.wait_ge(*full("vaT", l))
                A(vraw[:, 0, :], pair("vaT", l)[:, 0:TOK], ACT.Copy).then_inc(*free("vaT", l))
                act.wait_ge(*full("va", l))
                A(flat(va), pair("va", l)[:, 0:TOK], ACT.Copy).then_inc(*free("va", l))
                act.wait_ge(*read("va", l))
                for j in range(6):
                    n = TOK if j >= 4 else nt
                    if j:
                        act.wait_ge(*full("ass", l, j - 1))
                        act.wait_ge(*dve_done.at("qkn", l, j - 1))
                    A(asq[:, 0:n], qk[:, j, 0:n], ACT.Square).then_inc(*act_done.mark("asq", l, j))
                    act.wait_ge(*full("ass", l, j))
                    A(arr[:, 0:n], pair("ass", l, j)[:, 0:n], ACT.Sqrt, scale=1.0 / HD, bias=eps[:, 0:1])\
                        .then_inc(*free("ass", l, j))
                attention(act, l, "A")
                for name, dst in (("qb", qB), ("kb", kB)):
                    n = TOK if name == "kb" else nt
                    for m in range(4):
                        act.wait_ge(*full(name, l, m))
                        A(dst[:, m, 0:n], pair(name, l, m)[:, 0:n], ACT.Copy).then_inc(*free(name, l, m))
                for m in range(4):
                    act.wait_ge(*full("vbT", l, m))
                    if m >= 2:
                        act.wait_ge(*full("vb", l, m - 2))
                    A(vraw[:, m % 2, :], pair("vbT", l, m)[:, 0:TOK], ACT.Copy).then_inc(*free("vbT", l, m))
                attention(act, l, "B")
                for x in range(24):
                    act.wait_ge(*full("gate", l, x))
                    if x >= 2:
                        act.wait_ge(*dve_done.at("merge", l, x - 2))
                    A(gsig[:, x % 2, 0:nt], pair("gate", l, x)[:, 0:nt], ACT.Sigmoid).then_inc(*free("gate", l, x))
                for k in range(KC):
                    act.wait_ge(*dve_done.at("merge", l, 23))
                    A(hh[:, k, 0:nt], mT[:, k, 0:nt], ACT.Copy).then_inc(*act_done.mark("mhi", l, k))
                norm(l, "ffn", nt)
                for j in range(FF // P):
                    act.wait_ge(*full("ff1", l, j))
                    if j >= 2:
                        act.wait_ge(*dve_done.at("flo", l, j - 2))
                    else:
                        act.wait_ge(*dve_done.at("h", l, "ffn", KC - 1))
                    f = ftmp[:, j % 2, 0:nt]
                    A(f, pair("ff1", l, j)[:, 0:nt], ACT.Relu).then_inc(*free("ff1", l, j))
                    act.wait_ge(*dve_done.at("fsq", l, j))
                    A(fh[:, j // GF % 2, j % GF, 0:nt], f, ACT.Copy).then_inc(*act_done.mark("fhi", l, j))
            norm(DEPTH, "fin", LAT)
            for t in range(LT):
                act.wait_ge(*full("fin", t))
                A(r(16384 + 1024 * t, 1024), pair("fin", t)[:, :], ACT.Copy).then_inc(*free("fin", t))

        @block.vector
        def _(dve):
            V = nc.vector

            def norm(l, which, ntok):
                dve.wait_ge(*read("ss", l, which))
                V.reciprocal(rs_n[:, 0:ntok], rs_n[:, 0:ntok]).then_inc(*dve_done.mark("rs", l, which))
                dve.wait_ge(*dve_done.at("rs", l, which))
                for k in range(KC + 1):
                    if k < KC:
                        if k >= 2:
                            dve.wait_ge(*(act_done.at("fin", k - 2) if which == "fin" else dve_done.at("h", l, which, k - 2)))
                        V.tensor_tensor(ht[:, k % 2, 0:ntok], xT[:, k, 0:ntok], rs_n[:, 0:ntok], ALU.mult)\
                            .then_inc(*dve_done.mark("hx", l, which, k))
                    if k and which != "fin":
                        dve.wait_ge(*act_done.at("hhi", l, which, k - 1))
                        V.tensor_tensor(hl[:, k - 1, 0:ntok], ht[:, (k - 1) % 2, 0:ntok],
                                        hh[:, k - 1, 0:ntok].bitcast(F32), ALU.subtract)\
                            .then_inc(*dve_done.mark("h", l, which, k - 1))

            def attention(l, br):
                work = att_items(l)
                o = oA if br == "A" else oB
                for i in range(len(work) + 3):
                    if i < len(work):
                        h, t = work[i]
                        n = TOK if t < LT else CTX
                        dve.wait_ge(*full("S", br, l, i))
                        ps = pair("S", br, l, i)
                        if br == "B" and t < LT:
                            dve.wait_ge(*pool_done.at("E", l, h))
                            V.tensor_tensor(ps[:, 0:LAT], ps[:, 0:LAT],
                                            ebias[:, h % 2, 6 - 2 * t + 0:14 - 2 * t, :].rearrange("p a b -> p (a b)"),
                                            ALU.add).then_inc(*dve_done.mark("bias", l, i))
                            dve.wait_ge(*dve_done.at("bias", l, i))
                        if i >= 2:
                            dve.wait_ge(*read("S", br, l, i - 2))
                        V.tensor_reduce(stat[:, i % 2, 0:1], ps[:, 0:n], AX.X, ALU.max, negate=True)\
                            .then_inc(*dve_done.mark("max", br, l, i))
                        dve.wait_ge(*dve_done.at("max", br, l, i))
                        V.tensor_scalar(stat[:, i % 2, 1:2], stat[:, i % 2, 0:1], SCALE, None, ALU.mult)\
                            .then_inc(*dve_done.mark("nm", br, l, i))
                    if 1 <= i <= len(work):
                        j = i - 1
                        n = TOK if work[j][1] < LT else CTX
                        dve.wait_ge(*read("S", br, l, j))
                        V.reciprocal(stat[:, j % 2, 3:4], stat[:, j % 2, 2:3]).then_inc(*dve_done.mark("rsum", br, l, j))
                        dve.wait_ge(*dve_done.at("rsum", br, l, j))
                        V.tensor_scalar(prob[:, j % 2, 0:n], prob[:, j % 2, 0:n], stat[:, j % 2, 3:4], None, ALU.mult)\
                            .then_inc(*dve_done.mark("prob", br, l, j))
                    if i >= 3:
                        j = i - 3
                        h, t = work[j]
                        dve.wait_ge(*full("O", br, l, j))
                        lo = HD * (h % 2)
                        V.tensor_copy(o[lo:lo + HD, h // 2, t * P:t * P + P], pair("O", br, l, j)[0:HD, 0:P])\
                            .then_inc(*free("O", br, l, j))

            def modulation(l, i):
                dve.wait_ge(*full("mod", l, i))
                V.tensor_scalar(modcs[:, l, i, :], pair("mod", l, i)[:, 0:2], pcols[:, l, R_BMOD + i:R_BMOD + i + 1], None,
                                ALU.add).then_inc(*free("mod", l, i))

            def low(l, j):
                nt = TOK if l == 0 else LAT
                dve.wait_ge(*act_done.at("fhi", l, j))
                V.tensor_tensor(fl[:, j // GF % 2, j % GF, 0:nt], ftmp[:, j % 2, 0:nt],
                                fh[:, j // GF % 2, j % GF, 0:nt].bitcast(F32), ALU.subtract)\
                    .then_inc(*dve_done.mark("flo", l, j))

            def norm_gain(l, w):
                dve.wait_ge(*read("mod", l, 24 * w + 15))
                V.scalar_tensor_tensor(out=gains[:, l, w, :, :], in0=modcs[:, l, 24 * w + 8:24 * w + 16, :], scalar=1.0,
                                       in1=along(pcols[:, l, R_MIX + 8 * w:R_MIX + 8 * w + 8], 2),
                                       op0=ALU.add, op1=ALU.mult).then_inc(*dve_done.mark("gain", l, w))

            V.memset(eps[:, :], EPS).then_inc(*dve_done.mark("eps"))
            for l in range(DEPTH):
                nt = TOK if l == 0 else LAT
                pcol, modc = pcols[:, l, :], modcs[:, l, :, :]
                if l == 0:
                    for ll in range(DEPTH):
                        dve.wait_ge(*full("params", ll))
                        V.tensor_copy(pcols[:, ll, :], pair("params", ll)[:, 0:P]).then_inc(*free("params", ll))
                        dve.wait_ge(*read("params", ll))
                    for i in range(16):
                        modulation(0, i)
                    norm_gain(0, 0)
                norm(l, "mix", TOK)
                dve.wait_ge(*read_first("ba", l))
                dve.wait_ge(*abc_in.at(l))
                V.tensor_tensor(gt[:, :, :], pair("ba", l)[:, 0:96].rearrange("p (t n) -> p t n", t=TT)[:, :, 8:16],
                                abc[:, 1, :].unsqueeze(1).to_broadcast([P, TT, 8]), ALU.add)\
                    .then_inc(*free("ba", l, by=1))
                dve.wait_ge(*read("ba", l))
                V.scalar_tensor_tensor(out=gtmp[:, :, :], in0=gt[:, :, :], scalar=-1.0, in1=gt[:, :, :],
                                       op0=ALU.mult, op1=ALU.max).then_inc(*dve_done.mark("absa", l))
                dve.wait_ge(*act_done.at("expa", l))
                V.tensor_scalar(gtmp[:, :, :], gtmp[:, :, :], 1.0, None, ALU.add).then_inc(*dve_done.mark("1+e", l))
                dve.wait_ge(*act_done.at("lna", l))
                V.scalar_tensor_tensor(out=gt[:, :, :], in0=gt[:, :, :], scalar=0.0, in1=gtmp[:, :, :],
                                       op0=ALU.max, op1=ALU.add).then_inc(*dve_done.mark("sp", l))
                dve.wait_ge(*act_done.at("expA", l))
                dve.wait_ge(*dve_done.at("sp", l))
                V.scalar_tensor_tensor(out=gt[:, :, :], in0=gt[:, :, :], scalar=-1.0,
                                       in1=abc[:, 0, :].unsqueeze(1).to_broadcast([P, TT, 8]),
                                       op0=ALU.mult, op1=ALU.mult).then_inc(*dve_done.mark("g", l))
                V.tensor_scalar(nbeta[:, :, :], bg[:, :, 0:8], -1.0, None, ALU.mult).then_inc(*dve_done.mark("nbeta", l))
                dve.wait_ge(*spilled.at(l))
                V.memset(craw[:, :, :], 0.0).then_inc(*dve_done.mark("craw0", l))
                W = TOK + 4
                for j in range(12):
                    dve.wait_ge(*read("c", l, j // 4, j % 4))
                    if j >= 2:
                        dve.wait_ge(*act_done.at("silu", l, (j - 2) // 4, (j - 2) % 4))
                    for q in range(CONV):
                        tap = pcol[:, R_CONV + 12 * q + j:R_CONV + 12 * q + j + 1]
                        if q == 0:
                            ins = V.tensor_scalar(cacc[:, j % 2, 0:W], craw[:, j % 2, 0:W], tap, None, ALU.mult)
                        else:
                            dve.wait_ge(*dve_done.at("tap", l, j, q - 1))
                            ins = V.scalar_tensor_tensor(out=cacc[:, j % 2, 0:W], in0=craw[:, j % 2, q:q + W],
                                                         scalar=tap, in1=cacc[:, j % 2, 0:W], op0=ALU.mult, op1=ALU.add)
                        ins.then_inc(*dve_done.mark(*(("tap", l, j, q) if q < CONV - 1 else ("conv", l, j))))
                for m in range(4):
                    dve.wait_ge(*full("vtok", l, m))
                    V.tensor_copy(vtok[:, :, m * P:m * P + P],
                                  pair("vtok", l, m)[:, 0:TOK].rearrange("p (t n) -> p t n", t=TT))\
                        .then_inc(*free("vtok", l, m))
                for j in range(8):
                    x = (qT, kT)[j // 4][:, j % 4, :]
                    dve.wait_ge(*read("css", l, j))
                    V.reciprocal(crr[:, j % 2, :], crr[:, j % 2, :]).then_inc(*dve_done.mark("crr", l, j))
                    dve.wait_ge(*dve_done.at("crr", l, j))
                    V.scalar_tensor_tensor(out=x, in0=x, scalar=float(P) ** -0.5 if j < 4 else 1.0,
                                           in1=crr[:, j % 2, :], op0=ALU.mult, op1=ALU.mult)\
                        .then_inc(*dve_done.mark("l2", l, j))
                for h in range(4):
                    dve.wait_ge(*full("ktok", l, h))
                    V.tensor_copy(ktok[:, :, h * P:h * P + P],
                                  pair("ktok", l, h)[:, 0:TOK].rearrange("p (t n) -> p t n", t=TT))\
                        .then_inc(*free("ktok", l, h))
                dve.wait_ge(*full("gc", l))
                V.tensor_copy(gcs[:, :, :], pair("gc", l)[:, 0:32 * TT].rearrange("p (t n) -> p t n", t=TT))\
                    .then_inc(*free("gc", l))
                dve.wait_ge(*read("gc", l))
                V.tensor_tensor(gtmp[:, :, :], gcs[:, :, 8:16], gcs[:, :, 0:8], ALU.subtract)\
                    .then_inc(*dve_done.mark("gdiff", l))
                dve.wait_ge(*act_done.at("gex0", l))
                V.tensor_tensor(gex[:, :, 0, :], gex[:, :, 0, :], bg[:, :, 0:8], ALU.mult)\
                    .then_inc(*dve_done.mark("gb", l))
                V.memset(state[:, 0, :, :], 0.0).then_inc(*dve_done.mark("S0", l))
                seen = set()
                filler = iter([(0, i) for i in range(16, 48)] + [(1, i) for i in range(48)])
                for s in range(TT):
                    for d in range(2):
                        t = tiles[d][s]
                        dve.wait_ge(*read_first("bc", l, s, d))
                        if s:
                            dve.wait_ge(*full("kcd", l, s - 1, d))
                        V.tensor_tensor(wbuf[d], pair("bc", l, s, d)[:, 0:512].rearrange("p (h n) -> p h n", h=C_H),
                                        along(gcs[:, t, 4 * d:4 * d + 4]), ALU.subtract)\
                            .then_inc(*free("bc", l, s, d, by=1))
                        dve.wait_ge(*act_done.at("W", l, s, d))
                        dve.wait_ge(*full("G", l, s, d))
                        if s:
                            dve.wait_ge(*full("so", l, 2 * s - 1, d))
                        ps = pair("G", l, s, d)
                        V.tensor_tensor(flat(pbuf[d]), ps[:, 0:512], flat(wbuf[d]), ALU.mult)\
                            .then_inc(*free("G", l, s, d, by=1))
                        V.tensor_tensor(flat(aqbuf[d]), ps[:, 512:1024], flat(wbuf[d]), ALU.mult)\
                            .then_inc(*free("G", l, s, d, by=1))
                        dve.wait_ge(*read("G", l, s, d))
                        dve.wait_ge(*pool_done.at("MB", l, s, d))
                        V.tensor_tensor(pbuf[d], pbuf[d], p2buf[d], ALU.mult).then_inc(*dve_done.mark("A", l, s, d))
                    for d in range(2):
                        dve.wait_ge(*full("AT", l, s, d))
                        ps = pair("AT", l, s, d)
                        V.tensor_copy(flat(tbuf[d]), ps[:, 0:512]).then_inc(*free("AT", l, s, d, by=1))
                        V.tensor_tensor(xbuf[d], ps[:, 0:512].rearrange("p (h n) -> p h n", h=C_H), over_heads(ident),
                                        ALU.add).then_inc(*free("AT", l, s, d, by=1))
                    for i in range(5):
                        if i < 4:
                            for d in range(2):
                                dve.wait_ge(*full("pw", l, s, d, i))
                                V.tensor_copy(flat(power(d, i)[3]), pair("pw", l, s, d, i)[:, 512:1024])\
                                    .then_inc(*free("pw", l, s, d, i, by=1))
                        for d in range(2):
                            dve.wait_ge(*full("X", l, s, d, i))
                            V.tensor_tensor(flat(xbuf[d]), pair("X", l, s, d, i)[:, 0:512], flat(xbuf[d]), ALU.add)\
                                .then_inc(*free("X", l, s, d, i))
                        if l == 0:
                            for _, m in zip(range(3), filler):
                                modulation(*m)
                    for c in range(2):
                        for d in range(2):
                            t, cc, n = tiles[d][s], (c if d == 0 else 1 - c), 2 * s + c
                            lo = 64 * cc
                            ps = pair("so", l, n, d)
                            dve.wait_ge(*full("so", l, n, d))
                            if want_out(l, t):
                                o = Otok[lo:lo + 64, t, :]
                                if (t, cc) in seen:
                                    V.tensor_tensor(o, ps[0:64, 512:1024], o, ALU.add).then_inc(*free("so", l, n, d, by=1))
                                else:
                                    V.tensor_copy(o, ps[0:64, 512:1024]).then_inc(*free("so", l, n, d, by=1))
                                seen.add((t, cc))
                            dve.wait_ge(*pool_done.at("Sdec", l, n, d))
                            S1 = state[:, (n + 1) % 2, 4 * d:4 * d + 4, :].rearrange("p a b -> p (a b)")
                            V.tensor_tensor(S1, ps[:, 0:512], S1, ALU.add)\
                                .then_inc(*free("so", l, n, d, by=1 if want_out(l, t) else 2))
                if l == 0:
                    for ll, w in ((0, 1), (1, 0), (1, 1)):
                        norm_gain(ll, w)
                to = TT if l == 0 else LT
                dve.wait_ge(*pool_done.at("osq", l))
                V.tensor_reduce(small[:, 0:4 * to], osq[:, 0:to, :].rearrange("p t (h n) -> p (t h) n", h=C_H), AX.X,
                                ALU.add).then_inc(*dve_done.mark("oss", l))
                dve.wait_ge(*act_done.at("ors", l))
                V.reciprocal(small[:, 32:32 + 4 * to], small[:, 0:4 * to]).then_inc(*dve_done.mark("orr", l))
                dve.wait_ge(*dve_done.at("orr", l))
                ov = Otok[:, 0:to, :].rearrange("p t (h n) -> p (t h) n", h=C_H)
                V.tensor_tensor(ov, ov, along(small[:, 32:32 + 4 * to]), ALU.mult).then_inc(*dve_done.mark("onrm", l))
                for t in range(to):
                    dve.wait_ge(*full("oT", l, t))
                    if t == 0:
                        dve.wait_ge(*read("z", l, 3))
                    V.scalar_tensor_tensor(out=oC[:, :, t * P:t * P + P],
                                           in0=pair("oT", l, t)[:, 0:512].rearrange("p (h n) -> p h n", h=C_H),
                                           scalar=pcol[:, R_ONORM:R_ONORM + 1], in1=siluz[:, :, t * P:t * P + P],
                                           op0=ALU.mult, op1=ALU.mult).then_inc(*free("oT", l, t))
                for j in range(6):
                    n = TOK if j >= 4 else nt
                    dve.wait_ge(*read("ass", l, j))
                    V.reciprocal(arr[:, 0:n], arr[:, 0:n]).then_inc(*dve_done.mark("arr", l, j))
                    dve.wait_ge(*dve_done.at("arr", l, j))
                    g = pcol[:, (R_QN if j < 4 else R_KN):(R_QN if j < 4 else R_KN) + 1]
                    V.scalar_tensor_tensor(out=qk[:, j, 0:n], in0=qk[:, j, 0:n], scalar=g, in1=arr[:, 0:n],
                                           op0=ALU.mult, op1=ALU.mult).then_inc(*dve_done.mark("qkn", l, j))
                    dve.wait_ge(*full("rot", l, j))
                    V.tensor_tensor(rtmp[:, 0, :], pair("rot", l, j)[:, 0:LAT], cst[:, C_SIN:C_SIN + LAT], ALU.mult)\
                        .then_inc(*free("rot", l, j))
                    dve.wait_ge(*pool_done.at("cos", l, j))
                    dve.wait_ge(*read("rot", l, j))
                    V.tensor_tensor(qk[:, j, 0:LAT], rtmp[:, 0, :], rtmp[:, 1, :], ALU.add)\
                        .then_inc(*dve_done.mark("rope", l, j))
                attention(l, "A")
                for m in range(4):
                    dve.wait_ge(*full("vb", l, m))
                    V.tensor_copy(vB[:, :, m * P:m * P + P],
                                  pair("vb", l, m)[:, 0:TOK].rearrange("p (t n) -> p t n", t=TT)).then_inc(*free("vb", l, m))
                attention(l, "B")
                for x in range(24):
                    dc, n = divmod(x, 3)
                    dve.wait_ge(*full("br", l, x))
                    dve.wait_ge(*read("gate", l, x))
                    g, acc = gsig[:, x % 2, 0:nt], mT[:, dc, 0:nt]
                    V.tensor_tensor(g if n else acc, pair("br", l, x)[:, 0:nt], g, ALU.mult).then_inc(*free("br", l, x))
                    dve.wait_ge(*read("br", l, x))
                    if n:
                        V.tensor_tensor(acc, acc, g, ALU.add).then_inc(*dve_done.mark("merge", l, x))
                    else:
                        V.memset(small[:, 63:64], 0.0).then_inc(*dve_done.mark("merge", l, x))
                for k in range(KC):
                    dve.wait_ge(*act_done.at("mhi", l, k))
                    V.tensor_tensor(hl[:, k, 0:nt], mT[:, k, 0:nt], hh[:, k, 0:nt].bitcast(F32), ALU.subtract)\
                        .then_inc(*dve_done.mark("mlo", l, k))

                def residual(key, j, gate):
                    dve.wait_ge(*full(*key))
                    sp_ = spans(nt)
                    for t0, t1, c in sp_:
                        V.scalar_tensor_tensor(out=xT[:, j, t0:t1], in0=pair(*key)[:, t0:t1],
                                               scalar=modc[:, gate + j, c:c + 1], in1=xT[:, j, t0:t1],
                                               op0=ALU.mult, op1=ALU.add).then_inc(*free(*key, by=2 // len(sp_)))

                dve.wait_ge(*x_back.at(l))
                for j in range(KC):
                    residual(("out", l, j), j, 16)
                norm(l, "ffn", nt)
                for g in range(NG + 1):
                    if g < NG:
                        for j in range(GF * g, GF * g + GF):
                            f = ftmp[:, j % 2, 0:nt]
                            dve.wait_ge(*read("ff1", l, j))
                            V.tensor_tensor(f, f, f, ALU.mult).then_inc(*dve_done.mark("fsq", l, j))
                            if j % GF:
                                low(l, j - 1)
                        low(l, GF * g + GF - 1)
                    if g:
                        for j in range(KC):
                            if g > 1:
                                dve.wait_ge(*read("ff2", l, g - 2, j))
                            residual(("ff2", l, g - 1, j), j, 40)
            dve.wait_ge(*full("params", DEPTH))
            V.tensor_copy(pcols[:, 0, 0:KC], pair("params", DEPTH)[:, 0:KC]).then_inc(*free("params", DEPTH))
            norm(DEPTH, "fin", LAT)

        @block.gpsimd
        def _(pool):
            G = nc.gpsimd
            crow = a["conv_c"]
            for c, n in enumerate(("c", "c_ctx")):
                v = a[n][0] if n == "c" else a[n]
                pool.dma_start(craw_c[:, c, :], v.rearrange("(p k) -> p k", k=KC)).then_inc(*cond_in.mark(by=16))

            def params(l):
                if l:
                    pool.wait_ge(*full("params", l - 1))
                rows = lambda v: v.rearrange("(k p) -> k p", p=P)
                one = lambda v: v.rearrange("(a n) -> a n", a=1)
                if l == DEPTH:
                    return [(prow[0:KC, :], rows(a["norm_final"]))]
                out_ = [(prow[R_BMOD:R_BMOD + 48, :], rows(a["b_mod"][l])),
                        (prow[R_MIX:R_MIX + KC, :], rows(a["norm_mix"][l])),
                        (prow[R_FFN:R_FFN + KC, :], rows(a["norm_ffn"][l]))]
                for q in range(CONV):
                    out_.append((prow[R_CONV + 12 * q:R_CONV + 12 * q + 12, :], rows(crow[l, q])))
                out_.append((prow[R_ONORM:R_ONORM + 1, :], one(a["o_norm_c"][l])))
                for row, name in ((R_QN, "q_norm_a"), (R_KN, "k_norm_a")):
                    for u in range(2):
                        out_.append((prow[row:row + 1, u * HD:u * HD + HD], one(a[name][l])))
                out_.append((prow[R_FIN:R_FIN + 1, :], rows(a["norm_final"])[0:1, :]))
                return out_

            def load_params(l):
                for dst, src in params(l):
                    pool.dma_start(dst, src).then_inc(*params_in.mark(l, by=16))

            def split(l, name, i=0):
                w = raw_weights(pool, l, name, i)
                n = where[l, name, i][2]
                if n >= NSPL:
                    pool.wait_ge(*full(*book.get(("last",) + order[n - NSPL], ("x", 0))))
                h_, l_ = slot_view(wh, n % NSPL, l, name, i), slot_view(wl, n % NSPL, l, name, i)
                G.tensor_copy(h_, w).then_inc(*pool_done.mark("whi", l, name, i))
                pool.wait_ge(*pool_done.at("whi", l, name, i))
                G.tensor_tensor(l_, w, h_.bitcast(F32), ALU.subtract).then_inc(*pool_done.mark("wlo", l, name, i))

            for l in range(DEPTH):
                load_params(l)
            for l in range(DEPTH):
                nt = TOK if l == 0 else LAT
                if l:
                    pool.wait_ge(*dve_done.at("g", l - 1))
                for u, name in enumerate(("a_log_c", "dt_bias_c")):
                    pool.dma_start(abc[:, u, :], a[name][l].rearrange("(a d) h -> a (d h)", a=1).to_broadcast([P, 8]))\
                        .then_inc(*abc_in.mark(l, by=16))
                if l == 0:
                    load_params(DEPTH)
                split(l, "ba")
                for i in range(3):
                    split(l, "c", i)
                pool.wait_ge(*dve_done.at("hx", l, "mix", KC - 1))
                pool.dma_start(x_store, R[:, XT0:RN]).then_inc(*spilled.mark(l, by=16))
                for i in range(3, 12):
                    split(l, "c", i)
                if l:
                    pool.wait_ge(*e_in.at(l - 1, B_H - 1))
                G.memset(bpad[:, :], 0.0).then_inc(*pool_done.mark("bpad0", l))
                pool.wait_ge(*pool_done.at("bpad0", l))
                pool.dma_start(bpad[:, 48:79], a["rpb_b"][l].rearrange("h r c -> (h r) c"))\
                    .then_inc(*rpb_in.mark(l, by=16))
                pool.wait_ge(*rpb_in.at(l))
                G.tensor_scalar(bpad[:, :], bpad[:, :], 1.0 / SCALE, None, ALU.mult).then_inc(*pool_done.mark("bpad", l))
                pool.wait_ge(*pool_done.at("bpad", l))
                pool.dma_start(scratch.rearrange("(r c) -> r c", c=127), bpad[:, :]).then_inc(*pad_out.mark(l, by=16))
                pool.wait_ge(*pad_out.at(l))
                skew = bass.AP(scratch.tensor, 63, [[127, B_H * 15], [-1, GRID_W], [1, GRID_W]])
                pool.dma_start(toeplitz, skew).then_inc(*skew_out.mark(l, by=16))
                for s in range(TT):
                    for d in range(2):
                        t = tiles[d][s]
                        if s == 0:
                            pool.wait_ge(*read("gc", l))
                            pool.wait_ge(*dve_done.at("nbeta", l))
                            pool.wait_ge(*dve_done.at("l2", l, 7))
                            pool.wait_ge(*read("ktok", l, 3))
                        if s:
                            pool.wait_ge(*full("so", l, 2 * s - 1, d))
                        G.tensor_tensor(rbuf[d], over_heads(masks[m_cum[d]]), along(gt[:, t, 4 * d:4 * d + 4]), ALU.mult)\
                            .then_inc(*pool_done.mark("R", l, s, d))
                        G.tensor_tensor(p2buf[d], over_heads(masks[m_strict[d]]), along(nbeta[:, t, 4 * d:4 * d + 4]),
                                        ALU.mult).then_inc(*pool_done.mark("MB", l, s, d))
                        G.tensor_tensor(vbbuf[d], vtok[:, t, :].rearrange("p (h n) -> p h n", h=C_H),
                                        along(bg[:, t, 4 * d:4 * d + 4]), ALU.mult).then_inc(*pool_done.mark("vb", l, s, d))
                    for d in range(2):
                        t = tiles[d][s]
                        pool.wait_ge(*read("bc", l, s, d))
                        G.tensor_tensor(qdbuf[d], qT[:, :, t * P:t * P + P], ebuf[d], ALU.mult)\
                            .then_inc(*pool_done.mark("qd", l, s, d))
                        pool.wait_ge(*read("G", l, s, d))
                        G.tensor_tensor(aqbuf[d], aqbuf[d], over_heads(masks[m_aq[d]]), ALU.mult)\
                            .then_inc(*pool_done.mark("AQ", l, s, d))
                        pool.wait_ge(*dve_done.at("gb", l))
                        G.tensor_tensor(wbuf[d], ktok[:, t, :].rearrange("p (h n) -> p h n", h=C_H),
                                        along(gex[:, t, 0, 4 * d:4 * d + 4]), ALU.mult)\
                            .then_inc(*pool_done.mark("kbe", l, s, d))
                    for d in range(2):
                        t = tiles[d][s]
                        pool.wait_ge(*full("pw", l, s, d, 4))
                        pool.wait_ge(*act_done.at("gex1", l))
                        G.tensor_tensor(pbuf[d], ktok[:, t, :].rearrange("p (h n) -> p h n", h=C_H),
                                        along(gex[:, t, 1, 4 * d:4 * d + 4]), ALU.mult)\
                            .then_inc(*pool_done.mark("kd", l, s, d))
                    for c in range(2):
                        for d in range(2):
                            t, cc, n = tiles[d][s], (c if d == 0 else 1 - c), 2 * s + c
                            pool.wait_ge(*(read("so", l, n - 1, d) if n else dve_done.at("S0", l)))
                            G.tensor_tensor(state[:, (n + 1) % 2, 4 * d:4 * d + 4, :], state[:, n % 2, 4 * d:4 * d + 4, :],
                                            along(gex[:, t, 2 + cc, 4 * d:4 * d + 4]), ALU.mult)\
                                .then_inc(*pool_done.mark("Sdec", l, n, d))
                to = TT if l == 0 else LT
                for d in range(2):
                    pool.wait_ge(*read("so", l, 2 * TT - 1, d))
                G.tensor_tensor(osq[:, 0:to, :], Otok[:, 0:to, :], Otok[:, 0:to, :], ALU.mult)\
                    .then_inc(*pool_done.mark("osq", l))
                for i in range(4):
                    split(l, "z", i)
                for i in range(4):
                    split(l, "qa", i)
                for i in range(2):
                    split(l, "ka", i)
                split(l, "va")
                for i in range(3):
                    split(l, "qb", i)
                for j in range(6):
                    pool.wait_ge(*dve_done.at("qkn", l, j))
                    if j:
                        pool.wait_ge(*dve_done.at("rope", l, j - 1))
                    G.tensor_tensor(rtmp[:, 1, :], qk[:, j, 0:LAT], cst[:, C_COS:C_COS + LAT], ALU.mult)\
                        .then_inc(*pool_done.mark("cos", l, j))
                pool.wait_ge(*skew_out.at(l))
                per = LT if l else TT

                def bias(h):
                    if h >= 2:
                        pool.wait_ge(*full("T", "B", l, per * (h - 1) - 1))
                    for u in range(2):
                        src = toeplitz[15 * h + 1 - u:15 * h + 15 - u].rearrange("j c k -> c j k")
                        pool.dma_start(ebias[u * 64:u * 64 + 64, h % 2, :, :], src).then_inc(*e_in.mark(l, h, by=16))
                    pool.wait_ge(*e_in.at(l, h))
                    e = ebias[:, h % 2, :, :]
                    G.tensor_tensor(e, e, cst[:, C_MASK:C_MASK + GRID_W].unsqueeze(1).to_broadcast([P, 14, GRID_W]), ALU.add)\
                        .then_inc(*pool_done.mark("E", l, h))

                for h in range(2):
                    bias(h)
                for name, i0 in (("qb", 3), ("kb", 0), ("vb", 0)):
                    for i in range(i0, 4):
                        split(l, name, i)
                for i in range(2):
                    split(l, "gate", i)
                for h in range(2, B_H):
                    bias(h)
                pool.wait_ge(*full("O", "B", l, per * B_H - 1))
                pool.dma_start(R[:, XT0:RN], x_store).then_inc(*x_back.mark(l, by=16))
                for i in range(2, 24):
                    split(l, "gate", i)
                for i in range(8):
                    split(l, "out", i)
                for g in range(NG + 1):
                    if g < NG:
                        for i in range(GF * g, GF * g + GF):
                            split(l, "ff1", i)
                    if g:
                        for i in range(4):
                            split(l, "ff2", 4 * (g - 1) + i)


_INS = ["x", "c", "ctx", "c_ctx", "w_mod", "b_mod", "norm_mix", "w_in", "q_norm_a", "k_norm_a", "rpb_b", "conv_c",
        "a_log_c", "dt_bias_c", "o_norm_c", "w_branch", "w_out", "norm_ffn", "w_ffn1", "w_ffn2", "norm_final"]


def build(nc, arrays, book):
    a = {k: nc.dram_tensor(f"in_{k}", v.shape, F32, kind="ExternalInput").ap() for k, v in arrays.items()}
    out = nc.dram_tensor("out_0", (1, LAT, D), F32, kind="ExternalOutput").ap()
    scratch = nc.dram_tensor("bias_pad", (B_H * 15 * 127,), F32, kind="Internal").ap()
    toeplitz = nc.dram_tensor("bias_skewed", (B_H * 15, GRID_W, GRID_W), F32, kind="Internal").ap()
    x_store = nc.dram_tensor("x_store", (P, KC * TOK), F32, kind="Internal").ap()
    program(nc, a, out, scratch, toeplitz, x_store, book)


def kernel(**inputs):
    import concourse.bacc as _bacc
    from concourse.bass_utils import run_bass_kernel_spmd as _run

    arrays = {k: np.ascontiguousarray(inputs[k]) for k in _INS}
    arrays["consts"] = constants()
    book = {"final": False}
    build(_bacc.Bacc("TRN2", target_bir_lowering=False, num_devices=1), arrays, book)
    book["final"] = True
    nc = _bacc.Bacc("TRN2", target_bir_lowering=False, num_devices=1)
    build(nc, arrays, book)
    r = _run(nc, [{f"in_{k}": v for k, v in arrays.items()}], core_ids=[0])
    return r.results[0]["out_0"]
```

```python
from contextlib import ExitStack

import numpy as np
import concourse.bass as bass
from concourse import mybir

F32 = mybir.dt.float32
F32R = mybir.dt.float32r
ALU = mybir.AluOpType
ACT = mybir.ActivationFunctionType
AX = mybir.AxisListType

P = 128
D = 1024
KC = D // P
LAT, CTX = 512, 256
TOK = LAT + CTX
TT, LT = TOK // P, LAT // P
DEPTH = 2
GRID_W, ROWS = 64, LAT // 64
HD = 64
A_H, A_KV, B_H, C_H = 8, 2, 8, 4
WIN_R, WIN_C = 8, 16
CONV = 5
FF = 4 * D
EPS = 1e-6
NEG = -1e30
SCALE = HD ** -0.5
O_QA, O_KA, O_VA, O_QB, O_KB, O_VB, O_QKV, O_Z, O_BETA, O_A, O_GATE = (
    int(v) for v in np.cumsum([0, 512, 128, 128, 512, 512, 512, 1536, 512, 8, 8]))
SLOT = KC * P
NRAW, NSPL = 3, 3
GF = 4
C_ID, C_ONE, C_BLK, C_ROT, C_UI, C_LI, C_US, C_LS, C_COS, C_SIN, C_MASK = (
    int(v) for v in np.cumsum([0, P, P, P, P, P, P, P, P, LAT, LAT]))
C_N = C_MASK + GRID_W
R_BMOD, R_MIX, R_FFN, R_CONV, R_ONORM, R_QN, R_KN, R_FIN = 0, 48, 56, 64, 124, 125, 126, 127


def constants():
    c = np.zeros((P, C_N), np.float32)
    i = np.arange(P)
    same = (i[:, None] // 64) == (i[None, :] // 64)
    c[:, C_ID:C_ID + P] = np.eye(P)
    c[:, C_ONE:C_ONE + P] = 1
    c[:, C_BLK:C_BLK + P] = same
    for m in range(0, P, 2):
        c[m + 1, C_ROT + m] = -1
        c[m, C_ROT + m + 1] = 1
    c[:, C_UI:C_UI + P] = same & (i[:, None] <= i[None, :])
    c[:, C_LI:C_LI + P] = same & (i[:, None] >= i[None, :])
    c[:, C_US:C_US + P] = same & (i[:, None] < i[None, :])
    c[:, C_LS:C_LS + P] = same & (i[:, None] > i[None, :])
    t = np.arange(LAT)
    freq = (10000.0 ** (-np.arange(0, HD // 2, 2, dtype=np.float32) / np.float32(HD // 2))).astype(np.float32)
    pair = (i % HD) // 2
    pos = np.where((pair < 16)[:, None], (t // GRID_W)[None, :], (t % GRID_W)[None, :]).astype(np.float32)
    ang = pos * freq[pair % 16][:, None]
    c[:, C_COS:C_COS + LAT] = np.cos(ang)
    c[:, C_SIN:C_SIN + LAT] = np.sin(ang)
    col = i % GRID_W
    c0 = np.clip(col - WIN_C // 2, 0, GRID_W - WIN_C)
    kc = np.arange(GRID_W)
    inside = (kc[None, :] >= c0[:, None]) & (kc[None, :] < c0[:, None] + WIN_C)
    c[:, C_MASK:C_MASK + GRID_W] = np.where(inside, 0.0, NEG)
    return c


class Signal:

    def __init__(self, nc, ctx, name, book):
        self.sem = ctx.enter_context(nc.semaphore(name))
        self.n, self.book, self.name = 0, book, name

    def mark(self, *key, by=1):
        self.n += by
        self.book[(self.name,) + key] = self.n
        return self.sem, by

    def at(self, *key):
        if self.book["final"]:
            return self.sem, self.book[(self.name,) + key]
        return self.sem, 1


def program(nc, a, out, scratch, toeplitz, x_store, book):
    book["final"] = book.get("final", False)
    with ExitStack() as ctx:
        def sb(name, shape):
            return ctx.enter_context(nc.sbuf_tensor(name, shape, F32))

        def sig(name):
            return Signal(nc, ctx, name, book)

        hh, hl = (ctx.enter_context(nc.sbuf_tensor(n, [P, KC, TOK], F32R)) for n in ("hh", "hl"))
        wring = sb("wring", [P, NRAW, SLOT])
        wh, wl = (ctx.enter_context(nc.sbuf_tensor(n, [P, NSPL, SLOT], F32R)) for n in ("wh", "wl"))
        cst = sb("cst", [P, C_N])
        pcols = sb("pcols", [P, 2, P])
        ccol = sb("ccol", [P, 2, KC])
        modcs = sb("modcs", [P, 2, 48, 2])
        gains = sb("gains", [P, 2, 2, KC, 2])
        small = sb("small", [P, 64])
        eps = sb("eps", [P, 1])
        XT0, RN = 21504, 27648
        r_at = nc.sbuf_base if not callable(nc.sbuf_base) else nc.sbuf_base()
        r_at = (r_at + 31) // 32 * 32
        R = sb("R", [P, RN])
        fh, fl = (nc.alloc_sbuf_tensor_at(n, [P, 2, GF, TOK], F32R, offset=r_at + 4 * o)
                  for n, o in (("fh", 0), ("fl", 2 * GF * TOK)))
        PS = [ctx.enter_context(nc.psum_tensor(f"ps{i}", [P, 1024], F32)) for i in range(4)]

        def r(at, *shape):
            n = int(np.prod(shape))
            v = R[:, at:at + n]
            if len(shape) == 2:
                v = v.rearrange("p (a b) -> p a b", a=shape[0])
            if len(shape) == 3:
                v = v.rearrange("p (a b c) -> p a b c", a=shape[0], b=shape[1])
            return v

        ident, ones, blk, rot = (cst[:, c:c + P] for c in (C_ID, C_ONE, C_BLK, C_ROT))
        oC, oA, oB = r(0, 4, TOK), r(3072, 4, TOK), r(6144, 4, TOK)
        S0 = 9216
        N0 = 4 * GF * TOK
        sq_n, rs_n, ht = r(N0, 2, TOK), r(N0 + 2 * TOK, TOK), r(N0 + 3 * TOK, 3, TOK)
        ftmp = r(N0, 2, TOK)
        xT = r(XT0, KC, TOK)
        fin_T = r(0, KC, TOK)
        qT, kT = r(0, 4, TOK), r(3072, 4, TOK)
        ktok, vtok, Otok = r(6144, TT, 512), r(9216, TT, 512), r(12288, TT, 512)
        U0 = 15360
        rbuf, ebuf, wbuf, pbuf, p2buf, tbuf, xbuf, aqbuf, qdbuf, vbbuf = (
            [r(U0 + (2 * b + d) * 512, 4, P) for d in range(2)] for b in range(10))
        state = r(U0 + 10240, 2, 8, P)
        craw = r(U0, 2, TOK + 8)
        cacc = r(U0 + 2048, 2, TOK + 8)
        csq, crr = r(U0 + 6144, 2, TOK), r(U0 + 8192, 2, TOK)
        vT4 = r(12288, 4, TOK)
        baT = r(9216, TOK)
        siluz = r(9216, 4, TOK)
        osq = r(6144, TT, 512)
        bg = sb("bg", [P, TT, 16])
        gt = sb("gt", [P, TT, 8])
        gtmp = sb("gtmp", [P, TT, 8])
        gcs = sb("gcs", [P, TT, 32])
        gex = sb("gex", [P, TT, 4, 8])
        nbeta = sb("nbeta", [P, TT, 8])
        abc = sb("abc", [P, 2, 8])
        qk = r(S0, 6, TOK)
        va = r(S0 + 4608, TT, 128)
        asq, arr = r(6144, TOK), r(6144 + TOK, TOK)
        rtmp = r(6144 + 2 * TOK, 2, LAT)
        qB, kB, vB = r(S0 + 5376, 4, TOK), r(S0 + 8448, 4, TOK), r(S0 + 11520, TT, 512)
        prob = r(S0 + 14592, 2, TOK)
        probT = r(S0 + 16128, 3, TT, P)
        ebias = r(S0, 2, 14, GRID_W)
        stat = sb("stat", [P, 2, 4])
        mT = r(S0, KC, TOK)
        gsig = r(S0 + 6144, 2, TOK)
        vraw = prob
        prow = sb("prow", [P, P])
        craw_c = sb("craw_c", [P, 2, KC])
        bpad = R[0:B_H * 15, U0 + 10240:U0 + 10240 + 127]
        mrow = sb("mrow", [2, 512])
        tiles = ([4, 5, 0, 1, 2, 3], [5, 4, 3, 2, 1, 0])
        masks = {k: cst[:, c:c + P] for k, c in (("UI", C_UI), ("LI", C_LI), ("US", C_US), ("LS", C_LS))}
        NG = FF // P // GF
        later_mods = [(0, cb) for cb in range(4, 12)] + [(1, cb) for cb in range(12)]
        m_cum, m_strict, m_aq = ("UI", "LI"), ("LS", "US"), ("UI", "LI")

        def want_out(l, t):
            return l == 0 or t < LT

        def flat(v):
            return v.rearrange("p a b -> p (a b)")

        def over_heads(v):
            return v.unsqueeze(1).to_broadcast([P, C_H, P])

        def along(v, n=P):
            return v.unsqueeze(2).to_broadcast([v.shape[0], v.shape[1], n])

        def power(d, i):
            one, two = (pbuf[d], tbuf[d]), (p2buf[d], rbuf[d])
            return (*one, *two) if i % 2 == 0 else (*two, *one)

        ps_full = [ctx.enter_context(nc.semaphore(f"ps_full{i}")) for i in range(4)]
        ps_free = [ctx.enter_context(nc.semaphore(f"ps_free{i}")) for i in range(4)]
        w_full = [ctx.enter_context(nc.semaphore(f"w_full{i}")) for i in range(NRAW)]
        params_in, cond_in, consts_in = sig("params_in"), sig("cond_in"), sig("consts_in")
        spilled, x_back = sig("spilled"), sig("x_back")
        x_in = [sig(f"x_in{t}") for t in range(TT)]
        act_done, dve_done, pool_done, pe_done = sig("act_done"), sig("dve_done"), sig("pool_done"), sig("pe_done")
        abc_in, rpb_in, pad_out, skew_out, out_done, e_in = (sig(n) for n in ("abc_in", "rpb_in", "pad_out", "skew_out", "out_done", "e_in"))
        block = ctx.enter_context(nc.Block())
        turn = {"n": 0, "w": 0}

        def take(pe, *key):
            n = turn["n"]
            turn["n"] += 1
            book[("ps",) + key] = n
            if n >= 4:
                pe.wait_ge(ps_free[n % 4], 2 * (n // 4))
            return PS[n % 4]

        def full(*key):
            n = book.get(("ps",) + key, 0) if book["final"] else 0
            return ps_full[n % 4], n // 4 + 1

        def filled(*key):
            return ps_full[book[("ps",) + key] % 4], 1

        def pair(*key):
            return PS[book.get(("ps",) + key, 0) % 4]

        def free(*key, by=2):
            return ps_free[book.get(("ps",) + key, 0) % 4], by

        def read(*key):
            n = book.get(("ps",) + key, 0) if book["final"] else 0
            return ps_free[n % 4], 2 * (n // 4 + 1)

        def read_first(*key):
            sem, n = read(*key)
            return sem, n - 1

        def att_items(l):
            return [(h, t) for h in range(A_H) for t in range(TT if l == 0 else LT)]

        w_in = a["w_in"]

        def cols(w, l, c0, n=P, r0=0, rn=KC):
            return w[l, r0 * P:(r0 + rn) * P, c0:c0 + n].rearrange("(k p) n -> p k n", p=P)

        c_order = [4, 5, 6, 7, 8, 9, 10, 11, 0, 1, 2, 3]

        def mod_slot(l, i):
            cb, kk = divmod(i, 4)
            src = a["w_mod"][l, :, 512 * cb:512 * cb + 512].rearrange("(p k) n -> p k n", k=KC)
            return l, "mod", i, 2, [(0, 512, src[:, 2 * kk:2 * kk + 2, :])], False

        def plan():
            for i in range(16):
                yield mod_slot(0, i)
            for l in range(DEPTH):
                for p in range(12):
                    yield l, "c", c_order[p], KC, [(0, P, cols(w_in, l, O_QKV + P * c_order[p]))], True
                    if p == 1:
                        yield l, "ba", 0, KC, [(0, P, cols(w_in, l, O_BETA))], True
                if l == 0:
                    for i in range(16, 48):
                        yield mod_slot(0, i)
                    for i in range(48):
                        yield mod_slot(1, i)
                for name, o, n in (("z", O_Z, 4), ("qa", O_QA, 4)):
                    for i in range(n):
                        yield l, name, i, KC, [(0, P, cols(w_in, l, o + P * i))], True
                for g in range(A_KV):
                    yield l, "ka", g, KC, [(u * HD, HD, cols(w_in, l, O_KA + g * HD, HD)) for u in range(2)], True
                yield l, "va", 0, KC, [(0, P, cols(w_in, l, O_VA))], True
                for name, o in (("qb", O_QB), ("kb", O_KB), ("vb", O_VB)):
                    for i in range(4):
                        yield l, name, i, KC, [(0, P, cols(w_in, l, o + P * i))], True
                for i in range(24):
                    dc, n = divmod(i, 3)
                    yield l, "gate", i, KC, [(0, P, cols(w_in, l, O_GATE + n * D + P * dc))], True
                    yield l, "br", i, 4, [(0, P, a["w_branch"][l, n, :, P * dc:P * dc + P]
                                           .rearrange("(k p) n -> p k n", p=P))], False
                for i in range(8):
                    yield l, "out", i, KC, [(0, P, cols(a["w_out"], l, P * i))], True
                for g in range(FF // P // GF + 1):
                    if g < FF // P // GF:
                        for i in range(GF):
                            yield l, "ff1", GF * g + i, KC, [(0, P, cols(a["w_ffn1"], l, P * (GF * g + i)))], True
                    if g:
                        for i in range(4):
                            yield l, "ff2", 4 * (g - 1) + i, GF, \
                                [(0, 2 * P, cols(a["w_ffn2"], l, 2 * P * i, 2 * P, GF * (g - 1), GF))], True

        slots = list(plan())
        where, counts = {}, [0] * NRAW
        order = []
        for n, (l, name, i, kn, pieces, split_) in enumerate(slots):
            counts[n % NRAW] += 16 * len(pieces)
            where[l, name, i] = (n, counts[n % NRAW], len(order))
            if split_:
                order.append((l, name, i))

        def slot_view(t, s, l, name, i):
            kn, pieces = slots[where[l, name, i][0]][3:5]
            n = sum(p[1] for p in pieces)
            return t[:, s, 0:kn * n].rearrange("p (k n) -> p k n", k=kn)

        def raw_weights(eng, l, name, i):
            n, count, _ = where[l, name, i]
            eng.wait_ge(w_full[n % NRAW], count)
            return slot_view(wring, n % NRAW, l, name, i)

        def weights(pe, l, name, i=0):
            pe.wait_ge(*pool_done.at("wlo", l, name, i))
            s = where[l, name, i][2] % NSPL
            return slot_view(wh, s, l, name, i), slot_view(wl, s, l, name, i)

        def slot_read(l, name, i, *key):
            book["last", l, name, i] = key


        @block.tensor
        def _(pe):
            turn["n"] = 0
            mm, tr = nc.tensor.matmul, nc.tensor.transpose

            def project(key, w, ntok, rhs=None, kn=KC, m0=0, ready=None, ps=None, done=True):
                (ah, al), (rh, rl) = w, rhs or (hh, hl)
                ps = take(pe, *key)
                for t0, t1 in ((0, LAT), (LAT, TOK))[:1 if ntok == LAT else 2]:
                    for k in range(kn):
                        if ready and t0 == 0:
                            pe.wait_ge(*ready(k))
                        ahk, alk = ah[:, k, m0:m0 + P], al[:, k, m0:m0 + P]
                        mm(ps[:, t0:t1], ahk, rh[:, k, t0:t1], start=(k == 0), stop=False)
                        mm(ps[:, t0:t1], ahk, rl[:, k, t0:t1], start=False, stop=False)
                        last = mm(ps[:, t0:t1], alk, rh[:, k, t0:t1], start=False, stop=(k == kn - 1))
                last.then_inc(*filled(*key))

            def modulation(l, cb):
                ps = take(pe, "mod", l, cb)
                for kk in range(4):
                    w = raw_weights(pe, l, "mod", 4 * cb + kk)
                    for j in range(2):
                        last = mm(ps[0:2, 0:512], ccol[:, :, 2 * kk + j], w[:, j, :],
                                  start=(kk + j == 0), stop=(kk == 3 and j == 1))
                    if kk < 3:
                        last.then_inc(*pe_done.mark("mod", l, cb, kk))
                last.then_inc(*filled("mod", l, cb))

            def modulation_columns(l, cb):
                pe.wait_ge(*read("mod", l, cb))
                ps = take(pe, "modT", l, cb)
                for m in range(4):
                    last = tr(ps[:, 2 * m:2 * m + 2], mrow[:, m * P:m * P + P], ident[0:2, 0:2])
                last.then_inc(*filled("modT", l, cb))

            def b_project(l, x):
                name, m = ("qb", "kb", "vb")[x // 4], x % 4
                key = (name if x < 8 else "vbT", l, m)
                project(key, weights(pe, l, name, m), TOK if l == 0 or x >= 4 else LAT)
                slot_read(l, name, m, *key)
                if x >= 9:
                    turn_values(("vb", l, m - 1), vraw[:, (m - 1) % 2, :], read("vbT", l, m - 1), vB)

            def turn_values(key, src, i, into):
                pe.wait_ge(*i)
                ps = take(pe, *key)
                for t in range(TT):
                    last = tr(ps[:, t * P:t * P + P], src[:, t * P:t * P + P], ident)
                last.then_inc(*filled(*key))

            def attention(l, br):
                q, k, v = (qk, qk, va) if br == "A" else (qB, kB, vB)
                work = att_items(l)
                for i in range(len(work) + 4):
                    if i < len(work):
                        h, t = work[i]
                        if i == 0:
                            pe.wait_ge(*(dve_done.at("rope", l, 5) if br == "A" else read("kb", l, 3)))
                            pe.wait_ge(*(read("va", l) if br == "A" else read("vb", l, 3)))
                        lo = HD * (h % 2)
                        kc = 4 + h // 4 if br == "A" else h // 2
                        qs = q[lo:lo + HD, h // 2, t * P:t * P + P]
                        ps = take(pe, "S", br, l, i)
                        if t < LT:
                            mm(ps[:, 0:LAT], qs, k[lo:lo + HD, kc, 0:LAT], start=True, stop=True)
                            last = mm(ps[:, LAT:TOK], qs, k[lo:lo + HD, kc, LAT:TOK], start=True, stop=True)
                        else:
                            last = mm(ps[:, 0:CTX], qs, k[lo:lo + HD, kc, LAT:TOK], start=True, stop=True)
                        last.then_inc(*filled("S", br, l, i))
                    if i >= 2:
                        ps = take(pe, "T", br, l, i - 2)
                        if i >= 4:
                            h, t = work[i - 4]
                            b0 = 0 if t < LT else LT
                            c0 = HD * (h // 4 if br == "A" else h)
                            pe.wait_ge(*read("T", br, l, i - 4))
                            for b in range(b0, TT):
                                last = mm(ps[0:HD, TOK:TOK + P], v[:, b, c0:c0 + HD], probT[:, (i - 4) % 3, b - b0, :],
                                          start=(b == b0), stop=(b == TT - 1))
                        if i - 2 < len(work):
                            nk = TT if work[i - 2][1] < LT else TT - LT
                            pe.wait_ge(*dve_done.at("prob", br, l, i - 2))
                            for b in range(nk):
                                last = tr(ps[:, b * P:b * P + P], prob[:, i % 2, b * P:b * P + P], ident)
                        last.then_inc(*filled("T", br, l, i - 2))

            def norm(l, which, ntok):
                ps = take(pe, "ss", l, which)
                for k in range(KC):
                    pe.wait_ge(*act_done.at("sq", l, which, k))
                    for t0, t1 in ((0, LAT), (LAT, TOK))[:1 if ntok == LAT else 2]:
                        last = mm(ps[:, t0:t1], ones, sq_n[:, k % 2, t0:t1], start=(k == 0), stop=(k == KC - 1))
                    if k < KC - 1:
                        last.then_inc(*pe_done.mark("ss", l, which, k))
                last.then_inc(*filled("ss", l, which))

            pe.wait_ge(*consts_in.at())
            for l in range(DEPTH):
                if l == 0:
                    for t in range(TT):
                        pe.wait_ge(*x_in[t].at())
                        ps = take(pe, "x", t)
                        for k in range(KC):
                            last = tr(ps[:, k * P:k * P + P], r(S0 + 1024 * t, 1024)[:, k * P:k * P + P], ident)
                        last.then_inc(*filled("x", t))
                if l == 0:
                    def params(ll):
                        pe.wait_ge(*params_in.at(ll))
                        ps = take(pe, "params", ll)
                        tr(ps[:, 0:P], prow[:, :], ident).then_inc(*filled("params", ll))

                    params(0)
                    pe.wait_ge(*act_done.at("ccol"))
                    for cb in range(4):
                        modulation(0, cb)
                        modulation_columns(0, cb)
                    params(1)
                norm(l, "mix", TOK)
                for p in range(15):
                    if p < 12:
                        j = c_order[p]
                        project(("c", l, j), weights(pe, l, "c", j), TOK,
                                ready=(lambda k: dve_done.at("h", l, "mix", k)) if p == 0 else None)
                        slot_read(l, "c", j, "c", l, j)
                    if p == 1:
                        project(("baT", l), weights(pe, l, "ba"), TOK)
                        slot_read(l, "ba", 0, "baT", l)
                    if p == 2:
                        pe.wait_ge(*read("baT", l))
                        ps = take(pe, "ba", l)
                        for t in range(TT):
                            last = tr(ps[:, 16 * t:16 * t + 16], baT[0:16, t * P:t * P + P], ident[0:16, 0:16])
                        last.then_inc(*filled("ba", l))
                    if p == 4:
                        pe.wait_ge(*dve_done.at("g", l))
                        ps = take(pe, "gc", l)
                        for t in range(TT):
                            b = 32 * t
                            mm(ps[:, b:b + 4], cst[:, C_UI:C_UI + P], gt[:, t, 0:4], start=True, stop=True)
                            mm(ps[:, b + 4:b + 8], cst[:, C_LI:C_LI + P], gt[:, t, 4:8], start=True, stop=True)
                            mm(ps[:, b + 8:b + 16], blk, gt[:, t, :], start=True, stop=True)
                            for c in range(2):
                                last = mm(ps[:, b + 16 + 8 * c:b + 24 + 8 * c],
                                          blk[:, 64 * c:64 * c + 1].to_broadcast([P, P]), gt[:, t, :],
                                          start=True, stop=True)
                        last.then_inc(*filled("gc", l))
                    if p >= 3 and c_order[p - 3] < 8:
                        j = c_order[p - 3]
                        pe.wait_ge(*act_done.at("csq", l, j))
                        ps = take(pe, "css", l, j)
                        for t0, t1 in ((0, LAT), (LAT, TOK)):
                            last = mm(ps[:, t0:t1], ones, csq[:, j % 2, t0:t1], start=True, stop=True)
                        last.then_inc(*filled("css", l, j))
                    if 5 <= p < 9:
                        turn_values(("ktok", l, p - 5), kT[:, p - 5, :], dve_done.at("l2", l, p - 1), ktok)
                    if 6 <= p < 10:
                        turn_values(("vtok", l, p - 6), vT4[:, p - 6, :], act_done.at("silu", l, p + 2), vtok)
                pe.wait_ge(*read("ktok", l, 3))
                for s in range(TT):
                    for d in range(2):
                        t = tiles[d][s]
                        pe.wait_ge(*pool_done.at("R", l, s, d))
                        ps = take(pe, "bc", l, s, d)
                        mm(ps[:, 0:512], ones, flat(rbuf[d]), start=True, stop=True).then_inc(*filled("bc", l, s, d))
                        ps = take(pe, "G", l, s, d)
                        for h in range(C_H):
                            kk = kT[:, h, t * P:t * P + P]
                            mm(ps[:, h * P:h * P + P], kk, kk, start=True, stop=True)
                            last = mm(ps[:, 512 + h * P:512 + h * P + P], kk, qT[:, h, t * P:t * P + P],
                                      start=True, stop=True)
                        last.then_inc(*filled("G", l, s, d))
                    for d in range(2):
                        pe.wait_ge(*dve_done.at("A", l, s, d))
                        ps = take(pe, "AT", l, s, d)
                        for h in range(C_H):
                            last = tr(ps[:, h * P:h * P + P], pbuf[d][:, h, :], ident)
                        last.then_inc(*filled("AT", l, s, d))
                    if l == 0 and s == 0:
                        filler, turned = iter(later_mods), None
                    for i in range(5):
                        for d in range(2):
                            src, srcT, dst, dstT = power(d, i)
                            pe.wait_ge(*(read("pw", l, s, d, i - 1) if i else read("AT", l, s, d)))
                            ps = take(pe, "pw", l, s, d, i)
                            for h in range(C_H):
                                last = mm(ps[:, h * P:h * P + P], srcT[:, h, :], src[:, h, :], start=True, stop=True)
                                if i < 4:
                                    last = mm(ps[:, 512 + h * P:512 + h * P + P], src[:, h, :], srcT[:, h, :],
                                              start=True, stop=True)
                            last.then_inc(*filled("pw", l, s, d, i))
                        for d in range(2):
                            src, srcT, dst, dstT = power(d, i)
                            pe.wait_ge(*read("pw", l, s, d, i))
                            pe.wait_ge(*(read("X", l, s, d, i - 1) if i else read("AT", l, s, d)))
                            ps = take(pe, "X", l, s, d, i)
                            for h in range(C_H):
                                last = mm(ps[:, h * P:h * P + P], dst[:, h, :], xbuf[d][:, h, :], start=True, stop=True)
                            last.then_inc(*filled("X", l, s, d, i))
                        if l == 0:
                            if turned:
                                modulation_columns(*turned)
                            turned = next(filler, None)
                            if turned:
                                modulation(*turned)
                    for d in range(2):
                        pe.wait_ge(*pool_done.at("kbe", l, s, d))
                        pe.wait_ge(*read("X", l, s, d, 4))
                        ps = take(pe, "kcd", l, s, d)
                        for h in range(C_H):
                            last = mm(ps[:, h * P:h * P + P], wbuf[d][:, h, :], xbuf[d][:, h, :], start=True, stop=True)
                        last.then_inc(*filled("kcd", l, s, d))
                    for c in range(2):
                        for d in range(2):
                            t, cc, n = tiles[d][s], (c if d == 0 else 1 - c), 2 * s + c
                            lo, hi = 64 * cc, 64 * cc + 64
                            S = state[:, n % 2, :, :]
                            if c == 0:
                                pe.wait_ge(*read("kcd", l, s, d))
                                pe.wait_ge(*pool_done.at("vb", l, s, d))
                            pe.wait_ge(*(read("so", l, n - 1, d) if n else dve_done.at("S0", l)))
                            ps = take(pe, "vn", l, n, d)
                            for h in range(C_H):
                                o = ps[0:64, h * P:h * P + P]
                                mm(o, ebuf[d][:, h, lo:hi], S[:, 4 * d + h, :], start=True, stop=False)
                                last = mm(o, xbuf[d][lo:hi, h, lo:hi], vbbuf[d][lo:hi, h, :], start=False, stop=True)
                            last.then_inc(*filled("vn", l, n, d))
                        for d in range(2):
                            t, cc, n = tiles[d][s], (c if d == 0 else 1 - c), 2 * s + c
                            lo, hi = 64 * cc, 64 * cc + 64
                            S = state[:, n % 2, :, :]
                            pe.wait_ge(*read("vn", l, n, d))
                            pe.wait_ge(*pool_done.at("kd", l, s, d))
                            pe.wait_ge(*pool_done.at("AQ", l, s, d))
                            ps = take(pe, "so", l, n, d)
                            for h in range(C_H):
                                vn = tbuf[d][lo:hi, h, :]
                                last = mm(ps[:, h * P:h * P + P], pbuf[d][lo:hi, h, :], vn, start=True, stop=True)
                            if want_out(l, t):
                                for h in range(C_H):
                                    o = ps[0:64, 512 + h * P:512 + h * P + P]
                                    mm(o, qdbuf[d][:, h, lo:hi], S[:, 4 * d + h, :], start=True, stop=False)
                                    last = mm(o, aqbuf[d][lo:hi, h, lo:hi], tbuf[d][lo:hi, h, :], start=False, stop=True)
                            last.then_inc(*filled("so", l, n, d))
                for m in range(4):
                    project(("z", l, m), weights(pe, l, "z", m), TOK if l == 0 else LAT)
                    slot_read(l, "z", m, "z", l, m)
                for t in range(TT if l == 0 else LT):
                    pe.wait_ge(*dve_done.at("onrm", l))
                    ps = take(pe, "oT", l, t)
                    for h in range(C_H):
                        last = tr(ps[:, h * P:h * P + P], Otok[:, t, h * P:h * P + P], ident)
                    last.then_inc(*filled("oT", l, t))
                pe.wait_ge(*read("oT", l, (TT if l == 0 else LT) - 1))
                for m in range(4):
                    project(("qk", l, m), weights(pe, l, "qa", m), TOK if l == 0 else LAT)
                    slot_read(l, "qa", m, "qk", l, m)
                for m in range(2):
                    project(("qk", l, 4 + m), weights(pe, l, "ka", m), TOK)
                    slot_read(l, "ka", m, "qk", l, 4 + m)
                project(("vaT", l), weights(pe, l, "va"), TOK)
                slot_read(l, "va", 0, "vaT", l)
                turn_values(("va", l), vraw[:, 0, :], read("vaT", l), va)
                for j in range(6):
                    n = TOK if (l == 0 or j >= 4) else LAT
                    pe.wait_ge(*act_done.at("asq", l, j))
                    ps = take(pe, "ass", l, j)
                    for t0, t1 in ((0, LAT), (LAT, TOK))[:1 if n == LAT else 2]:
                        last = mm(ps[:, t0:t1], blk, asq[:, t0:t1], start=True, stop=True)
                    last.then_inc(*filled("ass", l, j))
                    b_project(l, 2 * j)
                    pe.wait_ge(*dve_done.at("qkn", l, j))
                    ps = take(pe, "rot", l, j)
                    mm(ps[:, 0:LAT], rot, qk[:, j, 0:LAT], start=True, stop=True).then_inc(*filled("rot", l, j))
                    b_project(l, 2 * j + 1)
                turn_values(("vb", l, 3), vraw[:, 1, :], read("vbT", l, 3), vB)
                attention(l, "A")
                attention(l, "B")
                nt = TOK if l == 0 else LAT
                for x in range(24):
                    project(("gate", l, x), weights(pe, l, "gate", x), nt)
                    slot_read(l, "gate", x, "gate", l, x)
                    w = raw_weights(pe, l, "br", x)
                    ps = take(pe, "br", l, x)
                    for t0, t1 in ((0, LAT), (LAT, TOK))[:1 if nt == LAT else 2]:
                        for k in range(4):
                            last = mm(ps[:, t0:t1], w[:, k, :], (oA, oB, oC)[x % 3][:, k, t0:t1],
                                      start=(k == 0), stop=(k == 3))
                    last.then_inc(*filled("br", l, x))
                    slot_read(l, "br", x, "br", l, x)
                for i in range(8):
                    project(("out", l, i), weights(pe, l, "out", i), nt,
                            ready=(lambda k: dve_done.at("mlo", l, k)) if i == 0 else None)
                    slot_read(l, "out", i, "out", l, i)
                norm(l, "ffn", nt)
                for g in range(NG + 1):
                    if g < NG:
                        for i in range(GF * g, GF * g + GF):
                            project(("ff1", l, i), weights(pe, l, "ff1", i), nt,
                                    ready=(lambda k: dve_done.at("h", l, "ffn", k)) if i == 0 else None)
                            slot_read(l, "ff1", i, "ff1", l, i)
                    if g:
                        b = (g - 1) % 2
                        pe.wait_ge(*dve_done.at("flo", l, GF * g - 1))
                        for i in range(4):
                            w = weights(pe, l, "ff2", 4 * (g - 1) + i)
                            for u in range(2):
                                project(("ff2", l, g - 1, 2 * i + u), w, nt, rhs=(fh[:, b, :, :], fl[:, b, :, :]),
                                        kn=GF, m0=u * P)
                            slot_read(l, "ff2", 4 * (g - 1) + i, "ff2", l, g - 1, 2 * i + 1)
            pe.wait_ge(*params_in.at(DEPTH))
            ps = take(pe, "params", DEPTH)
            tr(ps[:, 0:KC], prow[0:KC, :], ident[0:KC, 0:KC]).then_inc(*filled("params", DEPTH))
            norm(DEPTH, "fin", LAT)
            pe.wait_ge(*act_done.at("fin", KC - 1))
            for t in range(LT):
                ps = take(pe, "fin", t)
                for k in range(KC):
                    last = tr(ps[:, k * P:k * P + P], fin_T[:, k, t * P:t * P + P], ident)
                last.then_inc(*filled("fin", t))

        def spans(n):
            return ((0, LAT, 0), (LAT, TOK, 1))[:1 if n == LAT else 2]

        def attention(eng, l, br):
            work = att_items(l)
            o = oA if br == "A" else oB
            for i in range(len(work) + 4):
                if i < len(work):
                    n = TOK if work[i][1] < LT else CTX
                    eng.wait_ge(*dve_done.at("nm", br, l, i))
                    if i >= 2:
                        eng.wait_ge(*full("T", br, l, i - 2))
                    nc.scalar.activation(prob[:, i % 2, 0:n], pair("S", br, l, i)[:, 0:n], ACT.Exp, scale=SCALE,
                                         bias=stat[:, i % 2, 1:2], accum_out=stat[:, i % 2, 2:3])\
                        .then_inc(*free("S", br, l, i))
                if i >= 2:
                    j = i - 2
                    eng.wait_ge(*full("T", br, l, j))
                    if i >= 4:
                        h, t = work[i - 4]
                        lo = HD * (h % 2)
                        nc.scalar.activation(o[lo:lo + HD, h // 2, t * P:t * P + P],
                                             pair("T", br, l, j)[0:HD, TOK:TOK + P], ACT.Copy)\
                            .then_inc(*free("T", br, l, j, by=1 if j < len(work) else 2))
                    if j < len(work):
                        nb = TT if work[j][1] < LT else TT - LT
                        nc.scalar.activation(probT[:, j % 3, 0:nb, :],
                                             pair("T", br, l, j)[:, 0:nb * P].rearrange("p (b n) -> p b n", b=nb),
                                             ACT.Copy).then_inc(*free("T", br, l, j, by=1 if i >= 4 else 2))

        @block.sync
        def _(sp):
            sp.dma_start(cst[:, :], a["consts"]).then_inc(*consts_in.mark(by=16))
            for t in range(TT):
                src = a["x"][0, t * P:t * P + P, :] if t < LT else a["ctx"][0, (t - LT) * P:(t - LT) * P + P, :]
                sp.dma_start(r(S0 + 1024 * t, 1024), src).then_inc(*x_in[t].mark(by=16))
            for n, (l, name, i, kn, pieces, _) in enumerate(slots):
                if n >= NRAW:
                    before = slots[n - NRAW][:3]
                    if slots[n - NRAW][5]:
                        sp.wait_ge(*pool_done.at("wlo", *before))
                    elif before[1] == "mod":
                        cb, kk = divmod(before[2], 4)
                        sp.wait_ge(*(pe_done.at("mod", before[0], cb, kk) if kk < 3 else full("mod", before[0], cb)))
                    else:
                        sp.wait_ge(*full(*book.get(("last",) + before, ("x", 0))))
                for c0, cn, src in pieces:
                    sp.dma_start(slot_view(wring, n % NRAW, l, name, i)[:, :, c0:c0 + cn], src)\
                        .then_inc(w_full[n % NRAW], 16)
            for t in range(LT):
                sp.wait_ge(*read("fin", t))
                sp.dma_start(out[0, t * P:t * P + P, :], r(16384 + 1024 * t, 1024)).then_inc(*out_done.mark(t, by=16))
            sp.wait_ge(*out_done.at(LT - 1))

        @block.scalar
        def _(act):
            A = nc.scalar.activation

            def norm(l, which, ntok):
                for k in range(KC):
                    if l == 0 and which == "mix":
                        if k == 0:
                            act.wait_ge(*read("x", TT - 1))
                    else:
                        act.wait_ge(*(read("out", l, k) if which == "ffn" else read("ff2", l - 1, NG - 1, k)))
                    if k >= 2:
                        act.wait_ge(*pe_done.at("ss", l, which, k - 2))
                    A(sq_n[:, k % 2, 0:ntok], xT[:, k, 0:ntok], ACT.Square).then_inc(*act_done.mark("sq", l, which, k))
                act.wait_ge(*full("ss", l, which))
                act.wait_ge(*dve_done.at("eps"))
                A(rs_n[:, 0:ntok], pair("ss", l, which)[:, 0:ntok], ACT.Sqrt, scale=1.0 / D, bias=eps[:, 0:1])\
                    .then_inc(*free("ss", l, which))
                if which == "ffn" or l == 0:
                    act.wait_ge(*dve_done.at("gain", l, int(which == "ffn")))
                for k in range(KC):
                    if which == "fin":
                        act.wait_ge(*pool_done.at("hx", l, which, k))
                        A(fin_T[:, k, 0:ntok], ht[:, k % 3, 0:ntok], ACT.Copy, scale=pcols[:, 0, k:k + 1])\
                            .then_inc(*act_done.mark("fin", k))
                    else:
                        act.wait_ge(*dve_done.at("aff", l, which, k))
                        A(hh[:, k, 0:ntok], ht[:, k % 3, 0:ntok], ACT.Copy).then_inc(*act_done.mark("hhi", l, which, k))

            sent = [0]

            def high(l, name, i=0, ahead=2, cap=None):
                last = where[l, name, i][2] + ahead
                last = min(last, len(order) - 1 if cap is None else where[cap][2])
                while sent[0] <= last:
                    n, slot = sent[0], order[sent[0]]
                    w = raw_weights(act, *slot)
                    if n >= NSPL:
                        act.wait_ge(*full(*book.get(("last",) + order[n - NSPL], ("x", 0))))
                    A(slot_view(wh, n % NSPL, *slot), w, ACT.Copy).then_inc(*act_done.mark("whi", *slot))
                    sent[0] += 1

            act.wait_ge(*cond_in.at())
            A(ccol[:, :, :], craw_c[:, :, :], ACT.Silu).then_inc(*act_done.mark("ccol"))
            for l in range(DEPTH):
                nt = TOK if l == 0 else LAT
                if l == 0:
                    for t in range(TT):
                        act.wait_ge(*full("x", t))
                        A(xT[:, :, t * P:t * P + P], pair("x", t)[:, :].rearrange("p (k n) -> p k n", k=KC), ACT.Copy)\
                            .then_inc(*free("x", t))
                high(l, "c", c_order[0], ahead=1)
                norm(l, "mix", TOK)
                def decays(l):
                    act.wait_ge(*full("ba", l))
                    A(bg[:, :, 0:8], pair("ba", l)[:, 0:96].rearrange("p (t n) -> p t n", t=TT)[:, :, 0:8], ACT.Sigmoid)\
                        .then_inc(*free("ba", l, by=1))
                    act.wait_ge(*dve_done.at("absa", l))
                    A(gtmp[:, :, :], gtmp[:, :, :], ACT.Exp, scale=-1.0).then_inc(*act_done.mark("expa", l))
                    act.wait_ge(*dve_done.at("1+e", l))
                    A(gtmp[:, :, :], gtmp[:, :, :], ACT.Ln).then_inc(*act_done.mark("lna", l))
                    act.wait_ge(*abc_in.at(l))
                    A(abc[:, 0, :], abc[:, 0, :], ACT.Exp).then_inc(*act_done.mark("expA", l))

                act.wait_ge(*dve_done.at("craw0", l))
                for p in range(15):
                    if p < 12:
                        j = c_order[p]
                        high(l, "c", j, cap=(l, "c", c_order[11]))
                        act.wait_ge(*full("c", l, j))
                        if p >= 2:
                            act.wait_ge(*dve_done.at("conv", l, c_order[p - 2]))
                        ps = pair("c", l, j)
                        A(craw[:, j % 2, 2:2 + LAT], ps[:, 0:LAT], ACT.Copy).then_inc(*free("c", l, j, by=1))
                        A(craw[:, j % 2, LAT + 6:TOK + 6], ps[:, LAT:TOK], ACT.Copy).then_inc(*free("c", l, j, by=1))
                    if 1 <= p < 13:
                        j = c_order[p - 1]
                        act.wait_ge(*dve_done.at("conv", l, j))
                        o = (qT, kT, vT4)[j // 4][:, j % 4, :]
                        A(o[:, 0:LAT], cacc[:, j % 2, 0:LAT], ACT.Silu).then_inc(*act_done.mark("silu0", l, j))
                        A(o[:, LAT:TOK], cacc[:, j % 2, LAT + 4:TOK + 4], ACT.Silu).then_inc(*act_done.mark("silu", l, j))
                    if p == 1:
                        act.wait_ge(*full("baT", l))
                        A(baT[0:16, :], pair("baT", l)[0:16, 0:TOK], ACT.Copy).then_inc(*free("baT", l))
                    if p == 2:
                        decays(l)
                    if 2 <= p < 14 and c_order[p - 2] < 8:
                        j = c_order[p - 2]
                        act.wait_ge(*act_done.at("silu", l, j))
                        if j not in (0, 1, 4, 5):
                            act.wait_ge(*full("css", l, j - 2))
                        A(csq[:, j % 2, :], (qT, kT)[j // 4][:, j % 4, :], ACT.Square).then_inc(*act_done.mark("csq", l, j))
                    if p >= 3 and c_order[p - 3] < 8:
                        j = c_order[p - 3]
                        act.wait_ge(*full("css", l, j))
                        if j not in (4, 5):
                            act.wait_ge(*dve_done.at("l2", l, c_order[c_order.index(j) - 2] if j > 5 or j in (2, 3) else 6 + j))
                        A(crr[:, j % 2, :], pair("css", l, j)[:, 0:TOK], ACT.Sqrt, bias=eps[:, 0:1])\
                            .then_inc(*free("css", l, j))
                act.wait_ge(*read("gc", l))
                A(gex[:, :, 0, :], gcs[:, :, 0:8], ACT.Exp).then_inc(*act_done.mark("gex0", l))
                A(gex[:, :, 2:4, :].rearrange("p t a b -> p t (a b)"), gcs[:, :, 16:32], ACT.Exp)\
                    .then_inc(*act_done.mark("gex2", l))
                act.wait_ge(*dve_done.at("gdiff", l))
                A(gex[:, :, 1, :], gtmp[:, :, :], ACT.Exp).then_inc(*act_done.mark("gex1", l))
                for s in range(TT):
                    for d in range(2):
                        act.wait_ge(*full("bc", l, s, d))
                        if s:
                            act.wait_ge(*full("vn", l, 2 * s - 1, d))
                        A(flat(ebuf[d]), pair("bc", l, s, d)[:, 0:512], ACT.Exp).then_inc(*free("bc", l, s, d, by=1))
                        act.wait_ge(*read("bc", l, s, d))
                        A(flat(wbuf[d]), flat(wbuf[d]), ACT.Abs).then_inc(*act_done.mark("abs", l, s, d))
                        act.wait_ge(*act_done.at("abs", l, s, d))
                        A(flat(wbuf[d]), flat(wbuf[d]), ACT.Exp, scale=-1.0).then_inc(*act_done.mark("W", l, s, d))
                    for i in range(5):
                        for d in range(2):
                            act.wait_ge(*full("pw", l, s, d, i))
                            if i == 0:
                                act.wait_ge(*dve_done.at("A", l, s, d))
                            A(flat(power(d, i)[2]), pair("pw", l, s, d, i)[:, 0:512], ACT.Copy)\
                                .then_inc(*free("pw", l, s, d, i, by=1 if i < 4 else 2))
                    for d in range(2):
                        act.wait_ge(*full("kcd", l, s, d))
                        act.wait_ge(*pool_done.at("qd", l, s, d))
                        A(flat(ebuf[d]), pair("kcd", l, s, d)[:, 0:512], ACT.Copy, scale=-1.0)\
                            .then_inc(*free("kcd", l, s, d))
                    for c in range(2):
                        for d in range(2):
                            n, lo = 2 * s + c, 64 * (c if d == 0 else 1 - c)
                            act.wait_ge(*full("vn", l, n, d))
                            A(flat(tbuf[d])[lo:lo + 64, :], pair("vn", l, n, d)[0:64, 0:512], ACT.Copy)\
                                .then_inc(*free("vn", l, n, d))
                for m in range(4):
                    high(l, "z", m)
                    act.wait_ge(*full("z", l, m))
                    A(siluz[:, m, 0:nt], pair("z", l, m)[:, 0:nt], ACT.Silu).then_inc(*free("z", l, m))
                act.wait_ge(*dve_done.at("oss", l))
                A(small[:, 0:24], small[:, 0:24], ACT.Sqrt, scale=1.0 / P, bias=eps[:, 0:1])\
                    .then_inc(*act_done.mark("ors", l))
                for j in range(6):
                    n = TOK if j >= 4 else nt
                    high(l, *(("qa", j) if j < 4 else ("ka", j - 4)))
                    act.wait_ge(*full("qk", l, j))
                    A(qk[:, j, 0:n], pair("qk", l, j)[:, 0:n], ACT.Copy).then_inc(*free("qk", l, j))
                high(l, "va")
                act.wait_ge(*full("vaT", l))
                A(vraw[:, 0, :], pair("vaT", l)[:, 0:TOK], ACT.Copy).then_inc(*free("vaT", l))
                act.wait_ge(*full("va", l))
                A(flat(va), pair("va", l)[:, 0:TOK], ACT.Copy).then_inc(*free("va", l))
                act.wait_ge(*read("va", l))
                for j in range(6):
                    n = TOK if j >= 4 else nt
                    if j:
                        act.wait_ge(*dve_done.at("qkn", l, j - 1))
                    A(asq[:, 0:n], qk[:, j, 0:n], ACT.Square).then_inc(*act_done.mark("asq", l, j))
                    act.wait_ge(*full("ass", l, j))
                    A(arr[:, 0:n], pair("ass", l, j)[:, 0:n], ACT.Sqrt, scale=1.0 / HD, bias=eps[:, 0:1])\
                        .then_inc(*free("ass", l, j))
                    for x in (2 * j, 2 * j + 1):
                        name, m = ("qb", "kb", "vb")[x // 4], x % 4
                        n = TOK if x >= 4 else nt
                        high(l, name, m)
                        if x < 8:
                            act.wait_ge(*full(name, l, m))
                            A((qB, kB)[x // 4][:, m, 0:n], pair(name, l, m)[:, 0:n], ACT.Copy).then_inc(*free(name, l, m))
                        else:
                            act.wait_ge(*full("vbT", l, m))
                            if m >= 2:
                                act.wait_ge(*full("vb", l, m - 2))
                            A(vraw[:, m % 2, :], pair("vbT", l, m)[:, 0:TOK], ACT.Copy).then_inc(*free("vbT", l, m))
                attention(act, l, "A")
                attention(act, l, "B")
                for x in range(24):
                    high(l, "gate", x)
                    act.wait_ge(*full("gate", l, x))
                    if x >= 2:
                        act.wait_ge(*dve_done.at("merge", l, x - 2))
                    A(gsig[:, x % 2, 0:nt], pair("gate", l, x)[:, 0:nt], ACT.Sigmoid).then_inc(*free("gate", l, x))
                for k in range(KC):
                    act.wait_ge(*dve_done.at("merge", l, 23))
                    A(hh[:, k, 0:nt], mT[:, k, 0:nt], ACT.Copy).then_inc(*act_done.mark("mhi", l, k))
                for i in range(8):
                    high(l, "out", i)
                norm(l, "ffn", nt)
                for j in range(FF // P):
                    high(l, "ff1", j)
                    act.wait_ge(*full("ff1", l, j))
                    if j >= 2:
                        act.wait_ge(*dve_done.at("flo", l, j - 2))
                    else:
                        act.wait_ge(*dve_done.at("h", l, "ffn", KC - 1))
                    f = ftmp[:, j % 2, 0:nt]
                    A(f, pair("ff1", l, j)[:, 0:nt], ACT.Relu).then_inc(*free("ff1", l, j))
                    act.wait_ge(*dve_done.at("fsq", l, j))
                    A(fh[:, j // GF % 2, j % GF, 0:nt], f, ACT.Copy).then_inc(*act_done.mark("fhi", l, j))
                    if j % GF == GF - 1 and j >= GF:
                        for i in range(4):
                            high(l, "ff2", j + 1 - 2 * GF + i)
                for i in range(4):
                    high(l, "ff2", FF // P - GF + i)
            norm(DEPTH, "fin", LAT)
            for t in range(LT):
                act.wait_ge(*full("fin", t))
                A(r(16384 + 1024 * t, 1024), pair("fin", t)[:, :], ACT.Copy).then_inc(*free("fin", t))

        @block.vector
        def _(dve):
            V = nc.vector

            def norm(l, which, ntok):
                dve.wait_ge(*read("ss", l, which))
                V.reciprocal(rs_n[:, 0:ntok], rs_n[:, 0:ntok]).then_inc(*dve_done.mark("rs", l, which))
                dve.wait_ge(*dve_done.at("rs", l, which))
                if which == "fin":
                    return
                w = int(which == "ffn")
                for k in range(KC + 1):
                    if k < KC:
                        dve.wait_ge(*pool_done.at("hx", l, which, k))
                        dve.wait_ge(*dve_done.at("gain", l, w))
                        sp_ = spans(ntok)
                        for t0, t1, c in sp_:
                            V.tensor_scalar(ht[:, k % 3, t0:t1], ht[:, k % 3, t0:t1], gains[:, l, w, k, c:c + 1],
                                            modcs[:, l, 24 * w + k, c:c + 1], ALU.mult, ALU.add)\
                                .then_inc(*dve_done.mark("aff", l, which, k))
                    if k:
                        dve.wait_ge(*act_done.at("hhi", l, which, k - 1))
                        V.tensor_tensor(hl[:, k - 1, 0:ntok], ht[:, (k - 1) % 3, 0:ntok],
                                        hh[:, k - 1, 0:ntok].bitcast(F32), ALU.subtract)\
                            .then_inc(*dve_done.mark("h", l, which, k - 1))

            def attention(l, br):
                work = att_items(l)
                o = oA if br == "A" else oB
                for i in range(len(work) + 1):
                    if i < len(work):
                        h, t = work[i]
                        n = TOK if t < LT else CTX
                        dve.wait_ge(*full("S", br, l, i))
                        ps = pair("S", br, l, i)
                        if br == "B" and t < LT:
                            dve.wait_ge(*pool_done.at("E", l, h))
                            V.tensor_tensor(ps[:, 0:LAT], ps[:, 0:LAT],
                                            ebias[:, h % 2, 6 - 2 * t + 0:14 - 2 * t, :].rearrange("p a b -> p (a b)"),
                                            ALU.add).then_inc(*dve_done.mark("bias", l, i))
                            dve.wait_ge(*dve_done.at("bias", l, i))
                        if i >= 2:
                            dve.wait_ge(*read("S", br, l, i - 2))
                        V.tensor_reduce(stat[:, i % 2, 0:1], ps[:, 0:n], AX.X, ALU.max, negate=True)\
                            .then_inc(*dve_done.mark("max", br, l, i))
                        dve.wait_ge(*dve_done.at("max", br, l, i))
                        V.tensor_scalar(stat[:, i % 2, 1:2], stat[:, i % 2, 0:1], SCALE, None, ALU.mult)\
                            .then_inc(*dve_done.mark("nm", br, l, i))
                    if 1 <= i <= len(work):
                        j = i - 1
                        n = TOK if work[j][1] < LT else CTX
                        dve.wait_ge(*read("S", br, l, j))
                        V.reciprocal(stat[:, j % 2, 3:4], stat[:, j % 2, 2:3]).then_inc(*dve_done.mark("rsum", br, l, j))
                        dve.wait_ge(*dve_done.at("rsum", br, l, j))
                        V.tensor_scalar(prob[:, j % 2, 0:n], prob[:, j % 2, 0:n], stat[:, j % 2, 3:4], None, ALU.mult)\
                            .then_inc(*dve_done.mark("prob", br, l, j))
            def modulation(l, cb):
                dve.wait_ge(*full("mod", l, cb))
                if (l, cb) != (0, 0):
                    dve.wait_ge(*full("modT", *((l, cb - 1) if cb else (0, 11))))
                V.tensor_copy(mrow[:, :], pair("mod", l, cb)[0:2, 0:512]).then_inc(*free("mod", l, cb))

            def modulation_columns(l, cb):
                dve.wait_ge(*full("modT", l, cb))
                V.tensor_tensor(modcs[:, l, 4 * cb:4 * cb + 4, :],
                                pair("modT", l, cb)[:, 0:8].rearrange("p (m c) -> p m c", m=4),
                                along(pcols[:, l, R_BMOD + 4 * cb:R_BMOD + 4 * cb + 4], 2), ALU.add)\
                    .then_inc(*free("modT", l, cb))

            def low(l, j):
                nt = TOK if l == 0 else LAT
                dve.wait_ge(*act_done.at("fhi", l, j))
                V.tensor_tensor(fl[:, j // GF % 2, j % GF, 0:nt], ftmp[:, j % 2, 0:nt],
                                fh[:, j // GF % 2, j % GF, 0:nt].bitcast(F32), ALU.subtract)\
                    .then_inc(*dve_done.mark("flo", l, j))

            def norm_gain(l, w):
                dve.wait_ge(*read("modT", l, 6 * w + 3))
                V.scalar_tensor_tensor(out=gains[:, l, w, :, :], in0=modcs[:, l, 24 * w + 8:24 * w + 16, :], scalar=1.0,
                                       in1=along(pcols[:, l, R_MIX + 8 * w:R_MIX + 8 * w + 8], 2),
                                       op0=ALU.add, op1=ALU.mult).then_inc(*dve_done.mark("gain", l, w))

            V.memset(eps[:, :], EPS).then_inc(*dve_done.mark("eps"))
            for l in range(DEPTH):
                nt = TOK if l == 0 else LAT
                pcol, modc = pcols[:, l, :], modcs[:, l, :, :]
                if l == 0:
                    def params(ll):
                        dve.wait_ge(*full("params", ll))
                        V.tensor_copy(pcols[:, ll, :], pair("params", ll)[:, 0:P]).then_inc(*free("params", ll))
                        dve.wait_ge(*read("params", ll))

                    params(0)
                    for cb in range(4):
                        modulation(0, cb)
                        modulation_columns(0, cb)
                    params(1)
                    norm_gain(0, 0)
                norm(l, "mix", TOK)
                W = TOK + 4

                def decays(l):
                    dve.wait_ge(*read_first("ba", l))
                    dve.wait_ge(*abc_in.at(l))
                    V.tensor_tensor(gt[:, :, :], pair("ba", l)[:, 0:96].rearrange("p (t n) -> p t n", t=TT)[:, :, 8:16],
                                    abc[:, 1, :].unsqueeze(1).to_broadcast([P, TT, 8]), ALU.add)\
                        .then_inc(*free("ba", l, by=1))
                    dve.wait_ge(*read("ba", l))
                    V.scalar_tensor_tensor(out=gtmp[:, :, :], in0=gt[:, :, :], scalar=-1.0, in1=gt[:, :, :],
                                           op0=ALU.mult, op1=ALU.max).then_inc(*dve_done.mark("absa", l))
                    dve.wait_ge(*act_done.at("expa", l))
                    V.tensor_scalar(gtmp[:, :, :], gtmp[:, :, :], 1.0, None, ALU.add).then_inc(*dve_done.mark("1+e", l))
                    dve.wait_ge(*act_done.at("lna", l))
                    V.scalar_tensor_tensor(out=gt[:, :, :], in0=gt[:, :, :], scalar=0.0, in1=gtmp[:, :, :],
                                           op0=ALU.max, op1=ALU.add).then_inc(*dve_done.mark("sp", l))
                    dve.wait_ge(*act_done.at("expA", l))
                    dve.wait_ge(*dve_done.at("sp", l))
                    V.scalar_tensor_tensor(out=gt[:, :, :], in0=gt[:, :, :], scalar=-1.0,
                                           in1=abc[:, 0, :].unsqueeze(1).to_broadcast([P, TT, 8]),
                                           op0=ALU.mult, op1=ALU.mult).then_inc(*dve_done.mark("g", l))
                    V.tensor_scalar(nbeta[:, :, :], bg[:, :, 0:8], -1.0, None, ALU.mult)\
                        .then_inc(*dve_done.mark("nbeta", l))

                dve.wait_ge(*spilled.at(l))
                dve.wait_ge(*dve_done.at("h", l, "mix", KC - 1))
                V.memset(craw[:, :, :], 0.0).then_inc(*dve_done.mark("craw0", l))
                for p in range(15):
                    if p < 12:
                        j = c_order[p]
                        dve.wait_ge(*read("c", l, j))
                        if p >= 2:
                            dve.wait_ge(*act_done.at("silu", l, c_order[p - 2]))
                        for q in range(CONV):
                            tap = pcol[:, R_CONV + 12 * q + j:R_CONV + 12 * q + j + 1]
                            if q == 0:
                                ins = V.tensor_scalar(cacc[:, j % 2, 0:W], craw[:, j % 2, 0:W], tap, None, ALU.mult)
                            else:
                                dve.wait_ge(*dve_done.at("tap", l, j, q - 1))
                                ins = V.scalar_tensor_tensor(out=cacc[:, j % 2, 0:W], in0=craw[:, j % 2, q:q + W],
                                                             scalar=tap, in1=cacc[:, j % 2, 0:W], op0=ALU.mult, op1=ALU.add)
                            ins.then_inc(*dve_done.mark(*(("tap", l, j, q) if q < CONV - 1 else ("conv", l, j))))
                    if p == 2:
                        decays(l)
                    if p == 5:
                        dve.wait_ge(*full("gc", l))
                        V.tensor_copy(gcs[:, :, :], pair("gc", l)[:, 0:32 * TT].rearrange("p (t n) -> p t n", t=TT))\
                            .then_inc(*free("gc", l))
                    if p >= 3 and c_order[p - 3] < 8:
                        j = c_order[p - 3]
                        x = (qT, kT)[j // 4][:, j % 4, :]
                        dve.wait_ge(*read("css", l, j))
                        V.reciprocal(crr[:, j % 2, :], crr[:, j % 2, :]).then_inc(*dve_done.mark("crr", l, j))
                        dve.wait_ge(*dve_done.at("crr", l, j))
                        V.scalar_tensor_tensor(out=x, in0=x, scalar=float(P) ** -0.5 if j < 4 else 1.0,
                                               in1=crr[:, j % 2, :], op0=ALU.mult, op1=ALU.mult)\
                            .then_inc(*dve_done.mark("l2", l, j))
                    for name, dst, m in (("ktok", ktok, p - 5), ("vtok", vtok, p - 6)):
                        if 0 <= m < 4:
                            dve.wait_ge(*full(name, l, m))
                            V.tensor_copy(dst[:, :, m * P:m * P + P],
                                          pair(name, l, m)[:, 0:TOK].rearrange("p (t n) -> p t n", t=TT))\
                                .then_inc(*free(name, l, m))
                dve.wait_ge(*read("gc", l))
                V.tensor_tensor(gtmp[:, :, :], gcs[:, :, 8:16], gcs[:, :, 0:8], ALU.subtract)\
                    .then_inc(*dve_done.mark("gdiff", l))
                dve.wait_ge(*act_done.at("gex0", l))
                V.tensor_tensor(gex[:, :, 0, :], gex[:, :, 0, :], bg[:, :, 0:8], ALU.mult)\
                    .then_inc(*dve_done.mark("gb", l))
                dve.wait_ge(*pad_out.at(l))
                V.memset(state[:, 0, :, :], 0.0).then_inc(*dve_done.mark("S0", l))
                seen = set()
                filler, turned = iter(later_mods), None
                for s in range(TT):
                    for d in range(2):
                        t = tiles[d][s]
                        dve.wait_ge(*read_first("bc", l, s, d))
                        if s:
                            dve.wait_ge(*full("kcd", l, s - 1, d))
                        V.tensor_tensor(wbuf[d], pair("bc", l, s, d)[:, 0:512].rearrange("p (h n) -> p h n", h=C_H),
                                        along(gcs[:, t, 4 * d:4 * d + 4]), ALU.subtract)\
                            .then_inc(*free("bc", l, s, d, by=1))
                        dve.wait_ge(*act_done.at("W", l, s, d))
                        dve.wait_ge(*full("G", l, s, d))
                        if s:
                            dve.wait_ge(*full("so", l, 2 * s - 1, d))
                        ps = pair("G", l, s, d)
                        V.tensor_tensor(flat(pbuf[d]), ps[:, 0:512], flat(wbuf[d]), ALU.mult)\
                            .then_inc(*free("G", l, s, d, by=1))
                        V.tensor_tensor(flat(aqbuf[d]), ps[:, 512:1024], flat(wbuf[d]), ALU.mult)\
                            .then_inc(*free("G", l, s, d, by=1))
                        dve.wait_ge(*read("G", l, s, d))
                        dve.wait_ge(*pool_done.at("MB", l, s, d))
                        V.tensor_tensor(pbuf[d], pbuf[d], p2buf[d], ALU.mult).then_inc(*dve_done.mark("A", l, s, d))
                    for d in range(2):
                        dve.wait_ge(*full("AT", l, s, d))
                        ps = pair("AT", l, s, d)
                        V.tensor_copy(flat(tbuf[d]), ps[:, 0:512]).then_inc(*free("AT", l, s, d, by=1))
                        V.tensor_tensor(xbuf[d], ps[:, 0:512].rearrange("p (h n) -> p h n", h=C_H), over_heads(ident),
                                        ALU.add).then_inc(*free("AT", l, s, d, by=1))
                    for i in range(5):
                        if i < 4:
                            for d in range(2):
                                dve.wait_ge(*full("pw", l, s, d, i))
                                V.tensor_copy(flat(power(d, i)[3]), pair("pw", l, s, d, i)[:, 512:1024])\
                                    .then_inc(*free("pw", l, s, d, i, by=1))
                        for d in range(2):
                            dve.wait_ge(*full("X", l, s, d, i))
                            V.tensor_tensor(flat(xbuf[d]), pair("X", l, s, d, i)[:, 0:512], flat(xbuf[d]), ALU.add)\
                                .then_inc(*free("X", l, s, d, i))
                        if l == 0:
                            if turned:
                                modulation_columns(*turned)
                            turned = next(filler, None)
                            if turned:
                                modulation(*turned)
                    for c in range(2):
                        for d in range(2):
                            t, cc, n = tiles[d][s], (c if d == 0 else 1 - c), 2 * s + c
                            lo = 64 * cc
                            ps = pair("so", l, n, d)
                            dve.wait_ge(*full("so", l, n, d))
                            if want_out(l, t):
                                o = Otok[lo:lo + 64, t, :]
                                if (t, cc) in seen:
                                    V.tensor_tensor(o, ps[0:64, 512:1024], o, ALU.add).then_inc(*free("so", l, n, d, by=1))
                                else:
                                    V.tensor_copy(o, ps[0:64, 512:1024]).then_inc(*free("so", l, n, d, by=1))
                                seen.add((t, cc))
                            dve.wait_ge(*pool_done.at("Sdec", l, n, d))
                            S1 = state[:, (n + 1) % 2, 4 * d:4 * d + 4, :].rearrange("p a b -> p (a b)")
                            V.tensor_tensor(S1, ps[:, 0:512], S1, ALU.add)\
                                .then_inc(*free("so", l, n, d, by=1 if want_out(l, t) else 2))
                if l == 0:
                    for ll, w in ((0, 1), (1, 0), (1, 1)):
                        norm_gain(ll, w)
                to = TT if l == 0 else LT
                dve.wait_ge(*pool_done.at("osq", l))
                V.tensor_reduce(small[:, 0:4 * to], osq[:, 0:to, :].rearrange("p t (h n) -> p (t h) n", h=C_H), AX.X,
                                ALU.add).then_inc(*dve_done.mark("oss", l))
                dve.wait_ge(*act_done.at("ors", l))
                V.reciprocal(small[:, 32:32 + 4 * to], small[:, 0:4 * to]).then_inc(*dve_done.mark("orr", l))
                dve.wait_ge(*dve_done.at("orr", l))
                ov = Otok[:, 0:to, :].rearrange("p t (h n) -> p (t h) n", h=C_H)
                V.tensor_tensor(ov, ov, along(small[:, 32:32 + 4 * to]), ALU.mult).then_inc(*dve_done.mark("onrm", l))
                for t in range(to):
                    dve.wait_ge(*full("oT", l, t))
                    if t == 0:
                        dve.wait_ge(*read("z", l, 3))
                    V.scalar_tensor_tensor(out=oC[:, :, t * P:t * P + P],
                                           in0=pair("oT", l, t)[:, 0:512].rearrange("p (h n) -> p h n", h=C_H),
                                           scalar=pcol[:, R_ONORM:R_ONORM + 1], in1=siluz[:, :, t * P:t * P + P],
                                           op0=ALU.mult, op1=ALU.mult).then_inc(*free("oT", l, t))
                for j in range(6):
                    n = TOK if j >= 4 else nt
                    dve.wait_ge(*read("ass", l, j))
                    V.reciprocal(arr[:, 0:n], arr[:, 0:n]).then_inc(*dve_done.mark("arr", l, j))
                    dve.wait_ge(*dve_done.at("arr", l, j))
                    g = pcol[:, (R_QN if j < 4 else R_KN):(R_QN if j < 4 else R_KN) + 1]
                    V.scalar_tensor_tensor(out=qk[:, j, 0:n], in0=qk[:, j, 0:n], scalar=g, in1=arr[:, 0:n],
                                           op0=ALU.mult, op1=ALU.mult).then_inc(*dve_done.mark("qkn", l, j))
                    dve.wait_ge(*full("rot", l, j))
                    V.tensor_tensor(rtmp[:, 0, :], pair("rot", l, j)[:, 0:LAT], cst[:, C_SIN:C_SIN + LAT], ALU.mult)\
                        .then_inc(*free("rot", l, j))
                    dve.wait_ge(*pool_done.at("cos", l, j))
                    dve.wait_ge(*read("rot", l, j))
                    V.tensor_tensor(qk[:, j, 0:LAT], rtmp[:, 0, :], rtmp[:, 1, :], ALU.add)\
                        .then_inc(*dve_done.mark("rope", l, j))
                    for m in {4: (0,), 5: (1, 2, 3)}.get(j, ()):
                        dve.wait_ge(*full("vb", l, m))
                        V.tensor_copy(vB[:, :, m * P:m * P + P],
                                      pair("vb", l, m)[:, 0:TOK].rearrange("p (t n) -> p t n", t=TT))\
                            .then_inc(*free("vb", l, m))
                attention(l, "A")
                attention(l, "B")
                for x in range(24):
                    dc, n = divmod(x, 3)
                    dve.wait_ge(*full("br", l, x))
                    dve.wait_ge(*read("gate", l, x))
                    g, acc = gsig[:, x % 2, 0:nt], mT[:, dc, 0:nt]
                    V.tensor_tensor(g if n else acc, pair("br", l, x)[:, 0:nt], g, ALU.mult).then_inc(*free("br", l, x))
                    dve.wait_ge(*read("br", l, x))
                    if n:
                        V.tensor_tensor(acc, acc, g, ALU.add).then_inc(*dve_done.mark("merge", l, x))
                    else:
                        V.memset(small[:, 63:64], 0.0).then_inc(*dve_done.mark("merge", l, x))
                for k in range(KC):
                    dve.wait_ge(*act_done.at("mhi", l, k))
                    V.tensor_tensor(hl[:, k, 0:nt], mT[:, k, 0:nt], hh[:, k, 0:nt].bitcast(F32), ALU.subtract)\
                        .then_inc(*dve_done.mark("mlo", l, k))

                def residual(key, j, gate):
                    dve.wait_ge(*full(*key))
                    sp_ = spans(nt)
                    for t0, t1, c in sp_:
                        V.scalar_tensor_tensor(out=xT[:, j, t0:t1], in0=pair(*key)[:, t0:t1],
                                               scalar=modc[:, gate + j, c:c + 1], in1=xT[:, j, t0:t1],
                                               op0=ALU.mult, op1=ALU.add).then_inc(*free(*key, by=2 // len(sp_)))

                dve.wait_ge(*x_back.at(l))
                for j in range(KC):
                    residual(("out", l, j), j, 16)
                norm(l, "ffn", nt)
                for g in range(NG + 1):
                    if g < NG:
                        for j in range(GF * g, GF * g + GF):
                            f = ftmp[:, j % 2, 0:nt]
                            dve.wait_ge(*read("ff1", l, j))
                            V.tensor_tensor(f, f, f, ALU.mult).then_inc(*dve_done.mark("fsq", l, j))
                            if j % GF:
                                low(l, j - 1)
                        low(l, GF * g + GF - 1)
                    if g:
                        for j in range(KC):
                            if g > 1:
                                dve.wait_ge(*read("ff2", l, g - 2, j))
                            residual(("ff2", l, g - 1, j), j, 40)
            dve.wait_ge(*full("params", DEPTH))
            V.tensor_copy(pcols[:, 0, 0:KC], pair("params", DEPTH)[:, 0:KC]).then_inc(*free("params", DEPTH))
            norm(DEPTH, "fin", LAT)

        @block.gpsimd
        def _(pool):
            G = nc.gpsimd
            crow = a["conv_c"]
            for c, n in enumerate(("c", "c_ctx")):
                v = a[n][0] if n == "c" else a[n]
                pool.dma_start(craw_c[:, c, :], v.rearrange("(p k) -> p k", k=KC)).then_inc(*cond_in.mark(by=16))

            def params(l):
                if l:
                    pool.wait_ge(*full("params", l - 1))
                rows = lambda v: v.rearrange("(k p) -> k p", p=P)
                one = lambda v: v.rearrange("(a n) -> a n", a=1)
                if l == DEPTH:
                    return [(prow[0:KC, :], rows(a["norm_final"]))]
                out_ = [(prow[R_BMOD:R_BMOD + 48, :], rows(a["b_mod"][l])),
                        (prow[R_MIX:R_MIX + KC, :], rows(a["norm_mix"][l])),
                        (prow[R_FFN:R_FFN + KC, :], rows(a["norm_ffn"][l]))]
                for q in range(CONV):
                    out_.append((prow[R_CONV + 12 * q:R_CONV + 12 * q + 12, :], rows(crow[l, q])))
                out_.append((prow[R_ONORM:R_ONORM + 1, :], one(a["o_norm_c"][l])))
                for row, name in ((R_QN, "q_norm_a"), (R_KN, "k_norm_a")):
                    for u in range(2):
                        out_.append((prow[row:row + 1, u * HD:u * HD + HD], one(a[name][l])))
                out_.append((prow[R_FIN:R_FIN + 1, :], rows(a["norm_final"])[0:1, :]))
                return out_

            def load_params(l):
                for dst, src in params(l):
                    pool.dma_start(dst, src).then_inc(*params_in.mark(l, by=16))

            def split(l, name, i=0):
                w = raw_weights(pool, l, name, i)
                n = where[l, name, i][2]
                pool.wait_ge(*act_done.at("whi", l, name, i))
                G.tensor_tensor(slot_view(wl, n % NSPL, l, name, i), w,
                                slot_view(wh, n % NSPL, l, name, i).bitcast(F32), ALU.subtract)\
                    .then_inc(*pool_done.mark("wlo", l, name, i))

            def normed(l, which, ntok):
                pool.wait_ge(*dve_done.at("rs", l, which))
                for k in range(KC):
                    if k >= 3:
                        pool.wait_ge(*(act_done.at("fin", k - 3) if which == "fin" else dve_done.at("h", l, which, k - 3)))
                    G.tensor_tensor(ht[:, k % 3, 0:ntok], xT[:, k, 0:ntok], rs_n[:, 0:ntok], ALU.mult)\
                        .then_inc(*pool_done.mark("hx", l, which, k))

            for l in range(DEPTH):
                load_params(l)
            for l in range(DEPTH):
                nt = TOK if l == 0 else LAT
                if l:
                    pool.wait_ge(*dve_done.at("g", l - 1))
                for u, name in enumerate(("a_log_c", "dt_bias_c")):
                    pool.dma_start(abc[:, u, :], a[name][l].rearrange("(a d) h -> a (d h)", a=1).to_broadcast([P, 8]))\
                        .then_inc(*abc_in.mark(l, by=16))
                if l == 0:
                    load_params(DEPTH)
                for p in range(2):
                    split(l, "c", c_order[p])
                normed(l, "mix", TOK)
                pool.wait_ge(*pool_done.at("hx", l, "mix", KC - 1))
                pool.dma_start(x_store, R[:, XT0:RN]).then_inc(*spilled.mark(l, by=16))
                split(l, "ba")
                for p in range(2, 12):
                    split(l, "c", c_order[p])
                pool.wait_ge(*spilled.at(l))
                if l:
                    pool.wait_ge(*e_in.at(l - 1, B_H - 1))
                G.memset(bpad[:, :], 0.0).then_inc(*pool_done.mark("bpad0", l))
                pool.wait_ge(*pool_done.at("bpad0", l))
                pool.dma_start(bpad[:, 48:79], a["rpb_b"][l].rearrange("h r c -> (h r) c"))\
                    .then_inc(*rpb_in.mark(l, by=16))
                pool.wait_ge(*rpb_in.at(l))
                G.tensor_scalar(bpad[:, :], bpad[:, :], 1.0 / SCALE, None, ALU.mult).then_inc(*pool_done.mark("bpad", l))
                pool.wait_ge(*pool_done.at("bpad", l))
                pool.dma_start(scratch.rearrange("(r c) -> r c", c=127), bpad[:, :]).then_inc(*pad_out.mark(l, by=16))
                pool.wait_ge(*pad_out.at(l))
                skew = bass.AP(scratch.tensor, 63, [[127, B_H * 15], [-1, GRID_W], [1, GRID_W]])
                pool.dma_start(toeplitz, skew).then_inc(*skew_out.mark(l, by=16))
                for s in range(TT):
                    for d in range(2):
                        t = tiles[d][s]
                        if s == 0:
                            pool.wait_ge(*read("gc", l))
                            pool.wait_ge(*dve_done.at("nbeta", l))
                            pool.wait_ge(*dve_done.at("l2", l, 3))
                            pool.wait_ge(*read("vtok", l, 3))
                            pool.wait_ge(*read("ktok", l, 3))
                        if s:
                            pool.wait_ge(*full("so", l, 2 * s - 1, d))
                        G.tensor_tensor(rbuf[d], over_heads(masks[m_cum[d]]), along(gt[:, t, 4 * d:4 * d + 4]), ALU.mult)\
                            .then_inc(*pool_done.mark("R", l, s, d))
                        G.tensor_tensor(p2buf[d], over_heads(masks[m_strict[d]]), along(nbeta[:, t, 4 * d:4 * d + 4]),
                                        ALU.mult).then_inc(*pool_done.mark("MB", l, s, d))
                        G.tensor_tensor(vbbuf[d], vtok[:, t, :].rearrange("p (h n) -> p h n", h=C_H),
                                        along(bg[:, t, 4 * d:4 * d + 4]), ALU.mult).then_inc(*pool_done.mark("vb", l, s, d))
                    for d in range(2):
                        t = tiles[d][s]
                        pool.wait_ge(*read("bc", l, s, d))
                        G.tensor_tensor(qdbuf[d], qT[:, :, t * P:t * P + P], ebuf[d], ALU.mult)\
                            .then_inc(*pool_done.mark("qd", l, s, d))
                        pool.wait_ge(*read("G", l, s, d))
                        G.tensor_tensor(aqbuf[d], aqbuf[d], over_heads(masks[m_aq[d]]), ALU.mult)\
                            .then_inc(*pool_done.mark("AQ", l, s, d))
                        pool.wait_ge(*dve_done.at("gb", l))
                        G.tensor_tensor(wbuf[d], ktok[:, t, :].rearrange("p (h n) -> p h n", h=C_H),
                                        along(gex[:, t, 0, 4 * d:4 * d + 4]), ALU.mult)\
                            .then_inc(*pool_done.mark("kbe", l, s, d))
                    for d in range(2):
                        t = tiles[d][s]
                        pool.wait_ge(*full("pw", l, s, d, 4))
                        pool.wait_ge(*act_done.at("gex1", l))
                        G.tensor_tensor(pbuf[d], ktok[:, t, :].rearrange("p (h n) -> p h n", h=C_H),
                                        along(gex[:, t, 1, 4 * d:4 * d + 4]), ALU.mult)\
                            .then_inc(*pool_done.mark("kd", l, s, d))
                    for c in range(2):
                        for d in range(2):
                            t, cc, n = tiles[d][s], (c if d == 0 else 1 - c), 2 * s + c
                            pool.wait_ge(*(read("so", l, n - 1, d) if n else dve_done.at("S0", l)))
                            G.tensor_tensor(state[:, (n + 1) % 2, 4 * d:4 * d + 4, :], state[:, n % 2, 4 * d:4 * d + 4, :],
                                            along(gex[:, t, 2 + cc, 4 * d:4 * d + 4]), ALU.mult)\
                                .then_inc(*pool_done.mark("Sdec", l, n, d))
                to = TT if l == 0 else LT
                for d in range(2):
                    pool.wait_ge(*read("so", l, 2 * TT - 1, d))
                G.tensor_tensor(osq[:, 0:to, :], Otok[:, 0:to, :], Otok[:, 0:to, :], ALU.mult)\
                    .then_inc(*pool_done.mark("osq", l))
                for i in range(4):
                    split(l, "z", i)
                for i in range(4):
                    split(l, "qa", i)
                for i in range(2):
                    split(l, "ka", i)
                split(l, "va")
                for x in range(2):
                    split(l, "qb", x)
                for j in range(6):
                    pool.wait_ge(*dve_done.at("qkn", l, j))
                    if j:
                        pool.wait_ge(*dve_done.at("rope", l, j - 1))
                    G.tensor_tensor(rtmp[:, 1, :], qk[:, j, 0:LAT], cst[:, C_COS:C_COS + LAT], ALU.mult)\
                        .then_inc(*pool_done.mark("cos", l, j))
                    for x in (2 * j + 2, 2 * j + 3):
                        if x < 12:
                            split(l, ("qb", "kb", "vb")[x // 4], x % 4)
                for i in range(2):
                    split(l, "gate", i)
                pool.wait_ge(*skew_out.at(l))
                per = LT if l else TT

                def bias(h):
                    if h >= 2:
                        pool.wait_ge(*read("S", "B", l, per * (h - 1) - 1))
                    elif h == 0:
                        pool.wait_ge(*full("S", "A", l, per * A_H - 1))
                    for u in range(2):
                        src = toeplitz[15 * h + 1 - u:15 * h + 15 - u].rearrange("j c k -> c j k")
                        pool.dma_start(ebias[u * 64:u * 64 + 64, h % 2, :, :], src).then_inc(*e_in.mark(l, h, by=16))
                    pool.wait_ge(*e_in.at(l, h))
                    e = ebias[:, h % 2, :, :]
                    G.tensor_tensor(e, e, cst[:, C_MASK:C_MASK + GRID_W].unsqueeze(1).to_broadcast([P, 14, GRID_W]), ALU.add)\
                        .then_inc(*pool_done.mark("E", l, h))

                for h in range(2):
                    bias(h)
                for h in range(2, B_H):
                    bias(h)
                pool.wait_ge(*full("T", "B", l, per * B_H + 1))
                pool.dma_start(R[:, XT0:RN], x_store).then_inc(*x_back.mark(l, by=16))
                for i in range(2, 24):
                    split(l, "gate", i)
                for i in range(8):
                    split(l, "out", i)
                for i in range(2):
                    split(l, "ff1", i)
                normed(l, "ffn", nt)
                for g in range(NG + 1):
                    if g < NG:
                        for i in range(max(GF * g, 2), GF * g + GF):
                            split(l, "ff1", i)
                    if g:
                        for i in range(4):
                            split(l, "ff2", 4 * (g - 1) + i)
            normed(DEPTH, "fin", LAT)


_INS = ["x", "c", "ctx", "c_ctx", "w_mod", "b_mod", "norm_mix", "w_in", "q_norm_a", "k_norm_a", "rpb_b", "conv_c",
        "a_log_c", "dt_bias_c", "o_norm_c", "w_branch", "w_out", "norm_ffn", "w_ffn1", "w_ffn2", "norm_final"]


def build(nc, arrays, book):
    a = {k: nc.dram_tensor(f"in_{k}", v.shape, F32, kind="ExternalInput").ap() for k, v in arrays.items()}
    out = nc.dram_tensor("out_0", (1, LAT, D), F32, kind="ExternalOutput").ap()
    scratch = nc.dram_tensor("bias_pad", (B_H * 15 * 127,), F32, kind="Internal").ap()
    toeplitz = nc.dram_tensor("bias_skewed", (B_H * 15, GRID_W, GRID_W), F32, kind="Internal").ap()
    x_store = nc.dram_tensor("x_store", (P, KC * TOK), F32, kind="Internal").ap()
    program(nc, a, out, scratch, toeplitz, x_store, book)


def kernel(**inputs):
    import concourse.bacc as _bacc
    from concourse.bass_utils import run_bass_kernel_spmd as _run

    arrays = {k: np.ascontiguousarray(inputs[k]) for k in _INS}
    arrays["consts"] = constants()
    book = {"final": False}
    build(_bacc.Bacc("TRN2", target_bir_lowering=False, num_devices=1), arrays, book)
    book["final"] = True
    nc = _bacc.Bacc("TRN2", target_bir_lowering=False, num_devices=1)
    build(nc, arrays, book)
    r = _run(nc, [{f"in_{k}": v for k, v in arrays.items()}], core_ids=[0])
    return r.results[0]["out_0"]
```
